# Optimizing a Trainium2 kernel written in Bass

```python
import math
import jax, jax.numpy as jnp
from jax import lax
import numpy as np

D_MODEL = 1024
BATCH = 1
SEQ = 512
DEPTH = 2

MEM_LEN = 256
NORM_EPS = 1e-6
RWKV_HEADS = 8
RWKV_HEAD_DIM = 64
RWKV_WIDTH = RWKV_HEADS * RWKV_HEAD_DIM
DECAY_LORA = 64
ICLR_LORA = 64
GATE_LORA = 128
RWKV_IN = 3 * RWKV_WIDTH + 2 * DECAY_LORA + 2 * ICLR_LORA + GATE_LORA
RWKV_SPLITS = [RWKV_WIDTH, 2 * RWKV_WIDTH, 3 * RWKV_WIDTH,
               3 * RWKV_WIDTH + 2 * DECAY_LORA,
               3 * RWKV_WIDTH + 2 * DECAY_LORA + 2 * ICLR_LORA]
SGU_WIDTH = D_MODEL // 2
SGU_GROUPS = 4
SGU_GROUP_DIM = SGU_WIDTH // SGU_GROUPS
SGU_CHUNK = 128
AB_IN = RWKV_IN + 2 * SGU_WIDTH
AB_OUT = RWKV_WIDTH + SGU_WIDTH
DIFF_HEADS = 8
DIFF_HEAD_DIM = 64
DIFF_V_DIM = 2 * DIFF_HEAD_DIM
DIFF_QK_WIDTH = DIFF_HEADS * 2 * DIFF_HEAD_DIM
DIFF_V_WIDTH = DIFF_HEADS * DIFF_V_DIM
DIFF_IN = 2 * DIFF_QK_WIDTH + DIFF_V_WIDTH
Q_BLOCK = 128
CROSS_HEADS = 4
CROSS_HEAD_DIM = D_MODEL // CROSS_HEADS
D_FF = 2816
CONV_WIDTH = 3
N_EVEN = (DEPTH + 1) // 2
N_ODD = DEPTH // 2

kernel_name = 'hybrid_rwkv7_sgu_diffattn_encoder'

def rms_norm(x, gain):
    xf = x.astype(jnp.float32)
    normed = xf * lax.rsqrt(jnp.mean(xf * xf, axis=-1, keepdims=True) + NORM_EPS)
    return normed.astype(x.dtype) * gain

def alibi_slopes(n_heads):
    return 2.0 ** (-8.0 * jnp.arange(1, n_heads + 1, dtype=jnp.float32) / n_heads)

def token_shift_centred(z, mu_prev, mu_next):
    z_prev = jnp.pad(z[:, :-1], ((0, 0), (1, 0), (0, 0)))
    z_next = jnp.pad(z[:, 1:], ((0, 0), (0, 1), (0, 0)))
    return z + mu_prev * (z_prev - z) + mu_next * (z_next - z)

def rwkv7_step(state, inp):
    r, w, k, v, kk, a = inp
    sa = jnp.einsum('...vk,...k->...v', state, -kk)
    state = (state * w[..., None, :]
             + sa[..., :, None] * (kk * a)[..., None, :]
             + v[..., :, None] * k[..., None, :])
    y = jnp.einsum('...vk,...k->...v', state, r)
    return state, y

def rwkv7_bidirectional(z, mu_prev, mu_next, w0, w2, a0, a2, g2, k_k, k_a, r_k, out_gain):
    bsz, seq, _ = z.shape
    H, N = RWKV_HEADS, RWKV_HEAD_DIM
    z = token_shift_centred(z, mu_prev, mu_next)
    r, k, v, wl, al, gl = jnp.split(z, RWKV_SPLITS, axis=-1)
    wl = jnp.tanh(wl.reshape(bsz, seq, 2, DECAY_LORA))
    w_log = -jax.nn.softplus(-(w0 + jnp.einsum('btdr,drc->btdc', wl, w2))) - 0.5
    decay = jnp.exp(-jnp.exp(w_log.astype(jnp.float32)))
    a = jax.nn.sigmoid(a0 + jnp.einsum('btdr,drc->btdc', al.reshape(bsz, seq, 2, ICLR_LORA), a2))
    g = jax.nn.sigmoid(gl) @ g2
    kk = (k * k_k).reshape(bsz, seq, H, N).astype(jnp.float32)
    kk = kk * lax.rsqrt(jnp.sum(kk * kk, axis=-1, keepdims=True) + 1e-12)
    k_dir = k[:, :, None, :] * (1.0 + (a - 1.0) * k_a)

    rh = r.reshape(bsz, seq, H, N)
    vh = v.reshape(bsz, seq, H, N)
    dh = decay.reshape(bsz, seq, 2, H, N)
    ah = a.reshape(bsz, seq, 2, H, N)
    kh = k_dir.reshape(bsz, seq, 2, H, N)

    def dir_stack(fwd, bwd):
        s = jnp.stack([fwd, jnp.flip(bwd, axis=1)], axis=0).astype(jnp.float32)
        return jnp.transpose(s, (2, 0, 1, 3, 4))

    xs = (dir_stack(rh, rh), dir_stack(dh[:, :, 0], dh[:, :, 1]),
          dir_stack(kh[:, :, 0], kh[:, :, 1]), dir_stack(vh, vh),
          dir_stack(kk, kk), dir_stack(ah[:, :, 0], ah[:, :, 1]))
    state0 = jnp.zeros((2, bsz, H, N, N), jnp.float32)
    _, ys = lax.scan(rwkv7_step, state0, xs)
    y = ys[:, 0] + jnp.flip(ys[:, 1], axis=0)
    y = rms_norm(jnp.transpose(y, (1, 0, 2, 3)), out_gain).astype(z.dtype)
    bonus = jnp.sum(rh[:, :, None] * kh * r_k, axis=(2, 4))
    out = (y + bonus[..., None] * vh).reshape(bsz, seq, RWKV_WIDTH)
    return out * g

def chunked_spatial_gating(u, v, v_gain, w_s, b):
    bsz, seq, _ = v.shape
    vg = rms_norm(v, v_gain).reshape(bsz, seq // SGU_CHUNK, SGU_CHUNK, SGU_GROUPS, SGU_GROUP_DIM)
    s = jnp.einsum('gpq,bnqgc->bnpgc', w_s, vg) + jnp.transpose(b)[:, :, None]
    return u * s.reshape(bsz, seq, SGU_WIDTH)

def differential_attention(z, q_gain, k_gain, lq1, lk1, lq2, lk2, out_gain, lambda_init):
    bsz, seq, _ = z.shape
    H, Dh = DIFF_HEADS, DIFF_HEAD_DIM
    n_blocks = seq // Q_BLOCK
    q = rms_norm(z[..., :DIFF_QK_WIDTH].reshape(bsz, seq, H, 2, Dh), q_gain)
    k = rms_norm(z[..., DIFF_QK_WIDTH:2 * DIFF_QK_WIDTH].reshape(bsz, seq, H, 2, Dh), k_gain)
    v = z[..., 2 * DIFF_QK_WIDTH:].reshape(bsz, seq, H, DIFF_V_DIM)
    lam = (jnp.exp(jnp.sum(lq1.astype(jnp.float32) * lk1.astype(jnp.float32)))
           - jnp.exp(jnp.sum(lq2.astype(jnp.float32) * lk2.astype(jnp.float32))) + lambda_init)
    slopes = alibi_slopes(H)
    pos = jnp.arange(seq)
    scale = 1.0 / math.sqrt(Dh)
    qb = jnp.transpose(q.reshape(bsz, n_blocks, Q_BLOCK, H, 2, Dh), (1, 0, 2, 3, 4, 5))
    starts = jnp.arange(n_blocks) * Q_BLOCK

    def block(args):
        q_blk, start = args
        q_pos = start + jnp.arange(Q_BLOCK)
        dist = jnp.abs(q_pos[:, None] - pos[None, :]).astype(jnp.float32)
        bias = -slopes[:, None, None] * dist
        logits = jnp.einsum('bqhcd,bkhcd->bhcqk', q_blk, k).astype(jnp.float32) * scale
        p = jax.nn.softmax(logits + bias[None, :, None], axis=-1)
        attn = p[:, :, 0] - lam * p[:, :, 1]
        return jnp.einsum('bhqk,bkhe->bqhe', attn.astype(v.dtype), v)

    o = lax.map(block, (qb, starts))
    o = jnp.transpose(o, (1, 0, 2, 3, 4)).reshape(bsz, seq, H, DIFF_V_DIM)
    o = rms_norm(o, out_gain) * (1.0 - lambda_init)
    return o.reshape(bsz, seq, DIFF_V_WIDTH)

def memory_cross_attention(h, mem_n, wq, wkv, q_gain, k_gain, wo):
    bsz, seq, _ = h.shape
    m = mem_n.shape[1]
    q = rms_norm((h @ wq).reshape(bsz, seq, CROSS_HEADS, CROSS_HEAD_DIM), q_gain)
    kv = mem_n @ wkv
    k = rms_norm(kv[..., :D_MODEL].reshape(bsz, m, CROSS_HEADS, CROSS_HEAD_DIM), k_gain)
    v = kv[..., D_MODEL:].reshape(bsz, m, CROSS_HEADS, CROSS_HEAD_DIM)
    logits = jnp.einsum('bqhd,bkhd->bhqk', q, k).astype(jnp.float32) / math.sqrt(CROSS_HEAD_DIM)
    p = jax.nn.softmax(logits, axis=-1)
    o = jnp.einsum('bhqk,bkhd->bqhd', p.astype(v.dtype), v).reshape(bsz, seq, D_MODEL)
    return o @ wo

def conv_gated_ffn(h, w_up, conv_w, conv_b, w_down):
    seq = h.shape[1]
    u = h @ w_up
    pad = CONV_WIDTH // 2
    u_pad = jnp.pad(u, ((0, 0), (pad, pad), (0, 0)))
    u = conv_b + sum(u_pad[:, j:j + seq] * conv_w[j] for j in range(CONV_WIDTH))
    gate, val = jnp.split(u, 2, axis=-1)
    return (jax.nn.silu(gate) * val) @ w_down

def setup_inputs(seed: int = 0) -> dict:
    key = jax.random.key(seed)
    ks = iter(jax.random.split(key, 64))
    D, L, E, O = D_MODEL, DEPTH, N_EVEN, N_ODD

    def nrm(shape, scale):
        return jax.random.normal(next(ks), shape, jnp.float32) * scale

    def gain(shape):
        return 1.0 + nrm(shape, 0.02)

    def unif(shape, lo, hi):
        return jax.random.uniform(next(ks), shape, jnp.float32, lo, hi)

    return {
        'x': nrm((BATCH, SEQ, D), 1.0),
        'mem': nrm((BATCH, MEM_LEN, D), 1.0),
        'mem_norm': gain((D,)),
        'mix_norm': gain((L, D)),
        'cross_norm': gain((L, D)),
        'ffn_norm': gain((L, D)),
        'ab_w_in': nrm((E, D, AB_IN), D ** -0.5),
        'ab_shift_prev': unif((E, RWKV_IN), 0.0, 0.5),
        'ab_shift_next': unif((E, RWKV_IN), 0.0, 0.5),
        'rwkv_w0': -3.0 + nrm((E, 2, RWKV_WIDTH), 1.0),
        'rwkv_w2': nrm((E, 2, DECAY_LORA, RWKV_WIDTH), 0.5 * DECAY_LORA ** -0.5),
        'rwkv_a0': nrm((E, 2, RWKV_WIDTH), 0.5),
        'rwkv_a2': nrm((E, 2, ICLR_LORA, RWKV_WIDTH), ICLR_LORA ** -0.5),
        'rwkv_g2': nrm((E, GATE_LORA, RWKV_WIDTH), GATE_LORA ** -0.5),
        'rwkv_k_k': 0.85 + nrm((E, RWKV_WIDTH), 0.05),
        'rwkv_k_a': 1.0 + nrm((E, RWKV_WIDTH), 0.05),
        'rwkv_r_k': nrm((E, RWKV_HEADS, RWKV_HEAD_DIM), 0.1),
        'rwkv_out_gain': gain((E, RWKV_HEADS, RWKV_HEAD_DIM)),
        'sgu_v_gain': gain((E, SGU_WIDTH)),
        'sgu_w_s': nrm((E, SGU_GROUPS, SGU_CHUNK, SGU_CHUNK), SGU_CHUNK ** -0.5),
        'sgu_b': 1.0 + nrm((E, SGU_GROUPS, SGU_CHUNK), 0.01),
        'ab_w_out': nrm((E, AB_OUT, D), AB_OUT ** -0.5),
        'diff_w_in': nrm((O, D, DIFF_IN), D ** -0.5),
        'diff_q_gain': gain((O, DIFF_HEAD_DIM)),
        'diff_k_gain': gain((O, DIFF_HEAD_DIM)),
        'diff_lambda_q1': nrm((O, DIFF_HEAD_DIM), 0.1),
        'diff_lambda_k1': nrm((O, DIFF_HEAD_DIM), 0.1),
        'diff_lambda_q2': nrm((O, DIFF_HEAD_DIM), 0.1),
        'diff_lambda_k2': nrm((O, DIFF_HEAD_DIM), 0.1),
        'diff_out_gain': gain((O, DIFF_V_DIM)),
        'diff_w_out': nrm((O, DIFF_V_WIDTH, D), DIFF_V_WIDTH ** -0.5),
        'cross_wq': nrm((L, D, D), D ** -0.5),
        'cross_wkv': nrm((L, D, 2 * D), D ** -0.5),
        'cross_q_gain': gain((L, CROSS_HEAD_DIM)),
        'cross_k_gain': gain((L, CROSS_HEAD_DIM)),
        'cross_wo': nrm((L, D, D), D ** -0.5),
        'ffn_w_up': nrm((L, D, 2 * D_FF), D ** -0.5),
        'ffn_conv_w': nrm((L, CONV_WIDTH, 2 * D_FF), CONV_WIDTH ** -0.5),
        'ffn_conv_b': nrm((L, 2 * D_FF), 0.01),
        'ffn_w_down': nrm((L, D_FF, D), D_FF ** -0.5),
    }

def reference(x, mem, mem_norm, mix_norm, cross_norm, ffn_norm,
              ab_w_in, ab_shift_prev, ab_shift_next, rwkv_w0, rwkv_w2, rwkv_a0, rwkv_a2,
              rwkv_g2, rwkv_k_k, rwkv_k_a, rwkv_r_k, rwkv_out_gain,
              sgu_v_gain, sgu_w_s, sgu_b, ab_w_out,
              diff_w_in, diff_q_gain, diff_k_gain, diff_lambda_q1, diff_lambda_k1,
              diff_lambda_q2, diff_lambda_k2, diff_out_gain, diff_w_out,
              cross_wq, cross_wkv, cross_q_gain, cross_k_gain, cross_wo,
              ffn_w_up, ffn_conv_w, ffn_conv_b, ffn_w_down):
    mem_n = rms_norm(mem, mem_norm)
    for l in range(DEPTH):
        h = rms_norm(x, mix_norm[l])
        if l % 2 == 0:
            e = l // 2
            z = h @ ab_w_in[e]
            a_out = rwkv7_bidirectional(z[..., :RWKV_IN], ab_shift_prev[e], ab_shift_next[e],
                                        rwkv_w0[e], rwkv_w2[e], rwkv_a0[e], rwkv_a2[e],
                                        rwkv_g2[e], rwkv_k_k[e], rwkv_k_a[e], rwkv_r_k[e],
                                        rwkv_out_gain[e])
            u, v = jnp.split(jax.nn.gelu(z[..., RWKV_IN:]), 2, axis=-1)
            b_out = chunked_spatial_gating(u, v, sgu_v_gain[e], sgu_w_s[e], sgu_b[e])
            x = x + jnp.concatenate([a_out, b_out], axis=-1) @ ab_w_out[e]
        else:
            o = l // 2
            lambda_init = 0.8 - 0.6 * math.exp(-0.3 * l)
            c_out = differential_attention(h @ diff_w_in[o], diff_q_gain[o], diff_k_gain[o],
                                           diff_lambda_q1[o], diff_lambda_k1[o],
                                           diff_lambda_q2[o], diff_lambda_k2[o],
                                           diff_out_gain[o], lambda_init)
            x = x + c_out @ diff_w_out[o]
        x = x + memory_cross_attention(rms_norm(x, cross_norm[l]), mem_n, cross_wq[l],
                                       cross_wkv[l], cross_q_gain[l], cross_k_gain[l],
                                       cross_wo[l])
        x = x + conv_gated_ffn(rms_norm(x, ffn_norm[l]), ffn_w_up[l], ffn_conv_w[l],
                               ffn_conv_b[l], ffn_w_down[l])
    return x


_drawn_inputs = setup_inputs


def setup_inputs(seed=0):
    import zlib

    import numpy as np

    out = dict(_drawn_inputs(seed))
    spreads = {}
    factors = {'mem_norm': 8.0,
     'cross_norm': 8.0,
     'ffn_norm': 2.996,
     'rwkv_w2': 4.6,
     'rwkv_k_k': 3.94,
     'rwkv_out_gain': 7.572,
     'sgu_v_gain': 6.549,
     'sgu_b': 8.0,
     'diff_q_gain': 8.0,
     'diff_k_gain': 7.956,
     'diff_lambda_k1': 5.99,
     'diff_out_gain': 6.558,
     'cross_q_gain': 8.0,
     'cross_k_gain': 8.0,
     'ffn_conv_b': 6.085}
    for name, (base, spread) in spreads.items():
        noise = np.random.default_rng([zlib.crc32(name.encode()), seed]).standard_normal(out[name].shape)
        drawn = base * np.exp(spread * noise) if base else spread * noise
        out[name] = __import__('jax').numpy.asarray(drawn.astype(out[name].dtype))
    for name, factor in factors.items():
        out[name] = (out[name] * factor).astype(out[name].dtype)
    return out
```

```python
import math

import concourse.bass as bass
from concourse import mybir

F32 = mybir.dt.float32
F32R = mybir.dt.float32r
ALU = mybir.AluOpType
ACT = mybir.ActivationFunctionType
AX = mybir.AxisListType

P = 128
D = 1024
DC = D // P
SEQ = 512
NT = SEQ // P
MEM = 256
MT = MEM // P
EPS = 1e-6
BANK = 512
HD = 64
RW = 512
NJ = RW // P
CH = 64
NCH = SEQ // CH
RWKV_IN = 1920
SGU_G = 4
DH = 8
DHD = 64
XH = 4
XD = 256
FF = 2816
FC = FF // P
LAMBDA_INIT = 0.8 - 0.6 * math.exp(-0.3)
DECAY = math.exp(-0.5)

VEC_TILES = [
    [("mix_norm", 16), ("cross_norm", 16), ("ffn_norm", 16), ("mem_norm", 8), ("ab_shift_prev", 15),
     ("ab_shift_next", 15), ("rwkv_w0", 8), ("rwkv_a0", 8), ("rwkv_k_k", 4), ("rwkv_k_a", 4),
     ("rwkv_r_k", 4), ("rwkv_out_gain", 4), ("sgu_v_gain", 4), ("diff_out_gain", 1),
     ("diff_q_gain", 1), ("diff_k_gain", 1)],
    [("ffn_conv_b", 88), ("cross_q_gain", 4), ("cross_k_gain", 4)],
    [("ffn_conv_w", 88)], [("ffn_conv_w", 88)], [("ffn_conv_w", 88)],
]
COL = {}
for _i, _tile in enumerate(VEC_TILES):
    _r = 0
    for _name, _n in _tile:
        COL.setdefault(_name, _i * P + _r)
        _r += _n

KEEP = {"ident": (0, P), "dist": (P, 896)}
KEEP_W = P + 896
MASKS = ["LT", "UT", "UTI", "LTI", "T1f", "T1b"] + [f"X{d}{j}" for d in "fb" for j in range(2, 7)]
RK = {m: (i * P, P) for i, m in enumerate(MASKS)}
RK["bones"] = (len(MASKS) * P, P)
RK["reset"] = (len(MASKS) * P + P, SEQ)
RK["ident2"] = (len(MASKS) * P + P + SEQ, HD)
RK_W = len(MASKS) * P + P + SEQ + HD


class Tally:

    def __init__(self, sem):
        self.sem, self.n = sem, 0

    def sig(self, instruction, by=1):
        instruction.then_inc(self.sem, by)
        self.n += by
        return self.n


def build(nc, a, out):
    sems = {}

    def S(name):
        if name not in sems:
            sems[name] = nc.alloc_semaphore(name)
        return sems[name]

    left, base = {}, {}

    def shares(tag, kind, **totals):
        for x, n in totals.items():
            base[tag, x] = (S(f"{kind}_{x}"), left.get((kind, x), 0))
            left[kind, x] = left.get((kind, x), 0) + n

    def sem(tag, x):
        return base[tag, x][0]

    def at(tag, x, n):
        s, b = base[tag, x]
        return s, b + n

    low = (nc.sbuf_base + 31) // 32 * 32

    def sb(name, shape, at, dt=F32):
        return nc.alloc_sbuf_tensor_at(name, shape, dt, offset=low + at)

    X = sb("X", [P, NT, D], 0)
    WRAW = [sb(f"WRAW{i}", [P, 4, 512], 16384 + 8192 * i) for i in range(2)]
    WHI = [sb(f"WHI{i}", [P, 4, 512], 32768 + 16384 * i, F32R) for i in range(3)]
    WLO = [sb(f"WLO{i}", [P, 4, 512], 32768 + 16384 * i + 8192, F32R) for i in range(3)]
    HHI = [sb(f"HHI{k}", [P, SEQ], 81920 + 2048 * k, F32R) for k in range(DC)]
    HLO = [sb(f"HLO{k}", [P, SEQ], 98304 + 2048 * k, F32R) for k in range(DC)]
    COLS = sb("COLS", [P, 5 * P], 114688)
    KC = sb("KC", [P, KEEP_W], 117248)
    SM = sb("SM", [P, 256], 121344)
    LAM = sb("LAM", [P, 256], 122368)
    R0 = 123392
    ident = KC[:, 0:P]

    VROW = [sb(f"VROW{i}", [P, P], R0 + 40000 + 512 * i) for i in range(5)]
    RC = sb("RC", [P, RK_W], R0)
    r1 = R0 + 4 * RK_W
    WL2 = sb("WL2", [P, 3, 512], r1)
    SGUB = sb("SGUB", [P, 4, P], r1 + 6144)
    WS = sb("WS", [P, 4, P], r1 + 8192)
    r2 = r1 + 10240
    ZS = [sb(f"ZS{c}", [P, SEQ], r2 + 2048 * c) for c in range(15)]
    KK = sb("KK", [P, NJ, SEQ], r2 + 30720)
    r3 = r2 + 38912
    names7 = ["GBR", "GKA", "GKR", "AI", "TT", "UU", "XX"]
    U7 = {n: sb(n, [P, 8, P], r3 + 4096 * i) for i, n in enumerate(names7)}
    GBR, GKA, GKR, AI, TT, UU, XX = (U7[n] for n in names7)
    UG = sb("UG", [P, 4, SEQ], r3)
    VG = sb("VG", [P, NT, 512], r3 + 8192)
    WST = sb("WST", [P, 4, P], r3 + 16384)
    SQ1 = sb("SQ1", [P, 1024], r3 + 18432)
    BT = [sb(f"BT{i}", [P, SEQ], r3 + 22528 + 2048 * i) for i in range(2)]
    w0 = 16384
    PT = sb("PT", [P, NJ, NCH, HD], w0)
    QT = sb("QT", [P, NJ, NCH, HD], w0 + 8192)
    RT = sb("RT", [P, NJ, SEQ], w0 + 16384)
    ALP = sb("ALP", [P, 2, SEQ], w0 + 24576)
    RHO = sb("RHO", [P, 2, SEQ], w0 + 28672)
    BET = sb("BET", [P, SEQ], w0 + 32768)
    KAP = sb("KAP", [P, SEQ], w0 + 34816)
    AXT = sb("AXT", [P, 8, P], w0 + 36864)
    BPD = sb("BPD", [P, NT, 2, P], w0 + 40960)
    KPD = sb("KPD", [P, NT, 2, P], w0 + 45056)
    WU = sb("WU", [P, 8, P], w0 + 49152)
    TMP = [sb(f"TMP{i}", [P, SEQ], w0 + 53248 + 2048 * i) for i in range(4)]
    BON = [sb(f"BON{j}", [P, SEQ], w0 + 61440 + 2048 * j if j < 2 else r1 + 6144 + 2048 * (j - 2))
           for j in range(NJ)]
    YL = sb("YL", [P, NJ, SEQ], 81920)
    VTK = sb("VTK", [P, NT, RW], 98304)
    YQ = [sb(f"YQ{i}", [P, SEQ], r3 + 2048 * i) for i in range(5)]
    XN = sb("XN", [P, NT, D], R0 + 49152 + 8192)
    SQ = sb("SQ", [P, D], R0 + 49152 + 8192 + 16384)
    MNT = [sb(f"MHI{k}", [P, MEM], R0 + 1024 * k, F32R) for k in range(DC)]
    MNL = [sb(f"MLO{k}", [P, MEM], R0 + 8192 + 1024 * k, F32R) for k in range(DC)]
    MRAW = sb("MRAW", [P, MT, D], R0 + 16384)
    MXN = sb("MXN", [P, MT, D], R0 + 24576)
    KTOK = sb("KTOK", [P, MT, D], R0 + 16384)
    KFT = sb("KFT", [P, DC, MEM], R0 + 32768)
    VMEM = sb("VMEM", [P, MT, D], R0 + 40960)
    SQX = sb("SQX", [P, D], R0 + 49152)
    QTOK = sb("QTOK", [P, NT, D], R0)
    QFT = sb("QFT", [P, DC, SEQ], R0 + 53248)
    PTR = sb("PTR", [P, XH, MT, SEQ], R0)
    EX = [sb(f"EX{i}", [P, XH, MEM], R0 + 16384 + 4096 * i) for i in range(2)]
    GHI = [sb(f"GHI{k}", [P, SEQ], R0 + 2048 * k, F32R) for k in range(12)]
    GLO = [sb(f"GLO{k}", [P, SEQ], R0 + 24576 + 2048 * k, F32R) for k in range(12)]
    CG = [sb(f"CG{i}", [P, SEQ], R0 + 49152 + 2048 * i) for i in range(2)]
    CV = [sb(f"CV{i}", [P, SEQ], R0 + 53248 + 2048 * i) for i in range(2)]
    SG = [sb(f"SG{i}", [P, SEQ], R0 + 57344 + 2048 * i) for i in range(2)]
    TOK = sb("TOK", [P, NT, D], R0)
    QF = sb("QF", [P, DC, SEQ], R0 + 16384)
    KF = sb("KF", [P, DC, SEQ], R0 + 32768)
    VV = sb("VV", [P, NT, D], R0 + 49152)
    SS = [sb(f"SS{i}", [P, 2, SEQ], R0 + 65536 + 4096 * i) for i in range(2)]
    AT = [sb(f"AT{i}", [P, SEQ], R0 + 73728 + 2048 * i) for i in range(2)]
    ATT = [sb(f"ATT{i}", [P, NT, P], R0 + 77824 + 2048 * i) for i in range(2)]
    OTK = sb("OTK", [P, NT, D], R0)
    SQD = sb("SQD", [P, D], R0 + 77824)

    PS = nc.alloc_psum_tensor("PS", [P, 8, BANK], F32)

    def col(name, i=0, n=1):
        c = COL[name] + i
        return COLS[:, c:c + n]

    def rk(name, p0=0, p1=P):
        o, w = RK[name]
        return RC[p0:p1, o:o + w]

    def mask4(name):
        return rk(name).unsqueeze(1).to_broadcast([P, 4, P])

    plan, use = [], {}
    used_at = {}
    gemms = {}
    raw_level = []
    slot_total = [0, 0]

    def gemm(name, w, groups, k0, k1, nb):
        g_list, banks = [], 0
        for gi, pieces in enumerate(groups):
            n = nb if isinstance(nb, int) else nb[gi]
            steps = []
            for k in range(k0, k1, 4):
                nk = min(4, k1 - k)
                i = len(plan)
                slot_total[i % 2] += 16 * len(pieces)
                raw_level.append(slot_total[i % 2])
                plan.append((w, k, nk, pieces))
                steps.append((i, k - k0, nk))
                if k + nk < k1:
                    use[name] = use.get(name, 0) + 1
                    used_at[i] = ("wused", use[name])
                else:
                    used_at[i] = ("done", banks + n)
            g_list.append((steps, n, banks))
            banks += n
        gemms[name] = g_list
        shares(name, "g", done=banks, wused=use.get(name, 0), ev=banks)
        for steps, _, _ in g_list:
            for i, _, _ in steps:
                used_at[i] = at(name, *used_at[i])

    halves = [[(0, 512)], [(512, 512)]]
    gemm("zf", a["ab_w_in"][0], [[(512 * g, 512)] for g in range(3)] + [[(1536, 384)], [(1920, 512)]],
         0, DC, [4, 4, 4, 3, 4])
    gemm("zv", a["ab_w_in"][0], [[(2432, 512)]], 0, DC, 4)
    fence = len(plan)
    gemm("ab", a["ab_w_out"][0], halves, 0, DC, NT)

    def plan_tail(l):
        gemm(f"kv{l}", a["cross_wkv"][l], [[(512 * g, 512)] for g in range(4)], 0, DC, MT)
        gemm(f"xq{l}", a["cross_wq"][l], halves, 0, DC, NT)
        gemm(f"xo{l}", a["cross_wo"][l], halves, 0, DC, NT)
        for h, (c0, c1) in enumerate(((0, 12), (12, 22))):
            gemm(f"up{l}{h}", a["ffn_w_up"][l],
                 [[(c * P, 256), (FF + c * P, 256)] for c in range(c0, c1, 2)], 0, DC, 4)
            gemm(f"dn{l}{h}", a["ffn_w_down"][l], halves, c0, c1, NT)

    plan_tail(0)
    gemm("dq", a["diff_w_in"][0], halves, 0, DC, NT)
    gemm("dk", a["diff_w_in"][0], [[(1024, 512)], [(1536, 512)]], 0, DC, NT)
    gemm("dv", a["diff_w_in"][0], [[(2048, 512)], [(2560, 512)]], 0, DC, NT)
    gemm("do", a["diff_w_out"][0], halves, 0, DC, NT)
    plan_tail(1)

    class Engine:

        def __init__(self, name, eng):
            self.name, self.e = name, eng
            self.own = Tally(S(f"{name}_own"))
            self.met = 0
            self.split = 0

        def mine(self, instruction):
            self.own.sig(instruction)

        def wait_mine(self):
            self.e.wait_ge(self.own.sem, self.own.n)

        def meet(self):
            self.e.drain().then_inc(S(f"{self.name}_stage"), 1)
            self.met += 1
            for other in ("pe", "act", "dve", "pool"):
                if other != self.name:
                    self.e.wait_ge(S(f"{other}_stage"), self.met)

    def part(t, i):
        w, k, nk, pieces = plan[i]
        return t[:, 0:nk, 0:sum(n for _, n in pieces)]

    def split_hi(A, upto):
        while A.split < min(upto, len(plan)):
            i = A.split
            A.e.wait_ge(S(f"raw_in{i % 2}"), raw_level[i])
            if i >= 3:
                A.e.wait_ge(*used_at[i - 3])
            A.e.activation(part(WHI[i % 3], i), part(WRAW[i % 2], i), ACT.Copy).then_inc(S("w_hi"), 1)
            A.split += 1

    def split_lo(V, upto):
        while V.split < min(upto, len(plan)):
            i = V.split
            V.e.wait_ge(S("w_hi"), i + 1)
            V.e.tensor_tensor(part(WLO[i % 3], i), part(WRAW[i % 2], i), part(WHI[i % 3], i).bitcast(F32),
                              ALU.subtract).then_inc(S("w_lo"), 1)
            V.split += 1

    def gemm_pe(T, name, hi, lo, tokens_out, nt, freed, bank0=0):
        e = T.e
        for gi, (steps, nb, banks) in enumerate(gemms[name]):
            for si, (i, kb, nk) in enumerate(steps):
                e.wait_ge(S("w_lo"), i + 1)
                width = sum(n for _, n in plan[i][3])
                for b in range(nb):
                    if si == 0 and gi > 0:
                        for freed_sem, value in freed(gi, b):
                            e.wait_ge(freed_sem, value)
                    n = width if tokens_out else nt
                    o = PS[:, bank0 + b, 0:n]
                    for kk in range(nk):
                        k = kb + kk
                        for q, (wt, ht) in enumerate(((WHI, hi), (WHI, lo), (WLO, hi))):
                            w = wt[i % 3]
                            if tokens_out:
                                l, r = ht(k)[:, b * P:b * P + P], w[:, kk, 0:width]
                            else:
                                l, r = w[:, kk, b * P:b * P + P], ht(k)[:, 0:nt]
                            mm = e.matmul(o, l, r, start=(si == 0 and kk == 0 and q == 0),
                                          stop=(si == len(steps) - 1 and kk == nk - 1 and q == 2))
                    if si == len(steps) - 1:
                        mm.then_inc(sem(name, "done"), 1)
                if si < len(steps) - 1:
                    mm.then_inc(sem(name, "wused"), 1)

    def gemm_side(E, name, split, evac, limit=None):
        for gi, (steps, nb, banks) in enumerate(gemms[name]):
            for i, _, _ in steps:
                split(E, i + 3 if limit is None else min(i + 3, limit))
            if evac is not None:
                for b in range(nb):
                    E.e.wait_ge(*at(name, "done", banks + b + 1))
                    evac(gi, b, banks + b)

    def one_evac(name):
        def freed(gi, b):
            _, nb, banks = gemms[name][gi - 1]
            return [at(name, "ev", banks + min(b, nb - 1) + 1)]
        return freed

    hhi, hlo = (lambda k: HHI[k][:, :]), (lambda k: HLO[k][:, :])

    def norm_act(A, tag, src, sq, nt, gain, hi):
        e = A.e
        for t in range(nt):
            e.activation(sq[:, :], src[:, t, :], ACT.Square, accum_out=SM[:, t:t + 1]).then_inc(sem(tag, "sq"), 1)
            e.wait_ge(*at(tag, "sq", t + 1))
        for k in range(DC):
            e.wait_ge(*at(tag, "tp", k + 1))
            e.activation(hi(k)[:, 0:nt * P], PS[:, k % 4, 0:nt * P], ACT.Copy,
                         scale=gain(k)).then_inc(sem(tag, "hi"), 1)

    def norm_pool(G, tag, nt):
        G.e.wait_ge(*at(tag, "var", 1))
        G.e.tensor_tensor(SM[:, 8:8 + nt], SM[:, 4:4 + nt], SM[:, 16:16 + nt], ALU.pow).then_inc(sem(tag, "rstd"), 1)

    def norm_dve(V, tag, src, xn, nt, gain, hi, lo):
        e = V.e
        e.wait_ge(*at(tag, "sq", nt))
        e.tensor_scalar(SM[:, 4:4 + nt], SM[:, 0:nt], 1.0 / D, EPS, ALU.mult, ALU.add).then_inc(sem(tag, "var"), 1)
        e.wait_ge(*at(tag, "rstd", 1))
        for t in range(nt):
            e.tensor_scalar(xn[:, t, :], src[:, t, :], SM[:, 8 + t:9 + t], None, ALU.mult).then_inc(sem(tag, "xn"), 1)
        for k in range(DC):
            e.wait_ge(*at(tag, "hi", k + 1))
            e.scalar_tensor_tensor(lo(k)[:, 0:nt * P], PS[:, k % 4, 0:nt * P], gain(k), hi(k)[:, 0:nt * P].bitcast(F32),
                                   ALU.mult, ALU.subtract).then_inc(sem(tag, "lo"), 1)

    def norm_pe(T, tag, xn, nt):
        e = T.e
        for k in range(DC):
            if k >= 4:
                e.wait_ge(*at(tag, "lo", k - 3))
            for t in range(nt):
                if k == 0:
                    e.wait_ge(*at(tag, "xn", t + 1))
                mm = e.transpose(PS[:, k % 4, t * P:t * P + P], xn[:, t, k * P:k * P + P], ident)
            mm.then_inc(sem(tag, "tp"), 1)

    def add_residual(V, name):
        def evac(gi, b, n):
            o = X[:, b, gi * 512:gi * 512 + 512]
            V.e.tensor_tensor(o, o, PS[:, b, :], ALU.add).then_inc(sem(name, "ev"), 1)
        return evac

    def group_norm_dve(V, tag, tok, sq, nt, w):
        e, n = V.e, D // w
        for t in range(nt):
            V.mine(e.tensor_tensor(sq[:, :], tok[:, t, :], tok[:, t, :], ALU.mult))
            V.wait_mine()
            V.mine(e.tensor_reduce(SM[:, 32 + t * n:32 + t * n + n], sq[:, :].rearrange("p (g w) -> p g w", w=w),
                                   AX.X, ALU.add))
            V.wait_mine()
        e.tensor_scalar(SM[:, 96:96 + nt * n], SM[:, 32:32 + nt * n], 1.0 / w, EPS, ALU.mult, ALU.add)\
            .then_inc(sem(tag, "gvar"), 1)
        e.wait_ge(*at(tag, "grstd", 1))
        for t in range(nt):
            v = tok[:, t, :].rearrange("p (g w) -> p g w", w=w)
            e.tensor_tensor(v, v, SM[:, 160 + t * n:160 + t * n + n].unsqueeze(2).to_broadcast([P, n, w]),
                            ALU.mult).then_inc(sem(tag, "gn"), 1)

    def group_norm_pool(G, tag, nt, w):
        n = D // w * nt
        G.e.wait_ge(*at(tag, "gvar", 1))
        G.e.tensor_tensor(SM[:, 160:160 + n], SM[:, 96:96 + n], SM[:, 16:17].to_broadcast([P, n]), ALU.pow)\
            .then_inc(sem(tag, "grstd"), 1)

    def turn_pe(T, tag, tok, nt, bank0=0):
        e = T.e
        for k in range(DC):
            if k >= 4:
                e.wait_ge(*at(tag, "tev", k - 3))
            for t in range(nt):
                if k == 0:
                    e.wait_ge(*at(tag, "gn", t + 1))
                mm = e.transpose(PS[:, bank0 + k % 4, t * P:t * P + P], tok[:, t, k * P:k * P + P], ident)
            mm.then_inc(sem(tag, "ttp"), 1)

    def turn_act(A, tag, dst, nt, gain):
        for k in range(DC):
            A.e.wait_ge(*at(tag, "ttp", k + 1))
            A.e.activation(dst[:, k, 0:nt * P], PS[:, k % 4, 0:nt * P], ACT.Copy, scale=gain(k))\
                .then_inc(sem(tag, "tev"), 1)

    def half(hh):
        return slice(HD * hh, HD * hh + HD)

    def zf_act(A):
        def evac(gi, b, n):
            c = gi * 4 + b
            if gi < 4:
                A.e.activation(ZS[c][:, :], PS[:, b, :], ACT.Copy, scale=SM[:, 200 + c:201 + c])\
                    .then_inc(S("zf_main"), 1)
            else:
                A.e.activation(UG[:, b, :], PS[:, b, :], ACT.Gelu_apprx_tanh).then_inc(sem("zf", "ev"), 1)
        return evac

    def zf_dve(V):
        def evac(gi, b, n):
            c = gi * 4 + b
            if gi == 4:
                return
            V.e.wait_ge(S("zf_main"), n + 1)
            V.mine(V.e.scalar_tensor_tensor(ZS[c][:, 1:SEQ], PS[:, b, 0:SEQ - 1], col("ab_shift_prev", c),
                                            ZS[c][:, 1:SEQ], ALU.mult, ALU.add))
            V.wait_mine()
            V.e.scalar_tensor_tensor(ZS[c][:, 0:SEQ - 1], PS[:, b, 1:SEQ], col("ab_shift_next", c),
                                     ZS[c][:, 0:SEQ - 1], ALU.mult, ALU.add).then_inc(sem("zf", "ev"), 1)
        return evac

    def zf_freed(gi, b):
        _, nb, banks = gemms["zf"][gi - 1]
        return [at("zf", "ev", banks + min(b, nb - 1) + 1)]

    def sgu_act(A):
        e = A.e
        for t in range(NT):
            e.activation(SQ1[:, 0:512], VG[:, t, :], ACT.Square, accum_out=SM[:, t:t + 1]).then_inc(S("sgu_sq"), 1)
            e.wait_ge(S("sgu_sq"), t + 1)
        e.wait_ge(S("wst_tp"), 1)
        e.activation(WST[:, :, :], PS[:, 4, :].rearrange("p (g q) -> p g q", g=4), ACT.Copy).then_inc(S("wst"), 1)
        for g in range(SGU_G):
            e.wait_ge(S("sgu_b"), g + 1)
            e.activation(HHI[4 + g][:, :], BT[g % 2][:, :], ACT.Copy).then_inc(S("sgu_hi"), 1)

    def sgu_pool(G):
        G.e.wait_ge(S("sgu_var"), 1)
        G.e.tensor_tensor(SM[:, 8:12], SM[:, 4:8], SM[:, 16:20], ALU.pow).then_inc(S("sgu_rstd"), 1)

    def sgu_dve(V):
        e = V.e
        e.wait_ge(S("sgu_sq"), NT)
        e.tensor_scalar(SM[:, 4:8], SM[:, 0:4], 1.0 / 512, EPS, ALU.mult, ALU.add).then_inc(S("sgu_var"), 1)
        e.wait_ge(S("sgu_rstd"), 1)
        for t in range(NT):
            e.tensor_scalar(VG[:, t, :], VG[:, t, :], SM[:, 8 + t:9 + t], None, ALU.mult).then_inc(S("sgu_vg"), 1)
        for g in range(SGU_G):
            e.wait_ge(S("sgu_mm"), g + 1)
            if g >= 2:
                e.wait_ge(S("sgu_lo"), g - 1)
            b = BT[g % 2]
            V.mine(e.scalar_tensor_tensor(b[:, :].rearrange("p (n q) -> p n q", n=NT),
                                          PS[:, g, :].rearrange("p (n q) -> p n q", n=NT), col("sgu_v_gain", g),
                                          SGUB[:, g, :].unsqueeze(1).to_broadcast([P, NT, P]), ALU.mult, ALU.add))
            V.wait_mine()
            e.tensor_tensor(b[:, :], b[:, :], UG[:, g, :], ALU.mult).then_inc(S("sgu_b"), 1)
            e.wait_ge(S("sgu_hi"), g + 1)
            e.tensor_tensor(HLO[4 + g][:, :], b[:, :], HHI[4 + g][:, :].bitcast(F32), ALU.subtract)\
                .then_inc(S("sgu_lo"), 1)

    def sgu_pe(T):
        e = T.e
        for g in range(SGU_G):
            mm = e.transpose(PS[:, 4, g * P:g * P + P], WS[:, g, :], ident)
        mm.then_inc(S("wst_tp"), 1)
        e.wait_ge(S("wst"), 1)
        e.wait_ge(S("sgu_vg"), NT)
        for g in range(SGU_G):
            for n in range(NT):
                mm = e.matmul(PS[:, g, n * P:n * P + P], VG[:, n, g * P:g * P + P], WST[:, g, :], start=True, stop=True)
            mm.then_inc(S("sgu_mm"), 1)

    ZR, ZK, ZV, ZW, ZA, ZG = 0, 4, 8, 12, 13, 14

    def rw0_act(A):
        e = A.e
        e.activation(ZS[ZW][:, :], ZS[ZW][:, :], ACT.Tanh).then_inc(S("rw0_tanh"), 1)
        e.activation(ZS[ZG][:, :], ZS[ZG][:, :], ACT.Tanh, scale=0.5).then_inc(S("rw0_tanh"), 1)
        for t in range(NT):
            e.wait_ge(S("rw0_vtp"), t + 1)
            e.activation(VTK[:, t, :], PS[:, 4 + t, :], ACT.Copy).then_inc(S("rw0_vtk"), 1)
        for j in range(NJ):
            e.wait_ge(S("rw0_ss"), j + 1)
            e.activation(TMP[j][:, :], PS[:, j, :], ACT.Sqrt, bias=SM[:, 24:25]).then_inc(S("rw0_norm"), 1)

    def rw0_pe(T):
        e = T.e
        for t in range(NT):
            for j in range(NJ):
                mm = e.transpose(PS[:, 4 + t, j * P:j * P + P], ZS[ZV + j][:, t * P:t * P + P], ident)
            mm.then_inc(S("rw0_vtp"), 1)
        for j in range(NJ):
            e.wait_ge(S("rw0_sq"), j + 1)
            e.matmul(PS[:, j, :], rk("bones"), TMP[j][:, :], start=True, stop=True).then_inc(S("rw0_ss"), 1)

    def rw0_dve(V):
        e = V.e
        e.memset(BPD[:, :, :, :], 0.0)
        e.memset(KPD[:, :, :, :], 0.0)
        e.memset(ALP[:, :, :], 0.0)
        e.memset(RHO[:, :, :], 0.0)
        for j in range(NJ):
            V.mine(e.tensor_scalar(KK[:, j, :], ZS[ZK + j][:, :], col("rwkv_k_k", j), None, ALU.mult))
            V.wait_mine()
            e.tensor_tensor(TMP[j][:, :], KK[:, j, :], KK[:, j, :], ALU.mult).then_inc(S("rw0_sq"), 1)
        e.wait_ge(S("rw0_tanh"), 2)
        e.tensor_scalar(ZS[ZG][:, :], ZS[ZG][:, :], 0.5, 0.5, ALU.mult, ALU.add)
        for j in range(NJ):
            e.wait_ge(S("rw0_norm"), j + 1)
            V.mine(e.reciprocal(TMP[j][:, :], TMP[j][:, :]))
            V.wait_mine()
            e.tensor_tensor(KK[:, j, :], KK[:, j, :], TMP[j][:, :], ALU.mult)

    def pair_pe(T, d, j):
        e, n = T.e, d * NJ + j
        e.matmul(PS[:, 0, :], WL2[half(d), 0, j * P:j * P + P], ZS[ZW][half(d), :], start=True, stop=True)\
            .then_inc(S("p_lora"), 1)
        e.matmul(PS[:, 1, :], WL2[half(d), 1, j * P:j * P + P], ZS[ZA][half(d), :], start=True, stop=True)\
            .then_inc(S("p_lora"), 1)
        e.wait_ge(S("p_bon"), n + 1)
        e.matmul(PS[:, 2, :], rk("bones"), TMP[0][:, :], start=True, stop=True).then_inc(S("p_bonmm"), 1)
        e.wait_ge(S("p_fm"), n + 1)
        for hh in range(2):
            for t in range(NT):
                mm = e.transpose(PS[:, 3 + 4 * hh, t * HD:t * HD + HD], ALP[half(hh), hh, t * P:t * P + P],
                                 KC[half(hh), HD * hh:HD * hh + HD])
        mm.then_inc(S("p_tok"), 1)
        for q, src in enumerate((BET, KAP)):
            for t in range(NT):
                mm = e.transpose(PS[:, 4 + q, t * P:t * P + P], src[:, t * P:t * P + P], ident)
            mm.then_inc(S("p_tok"), 1)
        e.wait_ge(S("p_lorafree"), 2 * (n + 1))
        for g in range(2):
            for u in range(4 * g, 4 * g + 4):
                t, hh = divmod(u, 2)
                mm = e.matmul(PS[:, g, (u % 4) * P:(u % 4) * P + P], ALP[:, hh, t * P:t * P + P],
                              BET[:, t * P:t * P + P], start=True, stop=True)
            mm.then_inc(S("p_a"), 1)
        for q, (l, r) in enumerate(((KAP, ALP), (BET, RHO), (KAP, RHO))):
            for g in range(2):
                bank = (6, 7, 2, 3, 4, 5)[2 * q + g]
                if bank == 2:
                    e.wait_ge(S("p_bonfree"), n + 1)
                if bank == 7:
                    e.wait_ge(S("p_tokfree"), 3 * n + 1)
                if bank == 4:
                    e.wait_ge(S("p_tokfree"), 3 * n + 3)
                for t in (2 * g, 2 * g + 1):
                    mm = e.matmul(PS[:, bank, (t % 2) * 256:(t % 2) * 256 + 256].rearrange("p (h q) -> p h q", h=2),
                                  l[:, t * P:t * P + P], r[:, 0:2, t * P:t * P + P], start=True, stop=True)
                mm.then_inc(S("p_g"), 1)
        for g in range(2):
            e.wait_ge(S("p_t1"), 2 * n + g + 1)
            for u in range(4 * g, 4 * g + 4):
                mm = e.transpose(PS[:, g, (u % 4) * P:(u % 4) * P + P], TT[:, u, :], ident)
            mm.then_inc(S("p_u1"), 1)
        e.wait_ge(S("p_gfree"), 6 * (n + 1))
        for lv in range(5):
            for g in range(2):
                e.wait_ge(S("p_u"), (n * 6 + lv) * 2 + g + 1)
                for u in range(4 * g, 4 * g + 4):
                    mm = e.matmul(PS[:, 2 + g, (u % 4) * P:(u % 4) * P + P], AI[:, u, :], UU[:, u, :], start=True, stop=True)
                mm.then_inc(S("p_x"), 1)
            for g in range(2):
                e.wait_ge(S("p_xm"), (n * 5 + lv) * 2 + g + 1)
                for u in range(4 * g, 4 * g + 4):
                    mm = e.matmul(PS[:, g, (u % 4) * P:(u % 4) * P + P], TT[:, u, :], XX[:, u, :], start=True, stop=True)
                mm.then_inc(S("p_un"), 1)
                if lv < 4:
                    for u in range(4 * g, 4 * g + 4):
                        mm = e.matmul(PS[:, 4 + g, (u % 4) * P:(u % 4) * P + P], XX[:, u, :], TT[:, u, :], start=True, stop=True)
                    mm.then_inc(S("p_tn"), 1)
        for g in range(2):
            for u in range(4 * g, 4 * g + 4):
                t = u // 2
                mm = e.matmul(PS[:, 6 + g, (u % 4) * P:(u % 4) * P + P], GKA[:, u, :], VTK[:, t, j * P:j * P + P],
                              start=True, stop=True)
            mm.then_inc(S("p_x0"), 1)
        for g in range(2):
            e.wait_ge(S("p_u"), (n * 6 + 5) * 2 + g + 1)
            e.wait_ge(S("p_ax"), 2 * n + g + 1)
            for u in range(4 * g, 4 * g + 4):
                mm = e.matmul(PS[:, 2 + g, (u % 4) * P:(u % 4) * P + P], UU[:, u, :], AXT[:, u, :], start=True, stop=True)
            mm.then_inc(S("p_wu"), 1)
        e.wait_ge(S("p_wuc"), 2 * (n + 1))
        e.wait_ge(S("p_ax"), 2 * (n + 1))
        for u in range(8):
            t, hh = divmod(u, 2)
            mm = e.matmul(PS[half(hh), 4, t * P:t * P + P], WU[:, u, 0:HD], GBR[:, u, :], start=True, stop=True)
        mm.then_inc(S("p_r"), 1)
        for u in range(8):
            t, hh = divmod(u, 2)
            o = PS[half(hh), 5, t * P:t * P + P]
            e.matmul(o, WU[:, u, HD:P], GBR[:, u, :], start=True, stop=False)
            mm = e.matmul(o, VTK[:, t, j * P + HD * hh:j * P + HD * hh + HD], GKR[:, u, :], start=False, stop=True)
        mm.then_inc(S("p_y"), 1)
        for u in range(8):
            t, hh = divmod(u, 2)
            mm = e.matmul(PS[half(hh), 6, t * P:t * P + P].rearrange("p (c k) -> p c k", c=2), WU[:, u, 0:HD],
                          BPD[:, t, :, HD * hh:HD * hh + HD], start=True, stop=True)
        mm.then_inc(S("p_p"), 1)
        for u in range(8):
            t, hh = divmod(u, 2)
            for c in range(2):
                o = PS[half(hh), 7, (2 * t + c) * HD:(2 * t + c) * HD + HD]
                e.matmul(o, BPD[:, t, c, HD * hh:HD * hh + HD], WU[:, u, HD:P], start=True, stop=False)
                mm = e.matmul(o, KPD[:, t, c, HD * hh:HD * hh + HD], VTK[:, t, j * P + HD * hh:j * P + HD * hh + HD],
                              start=False, stop=True)
        mm.then_inc(S("p_q"), 1)
        e.wait_ge(S("p_end"), 4 * (n + 1))

    def pair_act(A, d, j):
        e, n = A.e, d * NJ + j
        c8 = d * NJ + j
        e.wait_ge(S("p_lora"), 2 * n + 1)
        e.activation(TMP[0][:, :], PS[:, 0, :], ACT.Tanh, scale=0.5, bias=SM[:, 216 + c8:217 + c8]).then_inc(S("p_lorafree"), 1)
        e.wait_ge(S("p_lora"), 2 * n + 2)
        e.activation(TMP[1][:, :], PS[:, 1, :], ACT.Tanh, scale=0.5, bias=SM[:, 224 + c8:225 + c8]).then_inc(S("p_lorafree"), 1)
        e.wait_ge(S("p_c"), n + 1)
        e.activation(TMP[3][:, :], TMP[3][:, :], ACT.Exp).then_inc(S("p_e"), 1)
        e.activation(TMP[0][:, :], TMP[2][:, :], ACT.Exp).then_inc(S("p_e"), 1)
        e.wait_ge(S("p_e"), 3 * n + 2)
        e.activation(TMP[2][:, :], TMP[2][:, :], ACT.Exp, scale=-1.0).then_inc(S("p_e"), 1)
        e.wait_ge(S("p_tok"), 3 * n + 1)
        for hh in range(2):
            i = e.activation(AXT[:, :, 0:HD].rearrange("p (t h) k -> p t h k", h=2)[:, :, hh, :],
                             PS[:, 3 + 4 * hh, 0:NT * HD].rearrange("p (t k) -> p t k", t=NT), ACT.Copy)
        i.then_inc(S("p_tokfree"), 1)
        for q, dst in enumerate((BPD, KPD)):
            e.wait_ge(S("p_tok"), 3 * n + 2 + q)
            for c in range(2):
                i = e.activation(dst[half(c), :, c, :], PS[half(c), 4 + q, :].rearrange("p (t k) -> p t k", t=NT), ACT.Copy)
            i.then_inc(S("p_tokfree"), 1)
        for g in range(2):
            e.wait_ge(S("p_u1"), 2 * n + g + 1)
            e.activation(UU[:, 4 * g:4 * g + 4, :], PS[:, g, :].rearrange("p (u k) -> p u k", u=4), ACT.Copy)\
                .then_inc(S("p_u"), 1)
        for lv in range(5):
            for g in range(2):
                e.wait_ge(S("p_un"), (n * 5 + lv) * 2 + g + 1)
                if lv < 4:
                    e.wait_ge(S("p_tn"), (n * 4 + lv) * 2 + g + 1)
                    A.mine(e.activation(TT[:, 4 * g:4 * g + 4, :], PS[:, 4 + g, :].rearrange("p (u k) -> p u k", u=4), ACT.Copy))
                e.activation(UU[:, 4 * g:4 * g + 4, :], PS[:, g, :].rearrange("p (u k) -> p u k", u=4), ACT.Copy)\
                    .then_inc(S("p_u"), 1)
        for g in range(2):
            e.wait_ge(S("p_x0"), 2 * n + g + 1)
            for hh in range(2):
                i = e.activation(
                    AXT[:, 4 * g:4 * g + 4, HD:P].rearrange("p (t h) k -> p t h k", h=2)[:, :, hh, :],
                    PS[:, 6 + g, :].rearrange("p (t h k) -> p t h k", h=2, k=P)[:, :, hh, HD * hh:HD * hh + HD], ACT.Copy)
            i.then_inc(S("p_ax"), 1)
        for g in range(2):
            e.wait_ge(S("p_wu"), 2 * n + g + 1)
            e.activation(WU[:, 4 * g:4 * g + 4, :], PS[:, 2 + g, :].rearrange("p (u k) -> p u k", u=4), ACT.Copy)\
                .then_inc(S("p_wuc"), 1)
        e.wait_ge(S("p_q"), n + 1)
        e.activation(QT[:, j, :, :], PS[:, 7, :].rearrange("p (c k) -> p c k", k=HD), ACT.Copy).then_inc(S("p_end"), 1)

    def pair_dve(V, d, j):
        e, n = V.e, d * NJ + j
        c8 = n
        r, k, kk = ZS[ZR + j], ZS[ZK + j], KK[:, j, :]
        e.wait_ge(S("p_lorafree"), 2 * n + 1)
        V.mine(e.tensor_scalar(TMP[0][:, :], TMP[0][:, :], -0.5 * DECAY, -0.5 * DECAY, ALU.mult, ALU.add))
        e.wait_ge(S("p_lorafree"), 2 * n + 2)
        V.mine(e.tensor_scalar(TMP[1][:, :], TMP[1][:, :], 0.5, 0.5, ALU.mult, ALU.add))
        V.wait_mine()
        if d == 0:
            V.mine(e.tensor_tensor_scan(TMP[2][:, :], rk("reset"), TMP[0][:, :], 0.0, ALU.mult, ALU.add))
        else:
            V.mine(e.tensor_tensor_scan(TMP[2][:, ::-1], rk("reset"), TMP[0][:, ::-1], 0.0, ALU.mult, ALU.add))
        V.wait_mine()
        e.tensor_tensor(TMP[3][:, :], TMP[2][:, :], TMP[0][:, :], ALU.subtract).then_inc(S("p_c"), 1)
        e.wait_ge(S("p_e"), 3 * n + 1)
        for hh in range(2):
            e.scalar_tensor_tensor(ALP[half(hh), hh, :], KK[half(hh), j, :], -1.0, TMP[3][half(hh), :], ALU.mult, ALU.mult)
        e.wait_ge(S("p_e"), 3 * n + 2)
        for hh in range(2):
            V.mine(e.tensor_tensor(RHO[half(hh), hh, :], r[half(hh), :], TMP[0][half(hh), :], ALU.mult))
        last = CH - 1 if d == 0 else 0
        V.mine(e.tensor_copy(SM[:, 128 + j * NCH:128 + (j + 1) * NCH], TMP[0][:, last::CH]))
        e.wait_ge(S("p_e"), 3 * n + 3)
        V.wait_mine()
        V.mine(e.tensor_scalar(TMP[3][:, :], TMP[1][:, :], col("rwkv_k_a", j), SM[:, 232 + j:233 + j], ALU.mult, ALU.add))
        V.mine(e.tensor_tensor(BET[:, :], kk, TMP[1][:, :], ALU.mult))
        V.wait_mine()
        V.mine(e.tensor_tensor(TMP[3][:, :], TMP[3][:, :], k[:, :], ALU.mult))
        V.wait_mine()
        e.scalar_tensor_tensor(TMP[0][:, :], TMP[3][:, :], col("rwkv_r_k", j), r[:, :], ALU.mult, ALU.mult)\
            .then_inc(S("p_bon"), 1)
        e.tensor_tensor(BET[:, :], BET[:, :], TMP[2][:, :], ALU.mult)
        e.tensor_tensor(KAP[:, :], TMP[3][:, :], TMP[2][:, :], ALU.mult).then_inc(S("p_fm"), 1)
        e.wait_ge(S("p_bonmm"), n + 1)
        if d == 0:
            e.tensor_copy(BON[j][:, :], PS[:, 2, :]).then_inc(S("p_bonfree"), 1)
        else:
            e.tensor_tensor(BON[j][:, :], BON[j][:, :], PS[:, 2, :], ALU.add).then_inc(S("p_bonfree"), 1)
        id4 = ident.unsqueeze(1).to_broadcast([P, 4, P])
        fb = "fb"[d]
        for g in range(2):
            e.wait_ge(S("p_a"), 2 * n + g + 1)
            ai, tt = AI[:, 4 * g:4 * g + 4, :], TT[:, 4 * g:4 * g + 4, :]
            V.mine(e.tensor_tensor(ai, PS[:, g, :].rearrange("p (u k) -> p u k", u=4), mask4("LT" if d == 0 else "UT"), ALU.mult))
            V.wait_mine()
            V.mine(e.tensor_tensor(ai, ai, id4, ALU.add))
            V.wait_mine()
            e.tensor_tensor(tt, ai, mask4("T1" + fb), ALU.mult).then_inc(S("p_t1"), 1)
        for q, (dst, m) in enumerate(((GKA, "UT" if d == 0 else "LT"), (GBR, "UTI" if d == 0 else "LTI"),
                                      (GKR, "UTI" if d == 0 else "LTI"))):
            for g in range(2):
                bank = (6, 7, 2, 3, 4, 5)[2 * q + g]
                e.wait_ge(S("p_g"), 6 * n + 2 * q + g + 1)
                e.tensor_tensor(dst[:, 4 * g:4 * g + 4, :], PS[:, bank, :].rearrange("p (u k) -> p u k", u=4), mask4(m),
                                ALU.mult).then_inc(S("p_gfree"), 1)
        for lv in range(5):
            for g in range(2):
                e.wait_ge(S("p_x"), (n * 5 + lv) * 2 + g + 1)
                e.tensor_tensor(XX[:, 4 * g:4 * g + 4, :], PS[:, 2 + g, :].rearrange("p (u k) -> p u k", u=4),
                                mask4(f"X{fb}{lv + 2}"), ALU.mult).then_inc(S("p_xm"), 1)
        e.wait_ge(S("p_r"), n + 1)
        for hh in range(2):
            i = e.tensor_tensor(RT[half(hh), j, :], PS[half(hh), 4, :], RHO[half(hh), hh, :], ALU.add)
        i.then_inc(S("p_end"), 1)
        e.wait_ge(S("p_y"), n + 1)
        if d == 0:
            e.tensor_copy(YL[:, j, :], PS[:, 5, :]).then_inc(S("p_end"), 1)
        else:
            e.tensor_tensor(YL[:, j, :], YL[:, j, :], PS[:, 5, :], ALU.add).then_inc(S("p_end"), 1)
        e.wait_ge(S("p_p"), n + 1)
        e.tensor_tensor(PT[:, j, :, :], PS[:, 6, :].rearrange("p (c k) -> p c k", k=HD),
                        rk("ident2").unsqueeze(1).to_broadcast([P, NCH, HD]), ALU.add).then_inc(S("p_end"), 1)

    def order(d):
        return list(range(NCH)) if d == 0 else list(range(NCH - 1, -1, -1))

    def chain_pe(T, d):
        e, o = T.e, order(d)
        for i in range(1, NCH):
            e.wait_ge(S("c_state"), d * NCH + i)
            for hh in range(2):
                for j in range(NJ):
                    mm = e.matmul(PS[half(hh), hh, j * HD:j * HD + HD], PT[half(hh), j, o[i], :],
                                  QT[half(hh), j, o[i - 1], :], start=True, stop=True)
            mm.then_inc(S("c_mm"), 1)
        e.wait_ge(S("c_yfree"), 2 * d + 2)
        for hh in range(2):
            for j in range(NJ):
                for i in range(1, NCH):
                    c = o[i]
                    mm = e.matmul(PS[half(hh), j + 4 * hh, c * HD:c * HD + HD], QT[half(hh), j, o[i - 1], :],
                                  RT[half(hh), j, c * CH:c * CH + CH], start=True, stop=True)
                mm.then_inc(S("c_y"), 1)

    def chain_dve(V, d):
        e, o = V.e, order(d)
        for i in range(NCH):
            c = o[i]
            if i > 0:
                e.wait_ge(S("c_mm"), d * (NCH - 1) + i)
                for hh in range(2):
                    s = QT[half(hh), :, c, :]
                    V.mine(e.tensor_tensor(s, s, PS[half(hh), hh, 0:NJ * HD].rearrange("p (j v) -> p j v", j=NJ), ALU.add))
                V.wait_mine()
            s = QT[:, :, c, :]
            ecl = SM[:, 128:128 + NJ * NCH].rearrange("p (j c) -> p j c", c=NCH)[:, :, c]
            e.tensor_tensor(s, s, ecl.unsqueeze(2).to_broadcast([P, NJ, HD]), ALU.mult).then_inc(S("c_state"), 1)
        e.drain().then_inc(S("c_yfree"), 2)
        lo, hi = (1, NCH) if d == 0 else (0, NCH - 1)
        for hh in range(2):
            for j in range(NJ):
                e.wait_ge(S("c_y"), d * 2 * NJ + hh * NJ + j + 1)
                y = YL[half(hh), j, lo * CH:hi * CH]
                e.tensor_tensor(y, y, PS[half(hh), j + 4 * hh, lo * CH:hi * CH], ALU.add)

    def fin_pe(T):
        e = T.e
        for j in range(NJ):
            e.wait_ge(S("f_sq"), j + 1)
            if j >= 2:
                e.wait_ge(S("f_out"), j - 1)
            e.matmul(PS[:, 2 * (j % 2), :], rk("bones"), YQ[j % 2][:, :], start=True, stop=True).then_inc(S("f_mm"), 1)
            e.matmul(PS[:, 2 * (j % 2) + 1, :], WL2[:, 2, j * P:j * P + P], ZS[ZG][:, :], start=True, stop=True)\
                .then_inc(S("f_mm"), 1)

    def fin_act(A):
        e = A.e
        for j in range(NJ):
            if j >= 2:
                e.wait_ge(S("f_out"), j - 1)
            e.activation(YQ[j % 2][:, :], YL[:, j, :], ACT.Square).then_inc(S("f_sq"), 1)
            e.wait_ge(S("f_mm"), 2 * j + 1)
            e.activation(YQ[2 + j % 2][:, :], PS[:, 2 * (j % 2), :], ACT.Sqrt, scale=1.0 / HD, bias=SM[:, 25:26])\
                .then_inc(S("f_norm"), 1)
            e.wait_ge(S("f_out"), j + 1)
            e.activation(HHI[j][:, :], YQ[2 + j % 2][:, :], ACT.Copy).then_inc(S("f_hi"), 1)

    def fin_dve(V):
        e = V.e
        for j in range(NJ):
            y = YQ[2 + j % 2]
            e.wait_ge(S("f_norm"), j + 1)
            V.mine(e.reciprocal(y[:, :], y[:, :]))
            V.mine(e.tensor_tensor(BON[j][:, :], BON[j][:, :], ZS[ZV + j][:, :], ALU.mult))
            V.wait_mine()
            V.mine(e.tensor_tensor(y[:, :], y[:, :], YL[:, j, :], ALU.mult))
            V.wait_mine()
            V.mine(e.scalar_tensor_tensor(y[:, :], y[:, :], col("rwkv_out_gain", j), BON[j][:, :], ALU.mult, ALU.add))
            V.wait_mine()
            e.wait_ge(S("f_mm"), 2 * j + 2)
            e.tensor_tensor(y[:, :], y[:, :], PS[:, 2 * (j % 2) + 1, :], ALU.mult).then_inc(S("f_out"), 1)
            e.wait_ge(S("f_hi"), j + 1)
            e.wait_ge(S("f_out"), j + 1)
            V.mine(e.tensor_tensor(HLO[j][:, :], y[:, :], HHI[j][:, :].bitcast(F32), ALU.subtract))
            V.wait_mine()

    SC = 1.0 / math.sqrt(XD)

    def xattn_pe(T, l):
        e = T.e
        for t in range(NT):
            for h in range(XH):
                bank = 4 * (t % 2) + h // 2
                if h % 2 == 0 and t >= 2:
                    e.wait_ge(*at(f"xa{l}", "xe", XH * (t - 1)))
                for k in range(2):
                    mm = e.matmul(PS[:, bank, (h % 2) * MEM:(h % 2) * MEM + MEM], QFT[:, 2 * h + k, t * P:t * P + P],
                                  KFT[:, 2 * h + k, :], start=(k == 0), stop=(k == 1))
            mm.then_inc(sem(f"xa{l}", "xl"), 1)
            if t >= 1:
                xturn_pe(e, l, t - 1)
        xturn_pe(e, l, NT - 1)
        e.wait_ge(*at(f"xa{l}", "xpc", 2 * NT))
        for c in range(DC):
            if c >= 4:
                e.wait_ge(*at(f"xa{l}", "xolo", c - 3))
            for k in range(MT):
                mm = e.matmul(PS[:, c % 4, :], VMEM[:, k, c * P:c * P + P], PTR[:, c // 2, k, :], start=(k == 0), stop=(k == 1))
            mm.then_inc(sem(f"xa{l}", "xpv"), 1)

    def xturn_pe(e, l, t):
        e.wait_ge(*at(f"xa{l}", "xn", t + 1))
        if t >= 2:
            e.wait_ge(*at(f"xa{l}", "xpc", 2 * (t - 1)))
        for hp in range(2):
            for q in range(4):
                h, k = 2 * hp + q // 2, q % 2
                mm = e.transpose(PS[:, 4 * (t % 2) + 2 + hp, q * P:q * P + P], EX[t % 2][:, h, k * P:k * P + P], ident)
            mm.then_inc(sem(f"xa{l}", "xtp"), 1)

    def xattn_act(A, l):
        e = A.e
        for t in range(NT):
            e.wait_ge(*at(f"xa{l}", "xmx", t + 1))
            for h in range(XH):
                e.activation(EX[t % 2][:, h, :], PS[:, 4 * (t % 2) + h // 2, (h % 2) * MEM:(h % 2) * MEM + MEM], ACT.Exp,
                             scale=SC, bias=SM[:, 40 + 4 * (t % 2) + h:41 + 4 * (t % 2) + h],
                             accum_out=SM[:, 48 + 4 * (t % 2) + h:49 + 4 * (t % 2) + h]).then_inc(sem(f"xa{l}", "xe"), 1)
            if t >= 1:
                xcopy_act(e, l, t - 1)
        xcopy_act(e, l, NT - 1)
        for c in range(DC):
            e.wait_ge(*at(f"xa{l}", "xpv", c + 1))
            e.activation(HHI[c][:, :], PS[:, c % 4, :], ACT.Copy).then_inc(sem(f"xa{l}", "xohi"), 1)

    def xcopy_act(e, l, t):
        for hp in range(2):
            e.wait_ge(*at(f"xa{l}", "xtp", 2 * t + hp + 1))
            e.activation(PTR[:, 2 * hp:2 * hp + 2, :, t * P:t * P + P],
                         PS[:, 4 * (t % 2) + 2 + hp, :].rearrange("p (h k q) -> p h k q", h=2, k=2), ACT.Copy)\
                .then_inc(sem(f"xa{l}", "xpc"), 1)

    def xattn_dve(V, l):
        e = V.e
        for t in range(NT):
            b = 4 * (t % 2)
            e.wait_ge(*at(f"xa{l}", "xl", t + 1))
            if t >= 2:
                e.wait_ge(*at(f"xa{l}", "xtp", 2 * (t - 1)))
            for q in range(2):
                V.mine(e.tensor_reduce(SM[:, 32 + b + 2 * q:34 + b + 2 * q], PS[:, b + q, :].rearrange("p (h k) -> p h k", h=2),
                                       AX.X, ALU.max))
            V.wait_mine()
            e.tensor_scalar(SM[:, 40 + b:44 + b], SM[:, 32 + b:36 + b], -SC, None, ALU.mult).then_inc(sem(f"xa{l}", "xmx"), 1)
            e.wait_ge(*at(f"xa{l}", "xe", XH * (t + 1)))
            V.mine(e.reciprocal(SM[:, 56 + b:60 + b], SM[:, 48 + b:52 + b]))
            V.wait_mine()
            v = EX[t % 2][:, :, :]
            e.tensor_tensor(v, v, SM[:, 56 + b:60 + b].unsqueeze(2).to_broadcast([P, XH, MEM]), ALU.mult)\
                .then_inc(sem(f"xa{l}", "xn"), 1)
        for c in range(DC):
            e.wait_ge(*at(f"xa{l}", "xohi", c + 1))
            e.tensor_tensor(HLO[c][:, :], PS[:, c % 4, :], HHI[c][:, :].bitcast(F32), ALU.subtract).then_inc(sem(f"xa{l}", "xolo"), 1)

    def convw(l, tap, c):
        i = (l * 3 + tap) * 44 + c
        tile, row = divmod(i, 88)
        return COLS[:, (2 + tile) * P + row:(2 + tile) * P + row + 1]

    def up_act(A, l, h):
        name = f"up{l}{h}"

        def evac(gi, b, n):
            c = 12 * h + 2 * gi + b % 2
            dst = (CG if b < 2 else CV)[b % 2]
            cc = c if b < 2 else FC + c
            if gi > 0:
                A.e.wait_ge(*at(name, "lo", 2 * (gi - 1) + b % 2 + 1))
            A.e.activation(dst[:, :], PS[:, b, :], ACT.Identity, scale=convw(l, 1, cc),
                           bias=col("ffn_conv_b", l * 44 + cc)).then_inc(sem(name, "main"), 1)
            if b < 2:
                A.e.wait_ge(*at(name, "ev", n + 1))
                A.e.activation(SG[b][:, :], CG[b][:, :], ACT.Silu).then_inc(sem(name, "silu"), 1)
            else:
                A.e.wait_ge(*at(name, "g", 2 * gi + b - 1))
                A.e.activation(GHI[2 * gi + b - 2][:, :], SG[b - 2][:, :], ACT.Copy).then_inc(sem(name, "hi"), 1)
        return evac

    def up_dve(V, l, h):
        name = f"up{l}{h}"

        def evac(gi, b, n):
            c = 12 * h + 2 * gi + b % 2
            cc = c if b < 2 else FC + c
            dst = (CG if b < 2 else CV)[b % 2]
            V.e.wait_ge(*at(name, "main", n + 1))
            V.mine(V.e.scalar_tensor_tensor(dst[:, 1:SEQ], PS[:, b, 0:SEQ - 1], convw(l, 0, cc), dst[:, 1:SEQ],
                                            ALU.mult, ALU.add))
            V.wait_mine()
            V.e.scalar_tensor_tensor(dst[:, 0:SEQ - 1], PS[:, b, 1:SEQ], convw(l, 2, cc), dst[:, 0:SEQ - 1],
                                     ALU.mult, ALU.add).then_inc(sem(name, "ev"), 1)
            if b >= 2:
                i = 2 * gi + b - 2
                V.e.wait_ge(*at(name, "silu", i + 1))
                V.e.wait_ge(*at(name, "ev", n + 1))
                V.e.tensor_tensor(SG[b - 2][:, :], SG[b - 2][:, :], CV[b - 2][:, :], ALU.mult).then_inc(sem(name, "g"), 1)
                V.e.wait_ge(*at(name, "hi", i + 1))
                V.e.tensor_tensor(GLO[i][:, :], SG[b - 2][:, :], GHI[i][:, :].bitcast(F32), ALU.subtract)\
                    .then_inc(sem(name, "lo"), 1)
        return evac

    DSC = 1.0 / math.sqrt(DHD)

    def dlog_pe(e, m):
        h, t = divmod(m, NT)
        b = 2 * (m % 2)
        if m >= 2:
            e.wait_ge(S("ds"), 2 * (m - 1))
        for c in range(2):
            mm = e.matmul(PS[:, b + c, :], QF[HD * c:HD * c + HD, h, t * P:t * P + P], KF[HD * c:HD * c + HD, h, :],
                          start=True, stop=True)
            mm.then_inc(S("dl"), 1)

    def dturn_pe(e, m):
        e.wait_ge(S("dat"), m + 1)
        if m >= 2:
            e.wait_ge(S("datc"), m - 1)
        for k in range(NT):
            mm = e.transpose(PS[:, 4 + m % 2, k * P:k * P + P], AT[m % 2][:, k * P:k * P + P], ident)
        mm.then_inc(S("dtp"), 1)

    def dpv_pe(e, m):
        h, t = divmod(m, NT)
        e.wait_ge(S("datc"), m + 1)
        if t == 0 and h >= 2:
            e.wait_ge(S("dov"), h - 1)
        for k in range(NT):
            mm = e.matmul(PS[:, 6 + h % 2, t * P:t * P + P], ATT[m % 2][:, k, :], VV[:, k, h * P:h * P + P],
                          start=(k == 0), stop=(k == NT - 1))
        mm.then_inc(S("dpv"), 1)

    NM = DH * NT

    def dattn_pe(T):
        for m in range(NM + 2):
            if m < NM:
                dlog_pe(T.e, m)
            if 1 <= m <= NM:
                dturn_pe(T.e, m - 1)
            if m >= 2:
                dpv_pe(T.e, m - 2)

    def dattn_act(A):
        e = A.e

        def copy(m):
            e.wait_ge(S("dtp"), m + 1)
            if m >= 2:
                e.wait_ge(S("dpv"), m - 1)
            e.activation(ATT[m % 2][:, :, :], PS[:, 4 + m % 2, :].rearrange("p (k q) -> p k q", k=NT), ACT.Copy)\
                .then_inc(S("datc"), 1)

        def head(h):
            e.wait_ge(S("dpv"), NT * (h + 1))
            e.activation(OTK[:, :, h * P:h * P + P], PS[:, 6 + h % 2, :].rearrange("p (t k) -> p t k", t=NT), ACT.Copy)\
                .then_inc(S("dov"), 1)

        for m in range(NM):
            b = 2 * (m % 2)
            e.wait_ge(S("dmx"), m + 1)
            for c in range(2):
                e.activation(SS[m % 2][:, c, :], SS[m % 2][:, c, :], ACT.Exp, scale=DSC, bias=SM[:, 36 + b + c:37 + b + c],
                             accum_out=SM[:, 40 + b + c:41 + b + c]).then_inc(S("de"), 1)
            if m >= 1:
                copy(m - 1)
            if m >= 2 and (m - 2) % NT == NT - 1:
                head((m - 2) // NT)
        copy(NM - 1)
        head(DH - 1)

    def dattn_dve(V):
        e = V.e

        def first(m):
            h, t = divmod(m, NT)
            slope = 2.0 ** (-8.0 * (h + 1) / DH)
            b = 2 * (m % 2)
            for c in range(2):
                e.wait_ge(S("dl"), 2 * m + c + 1)
                e.scalar_tensor_tensor(SS[m % 2][:, c, :], KC[:, P + 384 - P * t:P + 384 - P * t + SEQ], -slope / DSC,
                                       PS[:, b + c, :], ALU.mult, ALU.add).then_inc(S("ds"), 1)
            e.wait_ge(S("ds"), 2 * m + 2)
            V.mine(e.tensor_reduce(SM[:, 32 + b:34 + b], SS[m % 2][:, :, :], AX.X, ALU.max))
            V.wait_mine()
            e.tensor_scalar(SM[:, 36 + b:38 + b], SM[:, 32 + b:34 + b], -DSC, None, ALU.mult).then_inc(S("dmx"), 1)

        def second(m):
            b = 2 * (m % 2)
            e.wait_ge(S("de"), 2 * m + 2)
            V.mine(e.reciprocal(SM[:, 48 + b:50 + b], SM[:, 40 + b:42 + b]))
            V.wait_mine()
            V.mine(e.tensor_tensor(SM[:, 49 + b:50 + b], SM[:, 49 + b:50 + b], SM[:, 26:27], ALU.mult))
            if m >= 2:
                e.wait_ge(S("dtp"), m - 1)
            V.mine(e.tensor_scalar(AT[m % 2][:, :], SS[m % 2][:, 0, :], SM[:, 48 + b:49 + b], None, ALU.mult))
            V.wait_mine()
            e.scalar_tensor_tensor(AT[m % 2][:, :], SS[m % 2][:, 1, :], SM[:, 49 + b:50 + b], AT[m % 2][:, :],
                                   ALU.mult, ALU.add).then_inc(S("dat"), 1)

        for m in range(NM + 1):
            if m < NM:
                first(m)
            if m >= 1:
                second(m - 1)

    def dout_act(A):
        e = A.e
        for k in range(DC):
            e.wait_ge(*at("do", "ttp", k + 1))
            e.activation(HHI[k][:, :], PS[:, k % 4, :], ACT.Copy, scale=SM[:, 27:28]).then_inc(sem("do", "hi"), 1)

    def dout_dve(V):
        e = V.e
        for k in range(DC):
            e.wait_ge(*at("do", "hi", k + 1))
            e.scalar_tensor_tensor(HLO[k][:, :], PS[:, k % 4, :], SM[:, 27:28], HHI[k][:, :].bitcast(F32), ALU.mult,
                                   ALU.subtract).then_inc(sem("do", "tev"), 1)

    def loads(e):
        for t in range(NT):
            e.dma_start(X[:, t, :], a["x"][0, t * P:t * P + P, :]).then_inc(S("x_in"), 16)
        e.dma_start(KC[:, :], a["keep"]).then_inc(S("c_in"), 16)
        n = 0
        for i, tile in enumerate(VEC_TILES):
            row = 0
            for name, rows in tile:
                src = a[name]
                if name in ("diff_q_gain", "diff_k_gain"):
                    for h in range(2):
                        e.dma_start(VROW[i][row:row + 1, HD * h:HD * h + HD], src[0:1, :]).then_inc(S("v_in"), 16)
                        n += 16
                else:
                    if name == "ffn_conv_w":
                        v = src.rearrange("l t (r p) -> (l t r) p", p=P)[(i - 2) * 88:(i - 1) * 88, :]
                    elif name in ("rwkv_r_k", "rwkv_out_gain"):
                        v = src.rearrange("e (r h) n -> (e r) (h n)", h=2)
                    elif name in ("rwkv_w0", "rwkv_a0"):
                        v = src.rearrange("e d (r p) -> (e d r) p", p=P)
                    elif name == "mem_norm":
                        v = src.rearrange("(r p) -> r p", p=P)
                    else:
                        v = src.rearrange("e (r p) -> (e r) p", p=P)
                    e.dma_start(VROW[i][row:row + rows, :], v).then_inc(S("v_in"), 16)
                    n += 16
                row += rows
        assert n == V_IN
        e.dma_start(RC[:, :], a["rkc"]).then_inc(S("c_in"), 16)
        e.dma_start(WL2[:, 0, :], a["rwkv_w2"].rearrange("e d r c -> (e d r) c")).then_inc(S("c_in"), 16)
        e.dma_start(WL2[:, 1, :], a["rwkv_a2"].rearrange("e d r c -> (e d r) c")).then_inc(S("c_in"), 16)
        e.dma_start(WL2[:, 2, :], a["rwkv_g2"][0]).then_inc(S("c_in"), 16)
        e.dma_start(WS[:, :, :], a["sgu_w_s"][0].rearrange("g p q -> p g q")).then_inc(S("c_in"), 16)
        e.dma_start(SGUB[:, :, :].rearrange("p g q -> p (g q)"),
                    a["sgu_b"].rearrange("e g q -> e (g q)").to_broadcast([P, 512])).then_inc(S("c_in"), 16)
        for i, name in enumerate(("q1", "k1", "q2", "k2")):
            e.dma_start(LAM[:, HD * i:HD * i + HD], a[f"diff_lambda_{name}"].to_broadcast([P, HD])).then_inc(S("c_in"), 16)

    C_IN = 16 * 11
    V_IN = 16 * (sum(len(t) for t in VEC_TILES) + 2)

    def setup_pe(T):
        T.e.wait_ge(S("v_in"), V_IN)
        T.e.wait_ge(S("c_in"), C_IN)
        T.e.wait_ge(S("v_zero"), 5)
        for i in range(5):
            T.e.transpose(PS[:, i // 4, (i % 4) * P:(i % 4) * P + P], VROW[i][:, :], ident).then_inc(S("v_tp"), 1)

    def setup_pool(G):
        G.e.memset(SM[:, 16:24], -0.5)
        G.e.memset(SM[:, 24:25], 1e-12)
        G.e.memset(SM[:, 25:26], EPS)

    def setup_dve(V):
        e = V.e
        e.wait_ge(S("v_in"), V_IN)
        e.wait_ge(S("v_tp"), 5)
        V.mine(e.tensor_copy(COLS[:, 0:4 * P], PS[:, 0, :]))
        V.mine(e.tensor_copy(COLS[:, 4 * P:5 * P], PS[:, 1, 0:P]))
        V.wait_mine()
        e.wait_ge(S("c_in"), C_IN)
        V.mine(e.tensor_tensor(SM[:, 200:215], col("ab_shift_prev", 0, 15), col("ab_shift_next", 0, 15), ALU.add))
        V.wait_mine()
        e.tensor_scalar(SM[:, 200:215], SM[:, 200:215], -1.0, 1.0, ALU.mult, ALU.add)
        e.tensor_scalar(SM[:, 216:224], col("rwkv_w0", 0, 8), 0.5, None, ALU.mult)
        e.tensor_scalar(SM[:, 224:232], col("rwkv_a0", 0, 8), 0.5, None, ALU.mult)
        e.tensor_scalar(SM[:, 232:236], col("rwkv_k_a", 0, 4), -1.0, 1.0, ALU.mult, ALU.add)
        e.tensor_scalar(SM[:, 27:28], col("diff_out_gain"), 1.0 - LAMBDA_INIT, None, ALU.mult)
        for i in range(2):
            V.mine(e.tensor_tensor(LAM[:, P * i:P * i + HD], LAM[:, P * i:P * i + HD], LAM[:, P * i + HD:P * i + P], ALU.mult))
        V.wait_mine()
        for i in range(2):
            e.tensor_reduce(SM[:, 28 + i:29 + i], LAM[:, P * i:P * i + HD], AX.X, ALU.add).then_inc(S("lam_dot"), 1)
        e.wait_ge(S("lam_exp"), 1)
        V.mine(e.tensor_tensor(SM[:, 26:27], SM[:, 29:30], SM[:, 28:29], ALU.subtract))
        V.wait_mine()
        e.tensor_scalar(SM[:, 26:27], SM[:, 26:27], -LAMBDA_INIT, None, ALU.add)

    def setup_act(A):
        A.e.wait_ge(S("lam_dot"), 2)
        A.e.activation(SM[:, 28:30], SM[:, 28:30], ACT.Exp).then_inc(S("lam_exp"), 1)
        A.e.wait_ge(S("x_in"), 16 * NT)

    def gcol(name, l=0):
        return lambda k: col(name, l * DC + k)

    def norm_shares(tag, nt):
        shares(tag, "norm", sq=nt, var=1, rstd=1, xn=nt, tp=DC, hi=DC, lo=DC)

    def turn_shares(tag, nt):
        shares(tag, "turn", gvar=1, grstd=1, gn=nt, ttp=DC, tev=DC, hi=DC if tag == "do" else 0)

    def stage_list():
        st = []

        def add(**kw):
            st.append(kw)

        def norm(tag, gain, src=X, xn=XN, sq=SQ, nt=NT, hi=hhi, lo=hlo, first=None):
            norm_shares(tag, nt)
            add(pe=lambda T: norm_pe(T, tag, xn, nt),
                act=lambda A: norm_act(A, tag, src, sq, nt, gain, hi),
                dve=lambda V: norm_dve(V, tag, src, xn, nt, gain, hi, lo),
                pool=lambda G: norm_pool(G, tag, nt))

        def product(name, hi, lo, tokens_out, nt, act=None, dve=None, freed=None, limit=None):
            fr = freed or one_evac(name)
            add(pe=lambda T: gemm_pe(T, name, hi, lo, tokens_out, nt, fr),
                act=lambda A: gemm_side(A, name, split_hi, act(A) if act else None, limit),
                dve=lambda V: gemm_side(V, name, split_lo, dve(V) if dve else None, limit))

        def copy_out(name, dst):
            def make(A):
                def evac(gi, b, n):
                    A.e.activation(dst(gi, b), PS[:, b, :], ACT.Copy).then_inc(sem(name, "ev"), 1)
                return evac
            return make

        def residual(name, hi=hhi, lo=hlo):
            product(name, hi, lo, True, None, dve=lambda V: add_residual(V, name))

        add(pe=setup_pe, act=setup_act, dve=setup_dve, pool=setup_pool)
        norm("n0", gcol("mix_norm", 0))
        product("zf", hhi, hlo, False, SEQ, act=zf_act, dve=zf_dve, freed=zf_freed, limit=fence)

        def vg_act(A):
            def evac(gi, b, n):
                A.e.activation(VG[:, b, :], PS[:, b, :], ACT.Gelu_apprx_tanh).then_inc(sem("zv", "ev"), 1)
            return evac
        product("zv", hhi, hlo, True, None, act=vg_act, limit=fence)
        add(pe=sgu_pe, act=sgu_act, dve=sgu_dve, pool=sgu_pool)
        add(pe=rw0_pe, act=rw0_act, dve=rw0_dve)
        for d in range(2):
            for j in range(NJ):
                add(pe=lambda T, d=d, j=j: pair_pe(T, d, j), act=lambda A, d=d, j=j: pair_act(A, d, j),
                    dve=lambda V, d=d, j=j: pair_dve(V, d, j))
            add(pe=lambda T, d=d: chain_pe(T, d), dve=lambda V, d=d: chain_dve(V, d))
        add(pe=fin_pe, act=fin_act, dve=fin_dve)
        marks["weights_again"] = len(st)
        residual("ab")

        def tail(l):
            mhi, mlo = (lambda k: MNT[k][:, :]), (lambda k: MNL[k][:, :])

            norm_shares(f"m{l}", MT)

            def mem_pool(G):
                G.e.dma_start(MRAW[:, :, :], a["mem"][0].rearrange("(t p) d -> p t d", p=P)).then_inc(S("mem_in"), 16)
                norm_pool(G, f"m{l}", MT)

            def mem_act(A):
                A.e.wait_ge(S("mem_in"), 16 * (l + 1))
                norm_act(A, f"m{l}", MRAW, SQX, MT, gcol("mem_norm"), mhi)
            add(pe=lambda T: norm_pe(T, f"m{l}", MXN, MT), act=mem_act,
                dve=lambda V: norm_dve(V, f"m{l}", MRAW, MXN, MT, gcol("mem_norm"), mhi, mlo), pool=mem_pool)
            product(f"kv{l}", mhi, mlo, True, None,
                    act=copy_out(f"kv{l}", lambda gi, b: (KTOK if gi < 2 else VMEM)[:, b, (gi % 2) * 512:(gi % 2) * 512 + 512]))
            kg = lambda k: col("cross_k_gain", 2 * l + k % 2)
            qg = lambda k: col("cross_q_gain", 2 * l + k % 2)
            turn_shares(f"xk{l}", MT)
            add(pe=lambda T: turn_pe(T, f"xk{l}", KTOK, MT), act=lambda A: turn_act(A, f"xk{l}", KFT, MT, kg),
                dve=lambda V: group_norm_dve(V, f"xk{l}", KTOK, SQX, MT, XD), pool=lambda G: group_norm_pool(G, f"xk{l}", MT, XD))
            norm(f"nx{l}", gcol("cross_norm", l))
            product(f"xq{l}", hhi, hlo, True, None,
                    act=copy_out(f"xq{l}", lambda gi, b: QTOK[:, b, gi * 512:gi * 512 + 512]))
            turn_shares(f"xqn{l}", NT)
            shares(f"xa{l}", "xa", xe=XH * NT, xl=NT, xpc=2 * NT, xolo=DC, xpv=DC, xn=NT, xtp=2 * NT, xmx=NT, xohi=DC)
            add(pe=lambda T: turn_pe(T, f"xqn{l}", QTOK, NT), act=lambda A: turn_act(A, f"xqn{l}", QFT, NT, qg),
                dve=lambda V: group_norm_dve(V, f"xqn{l}", QTOK, SQX, NT, XD), pool=lambda G: group_norm_pool(G, f"xqn{l}", NT, XD))
            add(pe=lambda T: xattn_pe(T, l), act=lambda A: xattn_act(A, l), dve=lambda V: xattn_dve(V, l))
            residual(f"xo{l}")
            norm(f"nf{l}", gcol("ffn_norm", l))
            for h in range(2):
                n = len(gemms[f"up{l}{h}"])
                shares(f"up{l}{h}", "up", main=4 * n, silu=2 * n, g=2 * n, hi=2 * n, lo=2 * n)
                product(f"up{l}{h}", hhi, hlo, False, SEQ, act=lambda A, h=h: up_act(A, l, h), dve=lambda V, h=h: up_dve(V, l, h))
                residual(f"dn{l}{h}", lambda k: GHI[k][:, :], lambda k: GLO[k][:, :])

        tail(0)
        norm("n1", gcol("mix_norm", 1))
        for nm, dst, gain in (("dq", QF, "diff_q_gain"), ("dk", KF, "diff_k_gain")):
            product(nm, hhi, hlo, True, None, act=copy_out(nm, lambda gi, b: TOK[:, b, gi * 512:gi * 512 + 512]))
            turn_shares(nm, NT)
            add(pe=lambda T, nm=nm: turn_pe(T, nm, TOK, NT), act=lambda A, nm=nm, dst=dst, gain=gain: turn_act(A, nm, dst, NT, lambda k: col(gain)),
                dve=lambda V, nm=nm: group_norm_dve(V, nm, TOK, SQD, NT, DHD), pool=lambda G, nm=nm: group_norm_pool(G, nm, NT, DHD))
        product("dv", hhi, hlo, True, None, act=copy_out("dv", lambda gi, b: VV[:, b, gi * 512:gi * 512 + 512]))
        add(pe=dattn_pe, act=dattn_act, dve=dattn_dve)
        turn_shares("do", NT)
        add(pe=lambda T: turn_pe(T, "do", OTK, NT), act=dout_act,
            dve=lambda V: (group_norm_dve(V, "do", OTK, SQD, NT, P), dout_dve(V)), pool=lambda G: group_norm_pool(G, "do", NT, P))
        residual("do")
        tail(1)
        return st

    marks = {}
    stages = stage_list()
    for e in ("pe", "act", "dve", "pool"):
        S(f"{e}_stage")

    def run(E, key):
        for st in stages:
            if st.get(key):
                st[key](E)
            E.meet()

    block = nc.Block()
    with block:
        @block.tensor
        def _(e):
            run(Engine("pe", e), "pe")

        @block.scalar
        def _(e):
            run(Engine("act", e), "act")

        @block.vector
        def _(e):
            e.memset(VROW[0][:, :], 0.0).then_inc(S("v_zero"), 1)
            for i in range(1, 5):
                e.memset(VROW[i][:, :], 0.0).then_inc(S("v_zero"), 1)
            run(Engine("dve", e), "dve")

        @block.gpsimd
        def _(e):
            run(Engine("pool", e), "pool")

        @block.sync
        def _(e):
            e.wait_ge(S("v_zero"), 5)
            loads(e)
            for i, (w, k, nk, pieces) in enumerate(plan):
                if i == fence:
                    for o in ("pe", "act", "dve", "pool"):
                        e.wait_ge(S(f"{o}_stage"), marks["weights_again"])
                if i >= 2:
                    e.wait_ge(S("w_lo"), i - 1)
                off = 0
                for c0, n in pieces:
                    e.dma_start(WRAW[i % 2][:, 0:nk, off:off + n],
                                w[k * P:(k + nk) * P, c0:c0 + n].rearrange("(k p) n -> p k n", p=P))\
                        .then_inc(S(f"raw_in{i % 2}"), 16)
                    off += n
            for o in ("pe", "act", "dve", "pool"):
                e.wait_ge(S(f"{o}_stage"), len(stages))
            for t in range(NT):
                e.dma_start(out[0, t * P:t * P + P, :], X[:, t, :]).then_inc(S("stored"), 16)
            e.wait_ge(S("stored"), 16 * NT)


def host_constants():
    import numpy as np
    i = np.arange(P)
    p, f = i[:, None], i[None, :]
    same = lambda b: p // b == f // b
    c = {"LT": (p > f) & same(CH), "UT": (p < f) & same(CH), "UTI": (p <= f) & same(CH), "LTI": (p >= f) & same(CH),
         "T1f": (p >= f) & same(2), "T1b": (p <= f) & same(2)}
    for lv in range(2, 7):
        level = same(1 << lv) & ~same(1 << (lv - 1))
        c[f"Xf{lv}"] = (level & (p < f)) | (p == f)
        c[f"Xb{lv}"] = (level & (p > f)) | (p == f)
    c["bones"] = same(HD)
    c["reset"] = np.broadcast_to((np.arange(SEQ) % CH != 0)[None, :], (P, SEQ))
    c["ident2"] = (p % HD) == np.arange(HD)[None, :]
    rkc = np.zeros((P, RK_W), np.float32)
    for n, (o, w) in RK.items():
        rkc[:, o:o + w] = c[n]
    keep = np.zeros((P, KEEP_W), np.float32)
    keep[:, 0:P] = p == f
    keep[:, P:] = np.abs(p + 384 - np.arange(896)[None, :])
    return {"keep": keep, "rkc": rkc}


_INS = ['x', 'mem', 'mem_norm', 'mix_norm', 'cross_norm', 'ffn_norm', 'ab_w_in', 'ab_shift_prev', 'ab_shift_next',
        'rwkv_w0', 'rwkv_w2', 'rwkv_a0', 'rwkv_a2', 'rwkv_g2', 'rwkv_k_k', 'rwkv_k_a', 'rwkv_r_k', 'rwkv_out_gain',
        'sgu_v_gain', 'sgu_w_s', 'sgu_b', 'ab_w_out', 'diff_w_in', 'diff_q_gain', 'diff_k_gain', 'diff_lambda_q1',
        'diff_lambda_k1', 'diff_lambda_q2', 'diff_lambda_k2', 'diff_out_gain', 'diff_w_out', 'cross_wq', 'cross_wkv',
        'cross_q_gain', 'cross_k_gain', 'cross_wo', 'ffn_w_up', 'ffn_conv_w', 'ffn_conv_b', 'ffn_w_down']


def kernel(**inputs):
    import numpy as np
    import concourse.bacc as bacc
    from concourse.bass_utils import run_bass_kernel_spmd

    nc = bacc.Bacc("TRN2", target_bir_lowering=False, num_devices=1)
    arrays = {n: np.ascontiguousarray(inputs[n]) for n in _INS}
    arrays.update(host_constants())
    aps = {n: nc.dram_tensor(n, v.shape, mybir.dt.from_np(v.dtype), kind="ExternalInput").ap() for n, v in arrays.items()}
    out = nc.dram_tensor("out", (1, SEQ, D), F32, kind="ExternalOutput").ap()
    build(nc, aps, out)
    r = run_bass_kernel_spmd(nc, [arrays], core_ids=[0])
    return r.results[0]["out"]
```

```python
import math

import concourse.bass as bass
from concourse import mybir

F32 = mybir.dt.float32
F32R = mybir.dt.float32r
ALU = mybir.AluOpType
ACT = mybir.ActivationFunctionType
AX = mybir.AxisListType

P = 128
D = 1024
DC = D // P
SEQ = 512
NT = SEQ // P
MEM = 256
MT = MEM // P
EPS = 1e-6
BANK = 512
HD = 64
RW = 512
NJ = RW // P
CH = 64
NCH = SEQ // CH
RWKV_IN = 1920
SGU_G = 4
DH = 8
DHD = 64
XH = 4
XD = 256
FF = 2816
FC = FF // P
LAMBDA_INIT = 0.8 - 0.6 * math.exp(-0.3)
DECAY = math.exp(-0.5)

VEC_TILES = [
    [("mix_norm", 16), ("cross_norm", 16), ("ffn_norm", 16), ("mem_norm", 8), ("ab_shift_prev", 15),
     ("ab_shift_next", 15), ("rwkv_w0", 8), ("rwkv_a0", 8), ("rwkv_k_k", 4), ("rwkv_k_a", 4),
     ("rwkv_r_k", 4), ("rwkv_out_gain", 4), ("sgu_v_gain", 4), ("diff_out_gain", 1),
     ("diff_q_gain", 1), ("diff_k_gain", 1)],
    [("ffn_conv_b", 88), ("cross_q_gain", 4), ("cross_k_gain", 4)],
    [("ffn_conv_w", 88)], [("ffn_conv_w", 88)], [("ffn_conv_w", 88)],
]
COL = {}
for _i, _tile in enumerate(VEC_TILES):
    _r = 0
    for _name, _n in _tile:
        COL.setdefault(_name, _i * P + _r)
        _r += _n

DIST_W = SEQ + 384
MASKS = ["LT", "UT", "UTI", "LTI", "T1f", "T1b"] + [f"X{d}{j}" for d in "fb" for j in range(2, 7)]
RK = {m: (i * P, P) for i, m in enumerate(MASKS)}
RK["bones"] = (len(MASKS) * P, P)
RK["reset"] = (len(MASKS) * P + P, SEQ)
RK["ident2"] = (len(MASKS) * P + P + SEQ, HD)
RK_W = len(MASKS) * P + P + SEQ + HD


class Tally:

    def __init__(self, sem):
        self.sem, self.n = sem, 0

    def sig(self, instruction, by=1):
        instruction.then_inc(self.sem, by)
        self.n += by
        return self.n


def build(nc, a, out):
    sems = {}

    def S(name):
        if name not in sems:
            sems[name] = nc.alloc_semaphore(name)
        return sems[name]

    left, base = {}, {}

    def shares(tag, kind, **totals):
        for x, n in totals.items():
            base[tag, x] = (S(f"{kind}_{x}"), left.get((kind, x), 0))
            left[kind, x] = left.get((kind, x), 0) + n

    def sem(tag, x):
        return base[tag, x][0]

    def at(tag, x, n):
        s, b = base[tag, x]
        return s, b + n

    low = (nc.sbuf_base + 31) // 32 * 32

    def sb(name, shape, at, dt=F32):
        return nc.alloc_sbuf_tensor_at(name, shape, dt, offset=low + at)

    X = sb("X", [P, NT, D], 0)
    WRAW = [sb(f"WRAW{i}", [P, 4, 512], 16384 + 8192 * i) for i in range(2)]
    WHI = [sb(f"WHI{i}", [P, 4, 512], 32768 + 16384 * i, F32R) for i in range(3)]
    WLO = [sb(f"WLO{i}", [P, 4, 512], 32768 + 16384 * i + 8192, F32R) for i in range(3)]
    HHI = [sb(f"HHI{k}", [P, SEQ], 81920 + 2048 * k, F32R) for k in range(DC)]
    HLO = [sb(f"HLO{k}", [P, SEQ], 98304 + 2048 * k, F32R) for k in range(DC)]
    COLS = sb("COLS", [P, 5 * P], 114688)
    KC = sb("KC", [P, P], 117248)
    SM = sb("SM", [P, 256], 117760)
    DIST = sb("DIST", [P, DIST_W], 118784)
    LAM = sb("LAM", [P, 256], 122368)
    R0 = 123392
    ident = KC[:, 0:P]

    VROW = [sb(f"VROW{i}", [P, P], R0 + 40000 + 512 * i) for i in range(5)]
    RC = sb("RC", [P, RK_W], R0)
    r1 = R0 + 4 * RK_W
    WL2 = sb("WL2", [P, 3, 512], r1)
    SGUB = sb("SGUB", [P, 4, P], r1 + 6144)
    WS = sb("WS", [P, 4, P], r1 + 8192)
    r2 = r1 + 10240
    ZS = [sb(f"ZS{c}", [P, SEQ], r2 + 2048 * c) for c in range(15)]
    KK = sb("KK", [P, NJ, SEQ], r2 + 30720)
    r3 = r2 + 38912
    names7 = ["GBR", "GKA", "GKR", "AI", "TT", "UU", "XX"]
    U7 = {n: sb(n, [P, 8, P], r3 + 4096 * i) for i, n in enumerate(names7)}
    GBR, GKA, GKR, AI, TT, UU, XX = (U7[n] for n in names7)
    UG = sb("UG", [P, 4, SEQ], r3)
    VG = sb("VG", [P, NT, 512], r3 + 8192)
    WST = sb("WST", [P, 4, P], r3 + 16384)
    SQ1 = sb("SQ1", [P, 1024], r3 + 18432)
    BT = [sb(f"BT{i}", [P, SEQ], r3 + 22528 + 2048 * i) for i in range(2)]
    w0 = 16384
    PT = sb("PT", [P, NJ, NCH, HD], w0)
    QT = sb("QT", [P, NJ, NCH, HD], w0 + 8192)
    RT = sb("RT", [P, NJ, SEQ], w0 + 16384)
    ALP = sb("ALP", [P, 2, SEQ], w0 + 24576)
    RHO = [sb("RHO0", [P, 2, SEQ], w0 + 28672), sb("RHO1", [P, 2, SEQ], 118784)]
    BET = sb("BET", [P, SEQ], w0 + 32768)
    KAP = sb("KAP", [P, SEQ], w0 + 34816)
    AXT = sb("AXT", [P, 8, P], w0 + 36864)
    BPD = sb("BPD", [P, NT, 2, P], w0 + 40960)
    KPD = sb("KPD", [P, NT, 2, P], w0 + 45056)
    WU = sb("WU", [P, 8, P], w0 + 49152)
    TMP = [sb(f"TMP{i}", [P, SEQ], w0 + 53248 + 2048 * i) for i in range(4)]
    BON = [sb(f"BON{j}", [P, SEQ], w0 + 61440 + 2048 * j if j < 2 else r1 + 6144 + 2048 * (j - 2))
           for j in range(NJ)]
    YL = sb("YL", [P, NJ, SEQ], 81920)
    VTK = sb("VTK", [P, NT, RW], 98304)
    YQ = [sb(f"YQ{i}", [P, SEQ], r3 + 2048 * i) for i in range(5)]
    XN = sb("XN", [P, NT, D], R0 + 49152 + 8192)
    SQ = sb("SQ", [P, D], R0 + 49152 + 8192 + 16384)
    MNT = [sb(f"MHI{k}", [P, MEM], R0 + 1024 * k, F32R) for k in range(DC)]
    MNL = [sb(f"MLO{k}", [P, MEM], R0 + 8192 + 1024 * k, F32R) for k in range(DC)]
    MRAW = sb("MRAW", [P, MT, D], R0 + 16384)
    MXN = sb("MXN", [P, MT, D], R0 + 24576)
    KTOK = sb("KTOK", [P, MT, D], R0 + 16384)
    KFT = sb("KFT", [P, DC, MEM], R0 + 32768)
    VMEM = sb("VMEM", [P, MT, D], R0 + 40960)
    SQX = sb("SQX", [P, D], R0 + 49152)
    SQM = sb("SQM", [P, D], R0 + 53248)
    QTOK = sb("QTOK", [P, NT, D], R0 + 57344)
    QFT = sb("QFT", [P, DC, SEQ], R0)
    PTR = sb("PTR", [P, XH, MT, SEQ], R0 + 16384)
    EX = [sb(f"EX{i}", [P, XH, MEM], R0 + 57344 + 4096 * i) for i in range(2)]
    GHI = [sb(f"GHI{k}", [P, SEQ], R0 + 2048 * k, F32R) for k in range(12)]
    GLO = [sb(f"GLO{k}", [P, SEQ], R0 + 24576 + 2048 * k, F32R) for k in range(12)]
    CG = [sb(f"CG{i}", [P, SEQ], R0 + 49152 + 2048 * i) for i in range(2)]
    CV = [sb(f"CV{i}", [P, SEQ], R0 + 53248 + 2048 * i) for i in range(2)]
    SG = [sb(f"SG{i}", [P, SEQ], R0 + 57344 + 2048 * i) for i in range(2)]
    TOKK = sb("TOKK", [P, NT, D], R0)
    TOKQ = sb("TOKQ", [P, NT, D], R0 + 16384)
    KF = sb("KF", [P, DC, SEQ], R0 + 32768)
    QF = sb("QF", [P, DC, 2, SEQ], R0 + 49152)
    VV = sb("VV", [P, NT, D], R0)
    OTK = sb("OTK", [P, NT, D], R0 + 16384)
    SQD = sb("SQD", [P, D], R0 + 81920)
    AT = [sb(f"AT{i}", [P, SEQ], R0 + 81920 + 2048 * i) for i in range(2)]
    SS = [sb(f"SS{i}", [P, 2, SEQ], 81920 + 4096 * i) for i in range(3)]
    ATT = [sb(f"ATT{i}", [P, NT, P], 81920 + 12288 + 2048 * i) for i in range(2)]
    BIAS = [sb(f"BIAS{i}", [P, DIST_W], 98304 + 4096 * i) for i in range(2)]

    PS = nc.alloc_psum_tensor("PS", [P, 8, BANK], F32)

    def col(name, i=0, n=1):
        c = COL[name] + i
        return COLS[:, c:c + n]

    def rk(name, p0=0, p1=P):
        o, w = RK[name]
        return RC[p0:p1, o:o + w]

    def mask4(name):
        return rk(name).unsqueeze(1).to_broadcast([P, 4, P])

    plan, use = [], {}
    used_at = {}
    gemms = {}
    raw_level = []
    slot_total = [0, 0]

    def gemm(name, w, groups, k0, k1, nb):
        g_list, banks = [], 0
        for gi, pieces in enumerate(groups):
            n = nb if isinstance(nb, int) else nb[gi]
            steps = []
            for k in range(k0, k1, 4):
                nk = min(4, k1 - k)
                i = len(plan)
                slot_total[i % 2] += 16 * len(pieces)
                raw_level.append(slot_total[i % 2])
                plan.append((w, k, nk, pieces))
                steps.append((i, k - k0, nk))
                if k + nk < k1:
                    use[name] = use.get(name, 0) + 1
                    used_at[i] = ("wused", use[name])
                else:
                    used_at[i] = ("done", banks + n)
            g_list.append((steps, n, banks))
            banks += n
        gemms[name] = g_list
        shares(name, "g", done=banks, wused=use.get(name, 0), ev=banks)
        for steps, _, _ in g_list:
            for i, _, _ in steps:
                used_at[i] = at(name, *used_at[i])

    halves = [[(0, 512)], [(512, 512)]]
    gemm("zf", a["ab_w_in"][0], [[(512 * g, 512)] for g in range(3)] + [[(1536, 384)], [(1920, 512)]],
         0, DC, [4, 4, 4, 3, 4])
    gemm("zv", a["ab_w_in"][0], [[(2432, 512)]], 0, DC, 4)
    fence = len(plan)
    gemm("ab", a["ab_w_out"][0], halves, 0, DC, NT)

    def plan_tail(l):
        gemm(f"kk{l}", a["cross_wkv"][l], halves, 0, DC, MT)
        gemm(f"xq{l}", a["cross_wq"][l], halves, 0, DC, NT)
        gemm(f"kv{l}", a["cross_wkv"][l], [[(D, 512)], [(D + 512, 512)]], 0, DC, MT)
        gemm(f"xo{l}", a["cross_wo"][l], halves, 0, DC, NT)
        for h, (c0, c1) in enumerate(((0, 12), (12, 22))):
            gemm(f"up{l}{h}", a["ffn_w_up"][l],
                 [[(c * P, 256), (FF + c * P, 256)] for c in range(c0, c1, 2)], 0, DC, 4)
            gemm(f"dn{l}{h}", a["ffn_w_down"][l], halves, c0, c1, NT)

    plan_tail(0)
    gemm("dk", a["diff_w_in"][0], [[(1024, 512)], [(1536, 512)]], 0, DC, NT)
    gemm("dq", a["diff_w_in"][0], halves, 0, DC, NT)
    gemm("dv", a["diff_w_in"][0], [[(2048, 512)], [(2560, 512)]], 0, DC, NT)
    gemm("do", a["diff_w_out"][0], halves, 0, DC, NT)
    plan_tail(1)

    class Engine:

        def __init__(self, name, eng):
            self.name, self.e = name, eng
            self.own = Tally(S(f"{name}_own"))
            self.met = 0
            self.split = 0

        def mine(self, instruction):
            self.own.sig(instruction)

        def wait_mine(self):
            self.e.wait_ge(self.own.sem, self.own.n)

        def meet(self):
            self.e.drain().then_inc(S(f"{self.name}_stage"), 1)
            self.met += 1
            for other in ("pe", "act", "dve", "pool"):
                if other != self.name:
                    self.e.wait_ge(S(f"{other}_stage"), self.met)

    def part(t, i):
        w, k, nk, pieces = plan[i]
        return t[:, 0:nk, 0:sum(n for _, n in pieces)]

    def split_hi(A, upto):
        while A.split < min(upto, len(plan)):
            i = A.split
            A.e.wait_ge(S(f"raw_in{i % 2}"), raw_level[i])
            if i >= 3:
                A.e.wait_ge(*used_at[i - 3])
            A.e.activation(part(WHI[i % 3], i), part(WRAW[i % 2], i), ACT.Copy).then_inc(S("w_hi"), 1)
            A.split += 1

    def split_lo(V, upto):
        while V.split < min(upto, len(plan)):
            i = V.split
            V.e.wait_ge(S("w_hi"), i + 1)
            V.e.tensor_tensor(part(WLO[i % 3], i), part(WRAW[i % 2], i), part(WHI[i % 3], i).bitcast(F32),
                              ALU.subtract).then_inc(S("w_lo"), 1)
            V.split += 1

    def gemm_pe(T, name, hi, lo, tokens_out=True, nt=SEQ, bank0=0):
        e = T.e
        for gi, (steps, nb, banks) in enumerate(gemms[name]):
            for si, (i, kb, nk) in enumerate(steps):
                e.wait_ge(S("w_lo"), i + 1)
                width = sum(n for _, n in plan[i][3])
                for b in range(nb):
                    if si == 0 and banks_before[name, gi] is not None:
                        e.wait_ge(*bank_free(name, gi, b))
                    n = width if tokens_out else nt
                    o = PS[:, bank0 + b, 0:n]
                    for kk in range(nk):
                        k = kb + kk
                        for q, (wt, ht) in enumerate(((WHI, hi), (WHI, lo), (WLO, hi))):
                            w = wt[i % 3]
                            if tokens_out:
                                l, r = ht(k)[:, b * P:b * P + P], w[:, kk, 0:width]
                            else:
                                l, r = w[:, kk, b * P:b * P + P], ht(k)[:, 0:nt]
                            mm = e.matmul(o, l, r, start=(si == 0 and kk == 0 and q == 0),
                                          stop=(si == len(steps) - 1 and kk == nk - 1 and q == 2))
                    if si == len(steps) - 1:
                        mm.then_inc(sem(name, "done"), 1)
                if si < len(steps) - 1:
                    mm.then_inc(sem(name, "wused"), 1)

    def gemm_side(E, name, split, evac, limit=None):
        for gi, (steps, nb, banks) in enumerate(gemms[name]):
            for i, _, _ in steps:
                split(E, i + 3 if limit is None else min(i + 3, limit))
            if evac is not None:
                for b in range(nb):
                    E.e.wait_ge(*at(name, "done", banks + b + 1))
                    evac(gi, b, banks + b)

    banks_before, before = {}, None
    for _name, _groups in gemms.items():
        for _gi, (_, _nb, _banks) in enumerate(_groups):
            banks_before[_name, _gi] = before
            before = (_name, _nb, _banks)

    def bank_free(name, gi, b):
        other, nb, banks = banks_before[name, gi]
        return at(other, "ev", banks + min(b, nb - 1) + 1)

    hhi, hlo = (lambda k: HHI[k][:, :]), (lambda k: HLO[k][:, :])

    def norm_act_front(A, tag, src, sq, nt):
        e = A.e
        for t in range(nt):
            e.activation(sq[:, :], src[:, t, :], ACT.Square, accum_out=SM[:, t:t + 1]).then_inc(sem(tag, "sq"), 1)
            e.wait_ge(*at(tag, "sq", t + 1))

    def norm_act_back(A, tag, nt, gain, hi, b0=0):
        e = A.e
        for k in range(DC):
            e.wait_ge(*at(tag, "tp", k + 1))
            e.activation(hi(k)[:, 0:nt * P], PS[:, b0 + k % 4, 0:nt * P], ACT.Copy,
                         scale=gain(k)).then_inc(sem(tag, "hi"), 1)

    def norm_pool(G, tag, nt):
        G.e.wait_ge(*at(tag, "var", 1))
        G.e.tensor_tensor(SM[:, 8:8 + nt], SM[:, 4:4 + nt], SM[:, 16:16 + nt], ALU.pow).then_inc(sem(tag, "rstd"), 1)

    def norm_dve_front(V, tag, src, xn, nt):
        e = V.e
        e.wait_ge(*at(tag, "sq", nt))
        e.tensor_scalar(SM[:, 4:4 + nt], SM[:, 0:nt], 1.0 / D, EPS, ALU.mult, ALU.add).then_inc(sem(tag, "var"), 1)
        e.wait_ge(*at(tag, "rstd", 1))
        for t in range(nt):
            e.tensor_scalar(xn[:, t, :], src[:, t, :], SM[:, 8 + t:9 + t], None, ALU.mult).then_inc(sem(tag, "xn"), 1)

    def norm_dve_back(V, tag, nt, gain, hi, lo, b0=0):
        e = V.e
        for k in range(DC):
            e.wait_ge(*at(tag, "hi", k + 1))
            e.scalar_tensor_tensor(lo(k)[:, 0:nt * P], PS[:, b0 + k % 4, 0:nt * P], gain(k),
                                   hi(k)[:, 0:nt * P].bitcast(F32), ALU.mult, ALU.subtract).then_inc(sem(tag, "lo"), 1)

    def norm_pe(T, tag, xn, nt, b0=0):
        e = T.e
        for k in range(DC):
            if k >= 4:
                e.wait_ge(*at(tag, "lo", k - 3))
            for t in range(nt):
                if k == 0:
                    e.wait_ge(*at(tag, "xn", t + 1))
                mm = e.transpose(PS[:, b0 + k % 4, t * P:t * P + P], xn[:, t, k * P:k * P + P], ident)
            mm.then_inc(sem(tag, "tp"), 1)

    def add_residual(V, name):
        def evac(gi, b, n):
            o = X[:, b, gi * 512:gi * 512 + 512]
            V.e.tensor_tensor(o, o, PS[:, b, :], ALU.add).then_inc(sem(name, "ev"), 1)
        return evac

    def group_norm_dve(V, tag, tok, sq, nt, w, ready=None):
        e, n = V.e, D // w
        if ready is not None:
            e.wait_ge(*at(ready, "ev", gemms[ready][-1][2] + gemms[ready][-1][1]))
        for t in range(nt):
            V.mine(e.tensor_tensor(sq[:, :], tok[:, t, :], tok[:, t, :], ALU.mult))
            V.wait_mine()
            V.mine(e.tensor_reduce(SM[:, 32 + t * n:32 + t * n + n], sq[:, :].rearrange("p (g w) -> p g w", w=w),
                                   AX.X, ALU.add))
            V.wait_mine()
        e.tensor_scalar(SM[:, 96:96 + nt * n], SM[:, 32:32 + nt * n], 1.0 / w, EPS, ALU.mult, ALU.add)\
            .then_inc(sem(tag, "gvar"), 1)
        e.wait_ge(*at(tag, "grstd", 1))
        for t in range(nt):
            v = tok[:, t, :].rearrange("p (g w) -> p g w", w=w)
            e.tensor_tensor(v, v, SM[:, 160 + t * n:160 + t * n + n].unsqueeze(2).to_broadcast([P, n, w]),
                            ALU.mult).then_inc(sem(tag, "gn"), 1)

    def group_norm_pool(G, tag, nt, w):
        n = D // w * nt
        G.e.wait_ge(*at(tag, "gvar", 1))
        G.e.tensor_tensor(SM[:, 160:160 + n], SM[:, 96:96 + n], SM[:, 16:17].to_broadcast([P, n]), ALU.pow)\
            .then_inc(sem(tag, "grstd"), 1)

    def turn_pe(T, tag, tok, nt, bank0=4):
        e = T.e
        for k in range(DC):
            if k >= 4:
                e.wait_ge(*at(tag, "tev", k - 3))
            for t in range(nt):
                if k == 0:
                    e.wait_ge(*at(tag, "gn", t + 1))
                mm = e.transpose(PS[:, bank0 + k % 4, t * P:t * P + P], tok[:, t, k * P:k * P + P], ident)
            mm.then_inc(sem(tag, "ttp"), 1)

    def turn_split_act(A):
        for k in range(DC):
            A.e.wait_ge(*at("dq", "ttp", k + 1))
            for c in range(2):
                r = slice(DHD * c, DHD * c + DHD)
                i = A.e.activation(QF[r, k, c, :], PS[r, 4 + k % 4, :], ACT.Copy, scale=COLS[r, COL["diff_q_gain"]:COL["diff_q_gain"] + 1])
            i.then_inc(sem("dq", "tev"), 1)

    def turn_act(A, tag, dst, nt, gain, b0=4):
        for k in range(DC):
            A.e.wait_ge(*at(tag, "ttp", k + 1))
            A.e.activation(dst(k), PS[:, b0 + k % 4, 0:nt * P], ACT.Copy, scale=gain(k))\
                .then_inc(sem(tag, "tev"), 1)

    def half(hh):
        return slice(HD * hh, HD * hh + HD)

    def zf_act(A):
        def evac(gi, b, n):
            c = gi * 4 + b
            if gi < 4:
                A.e.activation(ZS[c][:, :], PS[:, b, :], ACT.Copy, scale=SM[:, 200 + c:201 + c])\
                    .then_inc(S("zf_main"), 1)
            else:
                A.e.activation(UG[:, b, :], PS[:, b, :], ACT.Gelu_apprx_tanh).then_inc(sem("zf", "ev"), 1)
        return evac

    def zf_dve(V):
        def evac(gi, b, n):
            c = gi * 4 + b
            if gi == 4:
                return
            V.e.wait_ge(S("zf_main"), n + 1)
            V.mine(V.e.scalar_tensor_tensor(ZS[c][:, 1:SEQ], PS[:, b, 0:SEQ - 1], col("ab_shift_prev", c),
                                            ZS[c][:, 1:SEQ], ALU.mult, ALU.add))
            V.wait_mine()
            V.e.scalar_tensor_tensor(ZS[c][:, 0:SEQ - 1], PS[:, b, 1:SEQ], col("ab_shift_next", c),
                                     ZS[c][:, 0:SEQ - 1], ALU.mult, ALU.add).then_inc(sem("zf", "ev"), 1)
        return evac

    def mix0_act(A):
        e = A.e
        for t in range(NT):
            e.activation(SQ1[:, 0:512], VG[:, t, :], ACT.Square, accum_out=SM[:, t:t + 1]).then_inc(S("sgu_sq"), 1)
            e.wait_ge(S("sgu_sq"), t + 1)
        e.wait_ge(S("wst_tp"), 1)
        e.activation(WST[:, :, :], PS[:, 3, :].rearrange("p (g q) -> p g q", g=4), ACT.Copy).then_inc(S("wst"), 1)
        for t in range(NT):
            e.wait_ge(S("rw0_vtp"), t + 1)
            e.activation(VTK[:, t, :], PS[:, 4 + t, :], ACT.Copy).then_inc(S("rw0_vtk"), 1)
        for j in range(NJ):
            e.wait_ge(S("rw0_ss"), j + 1)
            e.activation(TMP[j][:, :], PS[:, j, :], ACT.Sqrt, bias=SM[:, 24:25]).then_inc(S("rw0_norm"), 1)
        e.activation(ZS[ZW][:, :], ZS[ZW][:, :], ACT.Tanh).then_inc(S("rw0_tanh"), 1)
        e.activation(ZS[ZG][:, :], ZS[ZG][:, :], ACT.Tanh, scale=0.5).then_inc(S("rw0_tanh"), 1)
        for g in range(SGU_G):
            e.wait_ge(S("sgu_b"), g + 1)
            e.activation(HHI[4 + g][:, :], BT[g % 2][:, :], ACT.Copy).then_inc(S("sgu_hi"), 1)

    def sgu_pool(G):
        G.e.wait_ge(S("sgu_var"), 1)
        G.e.tensor_tensor(SM[:, 8:12], SM[:, 4:8], SM[:, 16:20], ALU.pow).then_inc(S("sgu_rstd"), 1)

    def mix0_dve(V):
        e = V.e
        for j in range(NJ):
            V.mine(e.tensor_scalar(KK[:, j, :], ZS[ZK + j][:, :], col("rwkv_k_k", j), None, ALU.mult))
            V.wait_mine()
            e.tensor_tensor(TMP[j][:, :], KK[:, j, :], KK[:, j, :], ALU.mult).then_inc(S("rw0_sq"), 1)
        e.wait_ge(S("sgu_sq"), NT)
        e.tensor_scalar(SM[:, 4:8], SM[:, 0:4], 1.0 / 512, EPS, ALU.mult, ALU.add).then_inc(S("sgu_var"), 1)
        e.memset(BPD[:, :, :, :], 0.0)
        e.wait_ge(S("sgu_rstd"), 1)
        for t in range(NT):
            e.tensor_scalar(VG[:, t, :], VG[:, t, :], SM[:, 8 + t:9 + t], None, ALU.mult).then_inc(S("sgu_vg"), 1)
        for z in (KPD[:, :, :, :], ALP[:, :, :], RHO[0][:, :, :], RHO[1][:, :, :]):
            e.memset(z, 0.0)
        for j in range(NJ):
            e.wait_ge(S("rw0_norm"), j + 1)
            V.mine(e.reciprocal(TMP[j][:, :], TMP[j][:, :]))
            V.wait_mine()
            e.tensor_tensor(KK[:, j, :], KK[:, j, :], TMP[j][:, :], ALU.mult)
        e.wait_ge(S("rw0_tanh"), 2)
        e.tensor_scalar(ZS[ZG][:, :], ZS[ZG][:, :], 0.5, 0.5, ALU.mult, ALU.add)
        for g in range(SGU_G):
            e.wait_ge(S("sgu_mm"), g + 1)
            if g >= 2:
                e.wait_ge(S("sgu_lo"), g - 1)
            b = BT[g % 2]
            V.mine(e.scalar_tensor_tensor(b[:, :].rearrange("p (n q) -> p n q", n=NT),
                                          PS[:, 4 + g, :].rearrange("p (n q) -> p n q", n=NT), col("sgu_v_gain", g),
                                          SGUB[:, g, :].unsqueeze(1).to_broadcast([P, NT, P]), ALU.mult, ALU.add))
            V.wait_mine()
            e.tensor_tensor(b[:, :], b[:, :], UG[:, g, :], ALU.mult).then_inc(S("sgu_b"), 1)
            e.wait_ge(S("sgu_hi"), g + 1)
            e.tensor_tensor(HLO[4 + g][:, :], b[:, :], HHI[4 + g][:, :].bitcast(F32), ALU.subtract)\
                .then_inc(S("sgu_lo"), 1)

    def mix0_pe(T):
        e = T.e
        for g in range(SGU_G):
            mm = e.transpose(PS[:, 3, g * P:g * P + P], WS[:, g, :], ident)
        mm.then_inc(S("wst_tp"), 1)
        for t in range(NT):
            for j in range(NJ):
                mm = e.transpose(PS[:, 4 + t, j * P:j * P + P], ZS[ZV + j][:, t * P:t * P + P], ident)
            mm.then_inc(S("rw0_vtp"), 1)
        for j in range(NJ):
            if j == 3:
                e.wait_ge(S("wst"), 1)
            e.wait_ge(S("rw0_sq"), j + 1)
            e.matmul(PS[:, j, :], rk("bones"), TMP[j][:, :], start=True, stop=True).then_inc(S("rw0_ss"), 1)
        e.wait_ge(S("sgu_vg"), NT)
        for g in range(SGU_G):
            e.wait_ge(S("rw0_vtk"), g + 1)
            for n in range(NT):
                mm = e.matmul(PS[:, 4 + g, n * P:n * P + P], VG[:, n, g * P:g * P + P], WST[:, g, :], start=True, stop=True)
            mm.then_inc(S("sgu_mm"), 1)

    ZR, ZK, ZV, ZW, ZA, ZG = 0, 4, 8, 12, 13, 14

    NPAIR = 2 * NJ
    LV = 5

    def quad(bank, k=P):
        return PS[:, bank, :].rearrange("p (u k) -> p u k", k=k)

    def uslot(u):
        return slice((u % 4) * P, (u % 4) * P + P)

    def lora_pe(e, n, which, bank):
        d, j = divmod(n, NJ)
        e.matmul(PS[:, bank, :], WL2[half(d), which, j * P:j * P + P], ZS[ZW + which][half(d), :], start=True, stop=True)\
            .then_inc(S("p_lora"), 1)

    def pair_pe(T, n):
        e = T.e
        j = n % NJ
        rho = RHO[n % 2]
        e.wait_ge(S("p_fm"), n + 1)
        for g in range(2):
            for u in range(4 * g, 4 * g + 4):
                t, hh = divmod(u, 2)
                mm = e.matmul(PS[:, 6 + g, uslot(u)], ALP[:, hh, t * P:t * P + P], BET[:, t * P:t * P + P],
                              start=True, stop=True)
            mm.then_inc(S("p_a"), 1)
        for q, (l, r) in enumerate(((KAP, ALP), (BET, rho), (KAP, rho))):
            for g in range(2):
                bank = (2, 3, 4, 5, 0, 1)[2 * q + g]
                if n > 0 and bank in (4, 5, 0, 1):
                    e.wait_ge(S({4: "p_rfree", 5: "p_yfree", 0: "p_pfree", 1: "p_qfree"}[bank]), n)
                for t in (2 * g, 2 * g + 1):
                    mm = e.matmul(PS[:, bank, (t % 2) * 256:(t % 2) * 256 + 256].rearrange("p (h q) -> p h q", h=2),
                                  l[:, t * P:t * P + P], r[:, 0:2, t * P:t * P + P], start=True, stop=True)
                mm.then_inc(S("p_g"), 1)
        for g in range(2):
            e.wait_ge(S("p_t1"), 2 * n + g + 1)
            for u in range(4 * g, 4 * g + 4):
                mm = e.transpose(PS[:, 6 + g, uslot(u)], TT[:, u, :], ident)
            mm.then_inc(S("p_u1"), 1)
        for lv in range(LV):
            for g in range(2):
                e.wait_ge(S("p_u"), (n * (LV + 1) + lv) * 2 + g + 1)
                if lv == 0:
                    e.wait_ge(S("p_gfree"), 6 * n + g + 1)
                for u in range(4 * g, 4 * g + 4):
                    mm = e.matmul(PS[:, 2 + g, uslot(u)], AI[:, u, :], UU[:, u, :], start=True, stop=True)
                mm.then_inc(S("p_x"), 1)
            if lv > 0:
                for g in range(2):
                    if lv == 1:
                        e.wait_ge(S("p_gfree"), 6 * n + 3 + g)
                    for u in range(4 * g, 4 * g + 4):
                        mm = e.transpose(PS[:, 4 + g, uslot(u)], UU[:, u, :], ident)
                    mm.then_inc(S("p_ttp"), 1)
            for g in range(2):
                e.wait_ge(S("p_xm"), (n * LV + lv) * 2 + g + 1)
                if lv > 0:
                    e.wait_ge(S("p_t"), (n * (LV - 1) + lv - 1) * 2 + g + 1)
                else:
                    e.wait_ge(S("p_gfree"), 6 * n + 5 + g)
                for u in range(4 * g, 4 * g + 4):
                    mm = e.matmul(PS[:, g, uslot(u)], TT[:, u, :], XX[:, u, :], start=True, stop=True)
                mm.then_inc(S("p_un"), 1)
            if lv == 0:
                for hh in range(2):
                    e.wait_ge(S("p_u"), n * (LV + 1) * 2 + hh + 1)
                    for t in range(NT):
                        mm = e.transpose(PS[:, 6 + hh, t * HD:t * HD + HD], ALP[half(hh), hh, t * P:t * P + P],
                                         KC[half(hh), HD * hh:HD * hh + HD])
                mm.then_inc(S("p_tok"), 1)
            if lv == 1:
                e.wait_ge(S("p_tokfree"), 3 * n + 1)
                e.matmul(PS[:, 6, :], rk("bones"), TMP[0][:, :], start=True, stop=True).then_inc(S("p_bonmm"), 1)
                if n + 1 < NPAIR:
                    lora_pe(e, n + 1, 0, 7)
            if lv == 2:
                e.wait_ge(S("p_bonfree"), n + 1)
                if n + 1 < NPAIR:
                    lora_pe(e, n + 1, 1, 6)
                    e.wait_ge(S("p_lorafree"), 2 * n + 3)
                for t in range(NT):
                    mm = e.transpose(PS[:, 7, t * P:t * P + P], BET[:, t * P:t * P + P], ident)
                mm.then_inc(S("p_tok"), 1)
            if lv == 3:
                if n + 1 < NPAIR:
                    e.wait_ge(S("p_lorafree"), 2 * n + 4)
                for t in range(NT):
                    mm = e.transpose(PS[:, 6, t * P:t * P + P], KAP[:, t * P:t * P + P], ident)
                mm.then_inc(S("p_tok"), 1)
        e.wait_ge(S("p_tokfree"), 3 * n + 3)
        for g in range(2):
            for u in range(4 * g, 4 * g + 4):
                mm = e.matmul(PS[:, 6 + g, uslot(u)], GKA[:, u, :], VTK[:, u // 2, j * P:j * P + P], start=True, stop=True)
            mm.then_inc(S("p_x0"), 1)
        for g in range(2):
            e.wait_ge(S("p_u"), (n * (LV + 1) + LV) * 2 + g + 1)
            e.wait_ge(S("p_ax"), 2 * n + g + 1)
            for u in range(4 * g, 4 * g + 4):
                mm = e.matmul(PS[:, 2 + g, uslot(u)], UU[:, u, :], AXT[:, u, :], start=True, stop=True)
            mm.then_inc(S("p_wu"), 1)
        e.wait_ge(S("p_wuc"), 2 * (n + 1))
        for u in range(8):
            t, hh = divmod(u, 2)
            mm = e.matmul(PS[half(hh), 4, t * P:t * P + P], WU[:, u, 0:HD], GBR[:, u, :], start=True, stop=True)
        mm.then_inc(S("p_r"), 1)
        for u in range(8):
            t, hh = divmod(u, 2)
            o = PS[half(hh), 5, t * P:t * P + P]
            e.matmul(o, WU[:, u, HD:P], GBR[:, u, :], start=True, stop=False)
            mm = e.matmul(o, VTK[:, t, j * P + HD * hh:j * P + HD * hh + HD], GKR[:, u, :], start=False, stop=True)
        mm.then_inc(S("p_y"), 1)
        for u in range(8):
            t, hh = divmod(u, 2)
            mm = e.matmul(PS[half(hh), 0, t * P:t * P + P].rearrange("p (c k) -> p c k", c=2), WU[:, u, 0:HD],
                          BPD[:, t, :, HD * hh:HD * hh + HD], start=True, stop=True)
        mm.then_inc(S("p_p"), 1)
        for u in range(8):
            t, hh = divmod(u, 2)
            for c in range(2):
                o = PS[half(hh), 1, (2 * t + c) * HD:(2 * t + c) * HD + HD]
                e.matmul(o, BPD[:, t, c, HD * hh:HD * hh + HD], WU[:, u, HD:P], start=True, stop=False)
                mm = e.matmul(o, KPD[:, t, c, HD * hh:HD * hh + HD], VTK[:, t, j * P + HD * hh:j * P + HD * hh + HD],
                              start=False, stop=True)
        mm.then_inc(S("p_q"), 1)

    def prep_tanh_act(e, n, which, bank):
        if which == 0:
            if n > 0:
                e.wait_ge(S("p_bonmm"), n)
        e.wait_ge(S("p_lora"), 2 * n + which + 1)
        if which == 1 and n > 0:
            e.wait_ge(S("p_fm"), n)
        e.activation(TMP[which][:, :], PS[:, bank, :], ACT.Tanh, scale=0.5,
                     bias=SM[:, 216 + 8 * which + n:217 + 8 * which + n]).then_inc(S("p_lorafree"), 1)

    def prep_exp_act(e, n):
        e.wait_ge(S("p_c"), n + 1)
        e.activation(TMP[3][:, :], TMP[3][:, :], ACT.Exp).then_inc(S("p_e"), 1)
        e.activation(TMP[0][:, :], TMP[2][:, :], ACT.Exp).then_inc(S("p_e"), 1)
        e.wait_ge(S("p_e"), 3 * n + 2)
        e.activation(TMP[2][:, :], TMP[2][:, :], ACT.Exp, scale=-1.0).then_inc(S("p_e"), 1)

    def pair_act(A, n):
        e = A.e
        j = n % NJ

        def copy_u(src, g):
            e.activation(UU[:, 4 * g:4 * g + 4, :], quad(src + g), ACT.Copy).then_inc(S("p_u"), 1)

        for g in range(2):
            e.wait_ge(S("p_u1"), 2 * n + g + 1)
            copy_u(6, g)
        for lv in range(LV):
            for g in range(2):
                e.wait_ge(S("p_un"), (n * LV + lv) * 2 + g + 1)
                copy_u(0, g)
            if lv + 1 < LV:
                for g in range(2):
                    e.wait_ge(S("p_ttp"), (n * (LV - 1) + lv) * 2 + g + 1)
                    e.activation(TT[:, 4 * g:4 * g + 4, :], quad(4 + g), ACT.Copy).then_inc(S("p_t"), 1)
            if lv == 0:
                e.wait_ge(S("p_tok"), 3 * n + 1)
                for hh in range(2):
                    i = e.activation(AXT[:, :, 0:HD].rearrange("p (t h) k -> p t h k", h=2)[:, :, hh, :],
                                     PS[:, 6 + hh, 0:NT * HD].rearrange("p (t k) -> p t k", t=NT), ACT.Copy)
                i.then_inc(S("p_tokfree"), 1)
            if lv == 1 and n + 1 < NPAIR:
                prep_tanh_act(e, n + 1, 0, 7)
            if lv == 2 and n + 1 < NPAIR:
                prep_tanh_act(e, n + 1, 1, 6)
            if lv in (2, 3):
                dst, bank = ((BPD, 7), (KPD, 6))[lv - 2]
                e.wait_ge(S("p_tok"), 3 * n + lv)
                for c in range(2):
                    i = e.activation(dst[half(c), :, c, :], PS[half(c), bank, :].rearrange("p (t k) -> p t k", t=NT), ACT.Copy)
                i.then_inc(S("p_tokfree"), 1)
            if lv == 3 and n + 1 < NPAIR:
                prep_exp_act(e, n + 1)
        for g in range(2):
            e.wait_ge(S("p_x0"), 2 * n + g + 1)
            for hh in range(2):
                i = e.activation(
                    AXT[:, 4 * g:4 * g + 4, HD:P].rearrange("p (t h) k -> p t h k", h=2)[:, :, hh, :],
                    PS[:, 6 + g, :].rearrange("p (t h k) -> p t h k", h=2, k=P)[:, :, hh, HD * hh:HD * hh + HD], ACT.Copy)
            i.then_inc(S("p_ax"), 1)
        for g in range(2):
            e.wait_ge(S("p_wu"), 2 * n + g + 1)
            e.activation(WU[:, 4 * g:4 * g + 4, :], quad(2 + g), ACT.Copy).then_inc(S("p_wuc"), 1)
        e.wait_ge(S("p_q"), n + 1)
        e.activation(QT[:, j, :, :], quad(1, HD), ACT.Copy).then_inc(S("p_qfree"), 1)

    def ecl(d, j):
        o = (128 if d == 0 else 64) + j * NCH
        return SM[:, o:o + NCH]

    def prep_sum_dve(V, n):
        e = V.e
        e.wait_ge(S("p_lorafree"), 2 * n + 1)
        V.mine(e.tensor_scalar(TMP[0][:, :], TMP[0][:, :], -0.5 * DECAY, -0.5 * DECAY, ALU.mult, ALU.add))
        e.wait_ge(S("p_lorafree"), 2 * n + 2)
        V.mine(e.tensor_scalar(TMP[1][:, :], TMP[1][:, :], 0.5, 0.5, ALU.mult, ALU.add))
        V.wait_mine()
        if n < NJ:
            V.mine(e.tensor_tensor_scan(TMP[2][:, :], rk("reset"), TMP[0][:, :], 0.0, ALU.mult, ALU.add))
        else:
            V.mine(e.tensor_tensor_scan(TMP[2][:, ::-1], rk("reset"), TMP[0][:, ::-1], 0.0, ALU.mult, ALU.add))
        V.wait_mine()
        e.tensor_tensor(TMP[3][:, :], TMP[2][:, :], TMP[0][:, :], ALU.subtract).then_inc(S("p_c"), 1)

    def prep_scale_dve(V, n):
        e = V.e
        d, j = divmod(n, NJ)
        r, k, kk, rho = ZS[ZR + j], ZS[ZK + j], KK[:, j, :], RHO[n % 2]
        e.wait_ge(S("p_e"), 3 * n + 1)
        for hh in range(2):
            e.scalar_tensor_tensor(ALP[half(hh), hh, :], KK[half(hh), j, :], -1.0, TMP[3][half(hh), :], ALU.mult, ALU.mult)
        e.wait_ge(S("p_e"), 3 * n + 2)
        for hh in range(2):
            V.mine(e.tensor_tensor(rho[half(hh), hh, :], r[half(hh), :], TMP[0][half(hh), :], ALU.mult))
        last = CH - 1 if d == 0 else 0
        V.mine(e.tensor_copy(ecl(d, j), TMP[0][:, last::CH]))
        e.wait_ge(S("p_e"), 3 * n + 3)
        V.wait_mine()
        V.mine(e.tensor_scalar(TMP[3][:, :], TMP[1][:, :], col("rwkv_k_a", j), SM[:, 232 + j:233 + j], ALU.mult, ALU.add))
        if n > 0:
            e.wait_ge(S("p_tok"), 3 * n)
        V.mine(e.tensor_tensor(BET[:, :], kk, TMP[1][:, :], ALU.mult))
        V.wait_mine()
        V.mine(e.tensor_tensor(TMP[3][:, :], TMP[3][:, :], k[:, :], ALU.mult))
        V.wait_mine()
        e.scalar_tensor_tensor(TMP[0][:, :], TMP[3][:, :], col("rwkv_r_k", j), r[:, :], ALU.mult, ALU.mult)
        e.tensor_tensor(BET[:, :], BET[:, :], TMP[2][:, :], ALU.mult)
        e.tensor_tensor(KAP[:, :], TMP[3][:, :], TMP[2][:, :], ALU.mult).then_inc(S("p_fm"), 1)

    def pair_dve(V, n):
        e = V.e
        d, j = divmod(n, NJ)
        id4 = ident.unsqueeze(1).to_broadcast([P, 4, P])
        fb = "fb"[d]
        for g in range(2):
            e.wait_ge(S("p_a"), 2 * n + g + 1)
            ai, tt = AI[:, 4 * g:4 * g + 4, :], TT[:, 4 * g:4 * g + 4, :]
            V.mine(e.tensor_tensor(ai, quad(6 + g), mask4("LT" if d == 0 else "UT"), ALU.mult))
            V.wait_mine()
            V.mine(e.tensor_tensor(ai, ai, id4, ALU.add))
            V.wait_mine()
            e.tensor_tensor(tt, ai, mask4("T1" + fb), ALU.mult).then_inc(S("p_t1"), 1)
        for q, (dst, m) in enumerate(((GKA, "UT" if d == 0 else "LT"), (GBR, "UTI" if d == 0 else "LTI"),
                                      (GKR, "UTI" if d == 0 else "LTI"))):
            for g in range(2):
                e.wait_ge(S("p_g"), 6 * n + 2 * q + g + 1)
                e.tensor_tensor(dst[:, 4 * g:4 * g + 4, :], quad((2, 3, 4, 5, 0, 1)[2 * q + g]), mask4(m),
                                ALU.mult).then_inc(S("p_gfree"), 1)
        for lv in range(LV):
            for g in range(2):
                e.wait_ge(S("p_x"), (n * LV + lv) * 2 + g + 1)
                e.tensor_tensor(XX[:, 4 * g:4 * g + 4, :], quad(2 + g), mask4(f"X{fb}{lv + 2}"), ALU.mult)\
                    .then_inc(S("p_xm"), 1)
            if lv == 1:
                e.wait_ge(S("p_bonmm"), n + 1)
                if d == 0:
                    e.tensor_copy(BON[j][:, :], PS[:, 6, :]).then_inc(S("p_bonfree"), 1)
                else:
                    e.tensor_tensor(BON[j][:, :], BON[j][:, :], PS[:, 6, :], ALU.add).then_inc(S("p_bonfree"), 1)
            if lv == 3 and n + 1 < NPAIR:
                prep_sum_dve(V, n + 1)
        if n + 1 < NPAIR:
            prep_scale_dve(V, n + 1)
        lo, hi, back = (1, NCH, -1) if d == 0 else (0, NCH - 1, 1)
        prev = ecl(d, j)[:, lo + back:hi + back].unsqueeze(2).to_broadcast([P, NCH - 1, HD])
        e.wait_ge(S("p_r"), n + 1)
        for hh in range(2):
            i = e.tensor_tensor(RT[half(hh), j, :], PS[half(hh), 4, :], RHO[n % 2][half(hh), hh, :], ALU.add)
        i.then_inc(S("p_rfree"), 1)
        e.wait_ge(S("p_y"), n + 1)
        if d == 0:
            e.tensor_copy(YL[:, j, :], PS[:, 5, :]).then_inc(S("p_yfree"), 1)
        else:
            e.tensor_tensor(YL[:, j, :], YL[:, j, :], PS[:, 5, :], ALU.add).then_inc(S("p_yfree"), 1)
        e.wait_ge(S("p_rfree"), n + 1)
        r = RT[:, j, lo * CH:hi * CH].rearrange("p (c t) -> p c t", t=CH)
        e.tensor_tensor(r, r, prev, ALU.mult)
        e.wait_ge(S("p_p"), n + 1)
        p = PT[:, j, lo:hi, :]
        e.tensor_tensor(p, quad(0, HD)[:, lo:hi, :], rk("ident2").unsqueeze(1).to_broadcast([P, NCH - 1, HD]), ALU.add)\
            .then_inc(S("p_pfree"), 1)
        e.wait_ge(S("p_pfree"), n + 1)
        e.tensor_tensor(p, p, prev, ALU.mult).then_inc(S("p_pt"), 1)

    def order(d):
        return list(range(NCH)) if d == 0 else list(range(NCH - 1, -1, -1))

    STEPS = NCH - 1

    def chain_pe(T, d):
        e, o = T.e, order(d)
        e.wait_ge(S("p_pt"), NJ * (d + 1))
        e.wait_ge(S("p_qfree"), NJ * (d + 1))
        for i in range(1, NCH):
            if i > 1:
                e.wait_ge(S("c_state"), d * (STEPS - 1) + i - 1)
            if i < STEPS:
                for hh in range(2):
                    for j in range(NJ):
                        mm = e.matmul(PS[half(hh), hh, j * HD:j * HD + HD], PT[half(hh), j, o[i], :],
                                      QT[half(hh), j, o[i - 1], :], start=True, stop=True)
                mm.then_inc(S("c_mm"), 1)
            if i > 2:
                e.wait_ge(S("c_yfree"), d * STEPS + i - 2)
            for hh in range(2):
                for j in range(NJ):
                    mm = e.matmul(PS[half(hh), 2 + 2 * (i % 2) + hh, j * HD:j * HD + HD], QT[half(hh), j, o[i - 1], :],
                                  RT[half(hh), j, o[i] * CH:o[i] * CH + CH], start=True, stop=True)
            mm.then_inc(S("c_y"), 1)
        e.wait_ge(S("c_yfree"), (d + 1) * STEPS)

    def chain_dve(V, d):
        e, o = V.e, order(d)
        e.wait_ge(S("p_yfree"), NJ * (d + 1))
        for i in range(1, NCH):
            if i < STEPS:
                e.wait_ge(S("c_mm"), d * (STEPS - 1) + i)
                for hh in range(2):
                    s = QT[half(hh), :, o[i], :]
                    m = e.tensor_tensor(s, s, PS[half(hh), hh, 0:NJ * HD].rearrange("p (j v) -> p j v", j=NJ), ALU.add)
                m.then_inc(S("c_state"), 1)
            e.wait_ge(S("c_y"), d * STEPS + i)
            for hh in range(2):
                y = YL[half(hh), :, o[i] * CH:o[i] * CH + CH]
                m = e.tensor_tensor(y, y, PS[half(hh), 2 + 2 * (i % 2) + hh, 0:NJ * CH].rearrange("p (j t) -> p j t", j=NJ),
                                    ALU.add)
            m.then_inc(S("c_yfree"), 1)

    def fin_pe(T):
        e = T.e
        for j in range(NJ):
            e.wait_ge(S("f_sq"), j + 1)
            if j >= 2:
                e.wait_ge(S("f_out"), j - 1)
            e.matmul(PS[:, 2 * (j % 2), :], rk("bones"), YQ[j % 2][:, :], start=True, stop=True).then_inc(S("f_mm"), 1)
            e.matmul(PS[:, 2 * (j % 2) + 1, :], WL2[:, 2, j * P:j * P + P], ZS[ZG][:, :], start=True, stop=True)\
                .then_inc(S("f_mm"), 1)

    def fin_act(A):
        e = A.e
        for j in range(NJ):
            if j >= 2:
                e.wait_ge(S("f_out"), j - 1)
            e.activation(YQ[j % 2][:, :], YL[:, j, :], ACT.Square).then_inc(S("f_sq"), 1)
            e.wait_ge(S("f_mm"), 2 * j + 1)
            e.activation(YQ[2 + j % 2][:, :], PS[:, 2 * (j % 2), :], ACT.Sqrt, scale=1.0 / HD, bias=SM[:, 25:26])\
                .then_inc(S("f_norm"), 1)
            e.wait_ge(S("f_out"), j + 1)
            e.activation(HHI[j][:, :], YQ[2 + j % 2][:, :], ACT.Copy).then_inc(S("f_hi"), 1)

    def fin_dve(V):
        e = V.e
        for j in range(NJ):
            y = YQ[2 + j % 2]
            e.wait_ge(S("f_norm"), j + 1)
            V.mine(e.reciprocal(y[:, :], y[:, :]))
            V.mine(e.tensor_tensor(BON[j][:, :], BON[j][:, :], ZS[ZV + j][:, :], ALU.mult))
            V.wait_mine()
            V.mine(e.tensor_tensor(y[:, :], y[:, :], YL[:, j, :], ALU.mult))
            V.wait_mine()
            V.mine(e.scalar_tensor_tensor(y[:, :], y[:, :], col("rwkv_out_gain", j), BON[j][:, :], ALU.mult, ALU.add))
            V.wait_mine()
            e.wait_ge(S("f_mm"), 2 * j + 2)
            e.tensor_tensor(y[:, :], y[:, :], PS[:, 2 * (j % 2) + 1, :], ALU.mult).then_inc(S("f_out"), 1)
            e.wait_ge(S("f_hi"), j + 1)
            e.wait_ge(S("f_out"), j + 1)
            V.mine(e.tensor_tensor(HLO[j][:, :], y[:, :], HHI[j][:, :].bitcast(F32), ALU.subtract))
            V.wait_mine()

    SC = 1.0 / math.sqrt(XD)

    def xattn_pe(T, l):
        e = T.e
        for t in range(NT):
            for h in range(XH):
                bank = 4 * (t % 2) + h // 2
                if h % 2 == 0 and t >= 2:
                    e.wait_ge(*at(f"xa{l}", "xe", XH * (t - 1)))
                for k in range(2):
                    mm = e.matmul(PS[:, bank, (h % 2) * MEM:(h % 2) * MEM + MEM], QFT[:, 2 * h + k, t * P:t * P + P],
                                  KFT[:, 2 * h + k, :], start=(k == 0), stop=(k == 1))
            mm.then_inc(sem(f"xa{l}", "xl"), 1)
            if t >= 1:
                xturn_pe(e, l, t - 1)
        xturn_pe(e, l, NT - 1)
        e.wait_ge(*at(f"xa{l}", "xpc", 2 * NT))
        for c in range(DC):
            if c >= 4:
                e.wait_ge(*at(f"xa{l}", "xolo", c - 3))
            for k in range(MT):
                mm = e.matmul(PS[:, c % 4, :], VMEM[:, k, c * P:c * P + P], PTR[:, c // 2, k, :], start=(k == 0), stop=(k == 1))
            mm.then_inc(sem(f"xa{l}", "xpv"), 1)

    def xturn_pe(e, l, t):
        e.wait_ge(*at(f"xa{l}", "xn", t + 1))
        if t >= 2:
            e.wait_ge(*at(f"xa{l}", "xpc", 2 * (t - 1)))
        for hp in range(2):
            for q in range(4):
                h, k = 2 * hp + q // 2, q % 2
                mm = e.transpose(PS[:, 4 * (t % 2) + 2 + hp, q * P:q * P + P], EX[t % 2][:, h, k * P:k * P + P], ident)
            mm.then_inc(sem(f"xa{l}", "xtp"), 1)

    def xattn_act(A, l):
        e = A.e
        for t in range(NT):
            e.wait_ge(*at(f"xa{l}", "xmx", t + 1))
            for h in range(XH):
                e.activation(EX[t % 2][:, h, :], PS[:, 4 * (t % 2) + h // 2, (h % 2) * MEM:(h % 2) * MEM + MEM], ACT.Exp,
                             scale=SC, bias=SM[:, 40 + 4 * (t % 2) + h:41 + 4 * (t % 2) + h],
                             accum_out=SM[:, 48 + 4 * (t % 2) + h:49 + 4 * (t % 2) + h]).then_inc(sem(f"xa{l}", "xe"), 1)
            if t >= 1:
                xcopy_act(e, l, t - 1)
        xcopy_act(e, l, NT - 1)
        for c in range(DC):
            e.wait_ge(*at(f"xa{l}", "xpv", c + 1))
            e.activation(HHI[c][:, :], PS[:, c % 4, :], ACT.Copy).then_inc(sem(f"xa{l}", "xohi"), 1)

    def xcopy_act(e, l, t):
        for hp in range(2):
            e.wait_ge(*at(f"xa{l}", "xtp", 2 * t + hp + 1))
            e.activation(PTR[:, 2 * hp:2 * hp + 2, :, t * P:t * P + P],
                         PS[:, 4 * (t % 2) + 2 + hp, :].rearrange("p (h k q) -> p h k q", h=2, k=2), ACT.Copy)\
                .then_inc(sem(f"xa{l}", "xpc"), 1)

    def xattn_dve(V, l):
        e = V.e
        for t in range(NT):
            b = 4 * (t % 2)
            e.wait_ge(*at(f"xa{l}", "xl", t + 1))
            if t >= 2:
                e.wait_ge(*at(f"xa{l}", "xtp", 2 * (t - 1)))
            for q in range(2):
                V.mine(e.tensor_reduce(SM[:, 32 + b + 2 * q:34 + b + 2 * q], PS[:, b + q, :].rearrange("p (h k) -> p h k", h=2),
                                       AX.X, ALU.max))
            V.wait_mine()
            e.tensor_scalar(SM[:, 40 + b:44 + b], SM[:, 32 + b:36 + b], -SC, None, ALU.mult).then_inc(sem(f"xa{l}", "xmx"), 1)
            e.wait_ge(*at(f"xa{l}", "xe", XH * (t + 1)))
            V.mine(e.reciprocal(SM[:, 56 + b:60 + b], SM[:, 48 + b:52 + b]))
            V.wait_mine()
            v = EX[t % 2][:, :, :]
            e.tensor_tensor(v, v, SM[:, 56 + b:60 + b].unsqueeze(2).to_broadcast([P, XH, MEM]), ALU.mult)\
                .then_inc(sem(f"xa{l}", "xn"), 1)
        for c in range(DC):
            e.wait_ge(*at(f"xa{l}", "xohi", c + 1))
            e.tensor_tensor(HLO[c][:, :], PS[:, c % 4, :], HHI[c][:, :].bitcast(F32), ALU.subtract).then_inc(sem(f"xa{l}", "xolo"), 1)

    def convw(l, tap, c):
        i = (l * 3 + tap) * 44 + c
        tile, row = divmod(i, 88)
        return COLS[:, (2 + tile) * P + row:(2 + tile) * P + row + 1]

    def up_act(A, l, h):
        name = f"up{l}{h}"

        def evac(gi, b, n):
            c = 12 * h + 2 * gi + b % 2
            dst = (CG if b < 2 else CV)[b % 2]
            cc = c if b < 2 else FC + c
            if gi > 0:
                A.e.wait_ge(*at(name, "lo", 2 * (gi - 1) + b % 2 + 1))
            A.e.activation(dst[:, :], PS[:, b, :], ACT.Identity, scale=convw(l, 1, cc),
                           bias=col("ffn_conv_b", l * 44 + cc)).then_inc(sem(name, "main"), 1)
            if b < 2:
                A.e.wait_ge(*at(name, "ev", n + 1))
                A.e.activation(SG[b][:, :], CG[b][:, :], ACT.Silu).then_inc(sem(name, "silu"), 1)
            else:
                A.e.wait_ge(*at(name, "g", 2 * gi + b - 1))
                A.e.activation(GHI[2 * gi + b - 2][:, :], SG[b - 2][:, :], ACT.Copy).then_inc(sem(name, "hi"), 1)
        return evac

    def up_dve(V, l, h):
        name = f"up{l}{h}"

        def evac(gi, b, n):
            c = 12 * h + 2 * gi + b % 2
            cc = c if b < 2 else FC + c
            dst = (CG if b < 2 else CV)[b % 2]
            V.e.wait_ge(*at(name, "main", n + 1))
            V.mine(V.e.scalar_tensor_tensor(dst[:, 1:SEQ], PS[:, b, 0:SEQ - 1], convw(l, 0, cc), dst[:, 1:SEQ],
                                            ALU.mult, ALU.add))
            V.wait_mine()
            V.e.scalar_tensor_tensor(dst[:, 0:SEQ - 1], PS[:, b, 1:SEQ], convw(l, 2, cc), dst[:, 0:SEQ - 1],
                                     ALU.mult, ALU.add).then_inc(sem(name, "ev"), 1)
            if b >= 2:
                i = 2 * gi + b - 2
                V.e.wait_ge(*at(name, "silu", i + 1))
                V.e.wait_ge(*at(name, "ev", n + 1))
                V.e.tensor_tensor(SG[b - 2][:, :], SG[b - 2][:, :], CV[b - 2][:, :], ALU.mult).then_inc(sem(name, "g"), 1)
                V.e.wait_ge(*at(name, "hi", i + 1))
                V.e.tensor_tensor(GLO[i][:, :], SG[b - 2][:, :], GHI[i][:, :].bitcast(F32), ALU.subtract)\
                    .then_inc(sem(name, "lo"), 1)
        return evac

    DSC = 1.0 / math.sqrt(DHD)
    NM = DH * NT

    def dlog_pe(e, m):
        h, t = divmod(m, NT)
        b = 2 * (m % 2)
        if m >= 2:
            e.wait_ge(S("ds"), 2 * (m - 1))
        for c in range(2):
            e.matmul(PS[:, b + c, :], QF[:, h, c, t * P:t * P + P], KF[:, h, :], start=True, stop=True).then_inc(S("dl"), 1)

    def dturn_pe(e, m):
        e.wait_ge(S("dat"), m + 1)
        if m >= 2:
            e.wait_ge(S("datc"), m - 1)
        for k in range(NT):
            mm = e.transpose(PS[:, 4 + m % 2, k * P:k * P + P], AT[m % 2][:, k * P:k * P + P], ident)
        mm.then_inc(S("dtp"), 1)

    def dpv_pe(e, m):
        h, t = divmod(m, NT)
        e.wait_ge(S("datc"), m + 1)
        if m >= 2:
            e.wait_ge(S("dov"), m - 1)
        for k in range(NT):
            mm = e.matmul(PS[:, 6 + m % 2, 0:P], ATT[m % 2][:, k, :], VV[:, k, h * P:h * P + P],
                          start=(k == 0), stop=(k == NT - 1))
        mm.then_inc(S("dpv"), 1)

    def dattn_pe(T):
        for m in range(NM + 3):
            if m < NM:
                dlog_pe(T.e, m)
            if 2 <= m < NM + 2:
                dturn_pe(T.e, m - 2)
            if m >= 3:
                dpv_pe(T.e, m - 3)

    def sx(m, i, n=1):
        o = 32 + 16 * (m % 4) + i
        return SM[:, o:o + n]

    def dattn_act(A):
        e = A.e

        def copy(m):
            e.wait_ge(S("dtp"), m + 1)
            if m >= 2:
                e.wait_ge(S("dpv"), m - 1)
            e.activation(ATT[m % 2][:, :, :], PS[:, 4 + m % 2, :].rearrange("p (k q) -> p k q", k=NT), ACT.Copy)\
                .then_inc(S("datc"), 1)

        def out(m):
            h, t = divmod(m, NT)
            e.wait_ge(S("dpv"), m + 1)
            e.activation(OTK[:, t, h * P:h * P + P], PS[:, 6 + m % 2, 0:P], ACT.Copy, scale=sx(m, 6))\
                .then_inc(S("dov"), 1)

        def bias(h):
            if h >= 2:
                e.wait_ge(S("ds"), 2 * NT * (h - 1))
            slope = 2.0 ** (-8.0 * (h + 1) / DH)
            e.activation(BIAS[h % 2][:, :], DIST[:, :], ACT.Copy, scale=-slope / DSC).then_inc(S("dbias"), 1)

        e.wait_ge(S("dist_in"), 16)
        bias(0)
        for m in range(NM + 3):
            if m < NM:
                if m % NT == 1 and m // NT + 1 < DH:
                    bias(m // NT + 1)
                e.wait_ge(S("dmx"), m + 1)
                for c in range(2):
                    e.activation(SS[m % 3][:, c, :], SS[m % 3][:, c, :], ACT.Exp, scale=DSC, bias=sx(m, 2 + c),
                                 accum_out=sx(m, 4 + c)).then_inc(S("de"), 1)
            if 2 <= m < NM + 2:
                copy(m - 2)
            if m >= 3:
                out(m - 3)

    def dattn_dve(V):
        e = V.e

        def first(m):
            h, t = divmod(m, NT)
            b = 2 * (m % 2)
            if t == 0:
                e.wait_ge(S("dbias"), h + 1)
            for c in range(2):
                e.wait_ge(S("dl"), 2 * m + c + 1)
                o = 384 - P * t
                e.tensor_tensor_reduce(SS[m % 3][:, c, :], PS[:, b + c, :], BIAS[h % 2][:, o:o + SEQ], 1.0, -3e38,
                                       ALU.add, ALU.max, sx(m, c)).then_inc(S("ds"), 1)
            e.wait_ge(S("ds"), 2 * m + 2)
            e.tensor_scalar(sx(m, 2, 2), sx(m, 0, 2), -DSC, None, ALU.mult).then_inc(S("dmx"), 1)

        def second(m):
            e.wait_ge(S("de"), 2 * m + 2)
            V.mine(e.reciprocal(sx(m, 6, 2), sx(m, 4, 2)))
            V.wait_mine()
            V.mine(e.scalar_tensor_tensor(sx(m, 8), sx(m, 4), SM[:, 26:27], sx(m, 7), ALU.mult, ALU.mult))
            V.wait_mine()
            if m >= 2:
                e.wait_ge(S("dtp"), m - 1)
            e.scalar_tensor_tensor(AT[m % 2][:, :], SS[m % 3][:, 1, :], sx(m, 8), SS[m % 3][:, 0, :],
                                   ALU.mult, ALU.add).then_inc(S("dat"), 1)

        for m in range(NM + 1):
            if m < NM:
                first(m)
            if m >= 1:
                second(m - 1)

    def dout_act(A):
        e = A.e
        for k in range(DC):
            e.wait_ge(*at("do", "ttp", k + 1))
            e.activation(HHI[k][:, :], PS[:, 4 + k % 4, :], ACT.Copy, scale=SM[:, 27:28]).then_inc(sem("do", "hi"), 1)

    def dout_dve(V):
        e = V.e
        for k in range(DC):
            e.wait_ge(*at("do", "hi", k + 1))
            e.scalar_tensor_tensor(HLO[k][:, :], PS[:, 4 + k % 4, :], SM[:, 27:28], HHI[k][:, :].bitcast(F32), ALU.mult,
                                   ALU.subtract).then_inc(sem("do", "tev"), 1)

    def loads(e):
        for t in range(NT):
            e.dma_start(X[:, t, :], a["x"][0, t * P:t * P + P, :]).then_inc(S("x_in"), 16)
        e.dma_start(KC[:, :], a["ident"]).then_inc(S("c_in"), 16)
        n = 0
        for i, tile in enumerate(VEC_TILES):
            row = 0
            for name, rows in tile:
                src = a[name]
                if name in ("diff_q_gain", "diff_k_gain"):
                    for h in range(2):
                        e.dma_start(VROW[i][row:row + 1, HD * h:HD * h + HD], src[0:1, :]).then_inc(S("v_in"), 16)
                        n += 16
                else:
                    if name == "ffn_conv_w":
                        v = src.rearrange("l t (r p) -> (l t r) p", p=P)[(i - 2) * 88:(i - 1) * 88, :]
                    elif name in ("rwkv_r_k", "rwkv_out_gain"):
                        v = src.rearrange("e (r h) n -> (e r) (h n)", h=2)
                    elif name in ("rwkv_w0", "rwkv_a0"):
                        v = src.rearrange("e d (r p) -> (e d r) p", p=P)
                    elif name == "mem_norm":
                        v = src.rearrange("(r p) -> r p", p=P)
                    else:
                        v = src.rearrange("e (r p) -> (e r) p", p=P)
                    e.dma_start(VROW[i][row:row + rows, :], v).then_inc(S("v_in"), 16)
                    n += 16
                row += rows
        assert n == V_IN
        e.dma_start(RC[:, :], a["rkc"]).then_inc(S("c_in"), 16)
        e.dma_start(WL2[:, 0, :], a["rwkv_w2"].rearrange("e d r c -> (e d r) c")).then_inc(S("c_in"), 16)
        e.dma_start(WL2[:, 1, :], a["rwkv_a2"].rearrange("e d r c -> (e d r) c")).then_inc(S("c_in"), 16)
        e.dma_start(WL2[:, 2, :], a["rwkv_g2"][0]).then_inc(S("c_in"), 16)
        e.dma_start(WS[:, :, :], a["sgu_w_s"][0].rearrange("g p q -> p g q")).then_inc(S("c_in"), 16)
        e.dma_start(SGUB[:, :, :].rearrange("p g q -> p (g q)"),
                    a["sgu_b"].rearrange("e g q -> e (g q)").to_broadcast([P, 512])).then_inc(S("c_in"), 16)
        for i, name in enumerate(("q1", "k1", "q2", "k2")):
            e.dma_start(LAM[:, HD * i:HD * i + HD], a[f"diff_lambda_{name}"].to_broadcast([P, HD])).then_inc(S("c_in"), 16)

    C_IN = 16 * 11
    V_IN = 16 * (sum(len(t) for t in VEC_TILES) + 2)

    def setup_pe(T):
        T.e.wait_ge(S("v_in"), V_IN)
        T.e.wait_ge(S("c_in"), C_IN)
        T.e.wait_ge(S("v_zero"), 5)
        for i in range(5):
            T.e.transpose(PS[:, i // 4, (i % 4) * P:(i % 4) * P + P], VROW[i][:, :], ident).then_inc(S("v_tp"), 1)

    def setup_pool(G):
        G.e.memset(SM[:, 16:24], -0.5)
        G.e.memset(SM[:, 24:25], 1e-12)
        G.e.memset(SM[:, 25:26], EPS)

    def setup_dve(V):
        e = V.e
        e.wait_ge(S("v_in"), V_IN)
        e.wait_ge(S("v_tp"), 5)
        V.mine(e.tensor_copy(COLS[:, 0:4 * P], PS[:, 0, :]))
        V.mine(e.tensor_copy(COLS[:, 4 * P:5 * P], PS[:, 1, 0:P]))
        V.wait_mine()
        e.wait_ge(S("c_in"), C_IN)
        V.mine(e.tensor_tensor(SM[:, 200:215], col("ab_shift_prev", 0, 15), col("ab_shift_next", 0, 15), ALU.add))
        V.wait_mine()
        e.tensor_scalar(SM[:, 200:215], SM[:, 200:215], -1.0, 1.0, ALU.mult, ALU.add)
        e.tensor_scalar(SM[:, 216:224], col("rwkv_w0", 0, 8), 0.5, None, ALU.mult)
        e.tensor_scalar(SM[:, 224:232], col("rwkv_a0", 0, 8), 0.5, None, ALU.mult)
        e.tensor_scalar(SM[:, 232:236], col("rwkv_k_a", 0, 4), -1.0, 1.0, ALU.mult, ALU.add)
        e.tensor_scalar(SM[:, 27:28], col("diff_out_gain"), 1.0 - LAMBDA_INIT, None, ALU.mult)
        for i in range(2):
            V.mine(e.tensor_tensor(LAM[:, P * i:P * i + HD], LAM[:, P * i:P * i + HD], LAM[:, P * i + HD:P * i + P], ALU.mult))
        V.wait_mine()
        for i in range(2):
            e.tensor_reduce(SM[:, 28 + i:29 + i], LAM[:, P * i:P * i + HD], AX.X, ALU.add).then_inc(S("lam_dot"), 1)
        e.wait_ge(S("lam_exp"), 1)
        V.mine(e.tensor_tensor(SM[:, 26:27], SM[:, 29:30], SM[:, 28:29], ALU.subtract))
        V.wait_mine()
        e.tensor_scalar(SM[:, 26:27], SM[:, 26:27], -LAMBDA_INIT, None, ALU.add)

    def setup_act(A):
        A.e.wait_ge(S("lam_dot"), 2)
        A.e.activation(SM[:, 28:30], SM[:, 28:30], ACT.Exp).then_inc(S("lam_exp"), 1)
        A.e.wait_ge(S("x_in"), 16 * NT)

    def gcol(name, l=0):
        return lambda k: col(name, l * DC + k)

    def norm_shares(tag, nt):
        shares(tag, "norm", sq=nt, var=1, rstd=1, xn=nt, tp=DC, hi=DC, lo=DC)

    def turn_shares(tag, nt):
        shares(tag, "turn", gvar=1, grstd=1, gn=nt, ttp=DC, tev=DC, hi=DC if tag == "do" else 0)

    norm_shares("n0", NT)
    for l in range(2):
        if l == 1:
            norm_shares("n1", NT)
            for tag in ("dk", "dq", "do"):
                turn_shares(tag, NT)
        norm_shares(f"m{l}", MT)
        norm_shares(f"nx{l}", NT)
        turn_shares(f"xk{l}", MT)
        turn_shares(f"xqn{l}", NT)
        shares(f"xa{l}", "xa", xe=XH * NT, xl=NT, xpc=2 * NT, xolo=DC, xpv=DC, xn=NT, xtp=2 * NT, xmx=NT, xohi=DC)
        norm_shares(f"nf{l}", NT)
        for h in range(2):
            n = len(gemms[f"up{l}{h}"])
            shares(f"up{l}{h}", "up", main=4 * n, silu=2 * n, g=2 * n, hi=2 * n, lo=2 * n)

    mhi, mlo = (lambda k: MNT[k][:, :]), (lambda k: MNL[k][:, :])
    ghi, glo = (lambda k: GHI[k][:, :]), (lambda k: GLO[k][:, :])

    def copy_out(A, name, dst):
        def evac(gi, b, n):
            A.e.activation(dst(gi, b), PS[:, b, :], ACT.Copy).then_inc(sem(name, "ev"), 1)
        return evac

    def to_tok(tok):
        return lambda gi, b: tok[:, b, gi * 512:gi * 512 + 512]

    def vg_act(A):
        def evac(gi, b, n):
            A.e.activation(VG[:, b, :], PS[:, b, :], ACT.Gelu_apprx_tanh).then_inc(sem("zv", "ev"), 1)
        return evac

    marks = {}

    def tensor_program(T):
        setup_pe(T)
        T.meet()
        norm_pe(T, "n0", XN, NT)
        T.meet()
        gemm_pe(T, "zf", hhi, hlo, tokens_out=False)
        gemm_pe(T, "zv", hhi, hlo)
        T.meet()
        mix0_pe(T)
        T.meet()
        lora_pe(T.e, 0, 0, 7)
        lora_pe(T.e, 0, 1, 6)
        T.e.wait_ge(S("p_lorafree"), 2)
        for d in range(2):
            for j in range(NJ):
                pair_pe(T, d * NJ + j)
            chain_pe(T, d)
        T.meet()
        fin_pe(T)
        T.meet()
        marks["weights_again"] = T.met
        for l in range(2):
            if l == 1:
                norm_pe(T, "n1", XN, NT)
                T.meet()
                gemm_pe(T, "dk", hhi, hlo)
                gemm_pe(T, "dq", hhi, hlo)
                turn_pe(T, "dk", TOKK, NT)
                gemm_pe(T, "dv", hhi, hlo)
                turn_pe(T, "dq", TOKQ, NT)
                T.meet()
                dattn_pe(T)
                T.meet()
                turn_pe(T, "do", OTK, NT)
                T.meet()
            gemm_pe(T, ("ab", "do")[l], hhi, hlo)
            norm_pe(T, f"m{l}", MXN, MT, 4)
            T.meet()
            gemm_pe(T, f"kk{l}", mhi, mlo)
            norm_pe(T, f"nx{l}", XN, NT, 4)
            T.e.wait_ge(*at(f"nx{l}", "lo", DC))
            gemm_pe(T, f"xq{l}", hhi, hlo)
            turn_pe(T, f"xk{l}", KTOK, MT)
            gemm_pe(T, f"kv{l}", mhi, mlo)
            turn_pe(T, f"xqn{l}", QTOK, NT)
            T.meet()
            xattn_pe(T, l)
            T.meet()
            gemm_pe(T, f"xo{l}", hhi, hlo)
            T.meet()
            norm_pe(T, f"nf{l}", XN, NT)
            T.meet()
            for h in range(2):
                gemm_pe(T, f"up{l}{h}", hhi, hlo, tokens_out=False)
                n = 2 * len(gemms[f"up{l}{h}"])
                T.e.wait_ge(*at(f"up{l}{h}", "lo", n))
                gemm_pe(T, f"dn{l}{h}", ghi, glo)
            T.meet()

    def scalar_program(A):
        def side(name, evac=None, limit=None):
            gemm_side(A, name, split_hi, evac, limit)

        setup_act(A)
        A.meet()
        norm_act_front(A, "n0", X, SQ, NT)
        norm_act_back(A, "n0", NT, gcol("mix_norm", 0), hhi)
        A.meet()
        side("zf", zf_act(A), fence)
        side("zv", vg_act(A), fence)
        A.meet()
        mix0_act(A)
        A.meet()
        prep_tanh_act(A.e, 0, 0, 7)
        prep_tanh_act(A.e, 0, 1, 6)
        prep_exp_act(A.e, 0)
        for n in range(NPAIR):
            pair_act(A, n)
        A.meet()
        fin_act(A)
        A.meet()
        for l in range(2):
            if l == 1:
                norm_act_front(A, "n1", X, SQ, NT)
                norm_act_back(A, "n1", NT, gcol("mix_norm", 1), hhi)
                A.meet()
                side("dk", copy_out(A, "dk", to_tok(TOKK)))
                side("dq", copy_out(A, "dq", to_tok(TOKQ)))
                turn_act(A, "dk", lambda k: KF[:, k, :], NT, lambda k: col("diff_k_gain"))
                side("dv", copy_out(A, "dv", to_tok(VV)))
                turn_split_act(A)
                A.meet()
                dattn_act(A)
                A.meet()
                dout_act(A)
                A.meet()
            A.e.wait_ge(S("mem_in"), 16 * (l + 1))
            norm_act_front(A, f"m{l}", MRAW, SQM, MT)
            side(("ab", "do")[l])
            norm_act_back(A, f"m{l}", MT, gcol("mem_norm"), mhi, 4)
            A.meet()
            norm_act_front(A, f"nx{l}", X, SQ, NT)
            side(f"kk{l}", copy_out(A, f"kk{l}", to_tok(KTOK)))
            norm_act_back(A, f"nx{l}", NT, gcol("cross_norm", l), hhi, 4)
            side(f"xq{l}", copy_out(A, f"xq{l}", to_tok(QTOK)))
            turn_act(A, f"xk{l}", lambda k: KFT[:, k, :], MT, lambda k: col("cross_k_gain", 2 * l + k % 2))
            side(f"kv{l}", copy_out(A, f"kv{l}", to_tok(VMEM)))
            turn_act(A, f"xqn{l}", lambda k: QFT[:, k, :], NT, lambda k: col("cross_q_gain", 2 * l + k % 2))
            A.meet()
            xattn_act(A, l)
            A.meet()
            side(f"xo{l}")
            A.meet()
            norm_act_front(A, f"nf{l}", X, SQ, NT)
            norm_act_back(A, f"nf{l}", NT, gcol("ffn_norm", l), hhi)
            A.meet()
            for h in range(2):
                side(f"up{l}{h}", up_act(A, l, h))
                side(f"dn{l}{h}")
            A.meet()

    def vector_program(V):
        def side(name, evac=None, limit=None):
            gemm_side(V, name, split_lo, evac, limit)

        setup_dve(V)
        V.meet()
        norm_dve_front(V, "n0", X, XN, NT)
        norm_dve_back(V, "n0", NT, gcol("mix_norm", 0), hhi, hlo)
        V.meet()
        side("zf", zf_dve(V), fence)
        side("zv", None, fence)
        V.meet()
        mix0_dve(V)
        V.meet()
        prep_sum_dve(V, 0)
        prep_scale_dve(V, 0)
        for d in range(2):
            for j in range(NJ):
                pair_dve(V, d * NJ + j)
            chain_dve(V, d)
        V.meet()
        fin_dve(V)
        V.meet()
        for l in range(2):
            if l == 1:
                norm_dve_front(V, "n1", X, XN, NT)
                norm_dve_back(V, "n1", NT, gcol("mix_norm", 1), hhi, hlo)
                V.meet()
                for h in range(2):
                    V.e.memset(QF[DHD * (1 - h):DHD * (1 - h) + DHD, :, h, :], 0.0)
                side("dk")
                group_norm_dve(V, "dk", TOKK, SQD, NT, DHD, "dk")
                side("dq")
                group_norm_dve(V, "dq", TOKQ, SQD, NT, DHD, "dq")
                side("dv")
                V.meet()
                dattn_dve(V)
                V.meet()
                group_norm_dve(V, "do", OTK, SQD, NT, P)
                dout_dve(V)
                V.meet()
            norm_dve_front(V, f"m{l}", MRAW, MXN, MT)
            side(("ab", "do")[l], add_residual(V, ("ab", "do")[l]))
            norm_dve_back(V, f"m{l}", MT, gcol("mem_norm"), mhi, mlo, 4)
            V.meet()
            norm_dve_front(V, f"nx{l}", X, XN, NT)
            side(f"kk{l}")
            norm_dve_back(V, f"nx{l}", NT, gcol("cross_norm", l), hhi, hlo, 4)
            group_norm_dve(V, f"xk{l}", KTOK, SQX, MT, XD, f"kk{l}")
            side(f"xq{l}")
            group_norm_dve(V, f"xqn{l}", QTOK, SQX, NT, XD, f"xq{l}")
            side(f"kv{l}")
            V.meet()
            xattn_dve(V, l)
            V.meet()
            side(f"xo{l}", add_residual(V, f"xo{l}"))
            V.meet()
            norm_dve_front(V, f"nf{l}", X, XN, NT)
            norm_dve_back(V, f"nf{l}", NT, gcol("ffn_norm", l), hhi, hlo)
            V.meet()
            for h in range(2):
                side(f"up{l}{h}", up_dve(V, l, h))
                side(f"dn{l}{h}", add_residual(V, f"dn{l}{h}"))
            V.meet()

    def pool_program(G):
        setup_pool(G)
        G.meet()
        norm_pool(G, "n0", NT)
        G.meet()
        G.meet()
        sgu_pool(G)
        G.meet()
        G.meet()
        G.meet()
        for l in range(2):
            if l == 1:
                norm_pool(G, "n1", NT)
                G.meet()
                G.e.dma_start(DIST[:, :], a["dist"]).then_inc(S("dist_in"), 16)
                group_norm_pool(G, "dk", NT, DHD)
                group_norm_pool(G, "dq", NT, DHD)
                G.meet()
                G.meet()
                group_norm_pool(G, "do", NT, P)
                G.meet()
            G.e.dma_start(MRAW[:, :, :], a["mem"][0].rearrange("(t p) d -> p t d", p=P)).then_inc(S("mem_in"), 16)
            norm_pool(G, f"m{l}", MT)
            G.meet()
            norm_pool(G, f"nx{l}", NT)
            group_norm_pool(G, f"xk{l}", MT, XD)
            group_norm_pool(G, f"xqn{l}", NT, XD)
            G.meet()
            G.meet()
            G.meet()
            norm_pool(G, f"nf{l}", NT)
            G.meet()
            G.meet()

    block = nc.Block()
    with block:
        @block.tensor
        def _(e):
            T = Engine("pe", e)
            tensor_program(T)
            marks["all"] = T.met

        @block.scalar
        def _(e):
            scalar_program(Engine("act", e))

        @block.vector
        def _(e):
            for i in range(5):
                e.memset(VROW[i][:, :], 0.0).then_inc(S("v_zero"), 1)
            vector_program(Engine("dve", e))

        @block.gpsimd
        def _(e):
            pool_program(Engine("pool", e))

        @block.sync
        def _(e):
            e.wait_ge(S("v_zero"), 5)
            loads(e)
            for i, (w, k, nk, pieces) in enumerate(plan):
                if i == fence:
                    for o in ("pe", "act", "dve", "pool"):
                        e.wait_ge(S(f"{o}_stage"), marks["weights_again"])
                if i >= 2:
                    e.wait_ge(S("w_lo"), i - 1)
                off = 0
                for c0, n in pieces:
                    e.dma_start(WRAW[i % 2][:, 0:nk, off:off + n],
                                w[k * P:(k + nk) * P, c0:c0 + n].rearrange("(k p) n -> p k n", p=P))\
                        .then_inc(S(f"raw_in{i % 2}"), 16)
                    off += n
            for o in ("pe", "act", "dve", "pool"):
                e.wait_ge(S(f"{o}_stage"), marks["all"])
            for t in range(NT):
                e.dma_start(out[0, t * P:t * P + P, :], X[:, t, :]).then_inc(S("stored"), 16)
            e.wait_ge(S("stored"), 16 * NT)


def host_constants():
    import numpy as np
    i = np.arange(P)
    p, f = i[:, None], i[None, :]
    same = lambda b: p // b == f // b
    c = {"LT": (p > f) & same(CH), "UT": (p < f) & same(CH), "UTI": (p <= f) & same(CH), "LTI": (p >= f) & same(CH),
         "T1f": (p >= f) & same(2), "T1b": (p <= f) & same(2)}
    for lv in range(2, 7):
        level = same(1 << lv) & ~same(1 << (lv - 1))
        c[f"Xf{lv}"] = (level & (p < f)) | (p == f)
        c[f"Xb{lv}"] = (level & (p > f)) | (p == f)
    c["bones"] = same(HD)
    c["reset"] = np.broadcast_to((np.arange(SEQ) % CH != 0)[None, :], (P, SEQ))
    c["ident2"] = (p % HD) == np.arange(HD)[None, :]
    rkc = np.zeros((P, RK_W), np.float32)
    for n, (o, w) in RK.items():
        rkc[:, o:o + w] = c[n]
    return {"ident": (p == f).astype(np.float32), "rkc": rkc,
            "dist": np.abs(p + 384 - np.arange(DIST_W)[None, :]).astype(np.float32)}


_INS = ['x', 'mem', 'mem_norm', 'mix_norm', 'cross_norm', 'ffn_norm', 'ab_w_in', 'ab_shift_prev', 'ab_shift_next',
        'rwkv_w0', 'rwkv_w2', 'rwkv_a0', 'rwkv_a2', 'rwkv_g2', 'rwkv_k_k', 'rwkv_k_a', 'rwkv_r_k', 'rwkv_out_gain',
        'sgu_v_gain', 'sgu_w_s', 'sgu_b', 'ab_w_out', 'diff_w_in', 'diff_q_gain', 'diff_k_gain', 'diff_lambda_q1',
        'diff_lambda_k1', 'diff_lambda_q2', 'diff_lambda_k2', 'diff_out_gain', 'diff_w_out', 'cross_wq', 'cross_wkv',
        'cross_q_gain', 'cross_k_gain', 'cross_wo', 'ffn_w_up', 'ffn_conv_w', 'ffn_conv_b', 'ffn_w_down']


def kernel(**inputs):
    import numpy as np
    import concourse.bacc as bacc
    from concourse.bass_utils import run_bass_kernel_spmd

    nc = bacc.Bacc("TRN2", target_bir_lowering=False, num_devices=1)
    arrays = {n: np.ascontiguousarray(inputs[n]) for n in _INS}
    arrays.update(host_constants())
    aps = {n: nc.dram_tensor(n, v.shape, mybir.dt.from_np(v.dtype), kind="ExternalInput").ap() for n, v in arrays.items()}
    out = nc.dram_tensor("out", (1, SEQ, D), F32, kind="ExternalOutput").ap()
    build(nc, aps, out)
    r = run_bass_kernel_spmd(nc, [arrays], core_ids=[0])
    return r.results[0]["out"]
```

```python
import math

import concourse.bass as bass
from concourse import mybir

F32 = mybir.dt.float32
F32R = mybir.dt.float32r
ALU = mybir.AluOpType
ACT = mybir.ActivationFunctionType
AX = mybir.AxisListType

P = 128
D = 1024
DC = D // P
SEQ = 512
NT = SEQ // P
MEM = 256
MT = MEM // P
EPS = 1e-6
BANK = 512
HD = 64
RW = 512
NJ = RW // P
CH = 64
NCH = SEQ // CH
SGU_G = 4
DH = 8
DHD = 64
XH = 4
XD = 256
FF = 2816
FC = FF // P
LAMBDA_INIT = 0.8 - 0.6 * math.exp(-0.3)
DECAY = math.exp(-0.5)

VEC_TILES = [
    [("mix_norm", 16), ("ffn_conv_b", 88), ("cross_q_gain", 4), ("cross_k_gain", 4)],
    [("cross_norm", 16), ("ffn_norm", 16), ("mem_norm", 8), ("ab_shift_prev", 15),
     ("ab_shift_next", 15), ("rwkv_w0", 8), ("rwkv_a0", 8), ("rwkv_k_k", 4), ("rwkv_k_a", 4),
     ("rwkv_r_k", 4), ("rwkv_out_gain", 4), ("sgu_v_gain", 4), ("diff_out_gain", 1),
     ("diff_q_gain", 1), ("diff_k_gain", 1)],
    [("ffn_conv_w", 88)], [("ffn_conv_w", 88)], [("ffn_conv_w", 88)],
]
COL = {}
for _i, _tile in enumerate(VEC_TILES):
    _r = 0
    for _name, _n in _tile:
        COL.setdefault(_name, _i * P + _r)
        _r += _n

DIST_W = SEQ + 384
MASKS = ["LT", "UT", "UTI", "LTI", "T1f", "T1b"] + [f"X{d}{j}" for d in "fb" for j in range(2, 7)]
RK = {m: (i * P, P) for i, m in enumerate(MASKS)}
RK["bones"] = (len(MASKS) * P, P)
RK["reset"] = (len(MASKS) * P + P, SEQ)
RK["ident2"] = (len(MASKS) * P + P + SEQ, HD)
RK_W = len(MASKS) * P + P + SEQ + HD


class Tally:

    def __init__(self, sem):
        self.sem, self.n = sem, 0

    def sig(self, instruction, by=1):
        instruction.then_inc(self.sem, by)
        self.n += by
        return self.n


def build(nc, a, out):
    sems = {}

    def S(name):
        if name not in sems:
            sems[name] = nc.alloc_semaphore(name)
        return sems[name]

    left, base = {}, {}

    def shares(tag, kind, **totals):
        for x, n in totals.items():
            base[tag, x] = (S(f"{kind}_{x}"), left.get((kind, x), 0))
            left[kind, x] = left.get((kind, x), 0) + n

    def sem(tag, x):
        return base[tag, x][0]

    def at(tag, x, n):
        s, b = base[tag, x]
        return s, b + n

    low = (nc.sbuf_base + 31) // 32 * 32

    def sb(name, shape, at, dt=F32):
        return nc.alloc_sbuf_tensor_at(name, shape, dt, offset=low + at)

    X = sb("X", [P, NT, D], 0)
    WRAW = [sb(f"WRAW{i}", [P, 4, 512], 16384 + 8192 * i) for i in range(2)]
    WHI = [sb(f"WHI{i}", [P, 4, 512], 32768 + 16384 * i, F32R) for i in range(3)]
    WLO = [sb(f"WLO{i}", [P, 4, 512], 32768 + 16384 * i + 8192, F32R) for i in range(3)]
    HIS = sb("HIS", [P, DC, SEQ], 81920, F32R)
    LOS = sb("LOS", [P, DC, SEQ], 98304, F32R)
    HHI, HLO = ([t[:, k, :] for k in range(DC)] for t in (HIS, LOS))
    COLS = sb("COLS", [P, 5 * P], 114688)
    KC = sb("KC", [P, P], 117248)
    SM = sb("SM", [P, 256], 117760)
    DIST = sb("DIST", [P, DIST_W], 118784)
    LAM = sb("LAM", [P, 256], 122368)
    R0 = 123392
    ident = KC[:, 0:P]

    VROW = [sb(f"VROW{i}", [P, P], R0 + 40000 + 512 * i) for i in range(5)]
    RC = sb("RC", [P, RK_W], R0)
    r1 = R0 + 4 * RK_W
    WL2 = sb("WL2", [P, 3, 512], r1)
    SGUB = sb("SGUB", [P, 4, P], r1 + 6144)
    WS = sb("WS", [P, 4, P], r1 + 8192)
    r2 = r1 + 10240
    ZS = [sb(f"ZS{c}", [P, SEQ], r2 + 2048 * c) for c in range(15)]
    KK = sb("KK", [P, NJ, SEQ], r2 + 30720)
    r3 = r2 + 38912
    names7 = ["GBR", "GKA", "GKR", "AI", "TT", "UU", "XX"]
    U7 = {n: sb(n, [P, 8, P], r3 + 4096 * i) for i, n in enumerate(names7)}
    GBR, GKA, GKR, AI, TT, UU, XX = (U7[n] for n in names7)
    UG = sb("UG", [P, 4, SEQ], r3)
    VG = sb("VG", [P, NT, 512], r3 + 8192)
    WST = sb("WST", [P, 4, P], r3 + 16384)
    SQN = [sb(f"SQN{j}", [P, SEQ], r3 + 18432 + 2048 * j) for j in range(NJ)]
    SQ1 = sb("SQ1", [P, 512], r3 + 26624)
    BT = [sb(f"BT{i}", [P, SEQ], r3 + 22528 + 2048 * i) for i in range(2)]
    w0 = 16384
    TMP = [sb(f"TMP{i}", [P, SEQ], w0 + 2048 * i) for i in range(4)]
    ALP = sb("ALP", [P, 2, SEQ], w0 + 8192)
    RHO = [sb("RHO0", [P, 2, SEQ], w0 + 12288), sb("RHO1", [P, 2, SEQ], 118784)]
    BET = sb("BET", [P, SEQ], w0 + 16384)
    KAP = sb("KAP", [P, SEQ], w0 + 18432)
    BPD = sb("BPD", [P, NT, 2, P], w0 + 20480)
    KPD = sb("KPD", [P, NT, 2, P], w0 + 24576)
    AXT = sb("AXT", [P, 8, P], w0 + 28672)
    WU = sb("WU", [P, 8, P], w0 + 32768)
    PT = sb("PT", [P, NJ, NCH, HD], w0 + 36864)
    QT = sb("QT", [P, NJ, NCH, HD], w0 + 45056)
    RT = sb("RT", [P, NJ, SEQ], w0 + 53248)
    BON = [sb(f"BON{j}", [P, SEQ], w0 + 61440 + 2048 * j if j < 2 else r1 + 6144 + 2048 * (j - 2))
           for j in range(NJ)]
    YL = sb("YL", [P, NJ, SEQ], 81920)
    VTK = sb("VTK", [P, NT, RW], 98304)
    YQ = [sb(f"YQ{i}", [P, SEQ], r3 + 2048 * i) for i in range(8)]
    XN = sb("XN", [P, NT, D], R0 + 49152 + 8192)
    SQ = sb("SQ", [P, D], R0 + 49152 + 8192 + 16384)
    MNT = [sb(f"MHI{k}", [P, MEM], R0 + 1024 * k, F32R) for k in range(DC)]
    MNL = [sb(f"MLO{k}", [P, MEM], R0 + 8192 + 1024 * k, F32R) for k in range(DC)]
    MRAW = sb("MRAW", [P, MT, D], R0 + 16384)
    MXN = sb("MXN", [P, MT, D], R0 + 24576)
    KTOK = sb("KTOK", [P, MT, D], R0 + 16384)
    KFT = sb("KFT", [P, DC, MEM], R0 + 32768)
    VMEM = sb("VMEM", [P, MT, D], R0 + 40960)
    SQX = sb("SQX", [P, D], R0 + 49152)
    SQM = sb("SQM", [P, D], R0 + 53248)
    QTOK = sb("QTOK", [P, NT, D], R0 + 57344)
    QFT = sb("QFT", [P, DC, SEQ], R0)
    PTR = sb("PTR", [P, XH, MT, SEQ], R0 + 16384)
    EX = [sb(f"EX{i}", [P, XH, MEM], R0 + 57344 + 4096 * i) for i in range(2)]
    GHI = [sb(f"GHI{k}", [P, SEQ], R0 + 2048 * k, F32R) for k in range(12)]
    GLO = [sb(f"GLO{k}", [P, SEQ], R0 + 24576 + 2048 * k, F32R) for k in range(12)]
    CG = [sb(f"CG{i}", [P, SEQ], R0 + 49152 + 2048 * i) for i in range(2)]
    CV = [sb(f"CV{i}", [P, SEQ], R0 + 53248 + 2048 * i) for i in range(2)]
    SG = [sb(f"SG{i}", [P, SEQ], R0 + 57344 + 2048 * i) for i in range(2)]
    TOKK = sb("TOKK", [P, NT, D], R0)
    TOKQ = sb("TOKQ", [P, NT, D], R0 + 16384)
    KF = sb("KF", [P, DC, SEQ], R0 + 32768)
    QF = sb("QF", [P, DC, 2, SEQ], R0 + 49152)
    VV = sb("VV", [P, NT, D], R0)
    OTK = sb("OTK", [P, NT, D], R0 + 16384)
    SQO = sb("SQO", [P, P], 122368)
    SQD = sb("SQD", [P, D], R0 + 81920)
    AT = [sb(f"AT{i}", [P, SEQ], R0 + 81920 + 2048 * i) for i in range(2)]
    SS = [sb(f"SS{i}", [P, 2, SEQ], 81920 + 4096 * i) for i in range(3)]
    ATT = [sb(f"ATT{i}", [P, NT, P], 81920 + 12288 + 2048 * i) for i in range(2)]
    BIAS = [sb(f"BIAS{i}", [P, DIST_W], 98304 + 4096 * i) for i in range(2)]

    PS = nc.alloc_psum_tensor("PS", [P, 8, BANK], F32)

    def col(name, i=0, n=1):
        c = COL[name] + i
        return COLS[:, c:c + n]

    def rk(name, p0=0, p1=P):
        o, w = RK[name]
        return RC[p0:p1, o:o + w]

    def mask4(name):
        return rk(name).unsqueeze(1).to_broadcast([P, 4, P])

    plan, use = [], {}
    used_at = {}
    gemms = {}
    raw_level = []
    slot_total = [0, 0]

    def gemm(name, w, groups, k0, k1, nb, late=False):
        widths = [nb] * len(groups) if isinstance(nb, int) else nb
        slabs = list(range(k0, k1, 4))
        order = [(gi, k) for gi in range(len(groups)) for k in slabs]
        if late:
            order = [(gi, k) for k in reversed(slabs) for gi in range(len(groups))]
        g_list = [([], n, sum(widths[:gi])) for gi, n in enumerate(widths)]
        for gi, k in order:
            steps, n, before = g_list[gi]
            pieces, nk, i = groups[gi], min(4, k1 - k), len(plan)
            slot_total[i % 2] += 16 * len(pieces)
            raw_level.append(slot_total[i % 2])
            plan.append((w, k, nk, pieces))
            steps.append((i, k - k0, nk))
            if len(steps) < len(slabs):
                use[name] = use.get(name, 0) + 1
                used_at[i] = ("wused", use[name])
            else:
                used_at[i] = ("done", before + n)
        banks = sum(widths)
        gemms[name] = g_list
        shares(name, "g", done=banks, wused=use.get(name, 0), ev=banks)
        for steps, _, _ in g_list:
            for i, _, _ in steps:
                used_at[i] = at(name, *used_at[i])

    halves = [[(0, 512)], [(512, 512)]]
    gemm("zf", a["ab_w_in"][0], [[(512 * g, 512)] for g in range(3)] + [[(1536, 384)]], 0, DC, [4, 4, 4, 3])
    gemm("zu", a["ab_w_in"][0], [[(1920, 512)]], 0, DC, 4)
    gemm("zv", a["ab_w_in"][0], [[(2432, 512)]], 0, DC, 4)
    fence = len(plan)
    gemm("ab", a["ab_w_out"][0], halves, 0, DC, NT, late=True)

    def plan_tail(l):
        gemm(f"kk{l}", a["cross_wkv"][l], halves, 0, DC, MT)
        gemm(f"xq{l}", a["cross_wq"][l], halves, 0, DC, NT)
        gemm(f"kv{l}", a["cross_wkv"][l], [[(D, 512)], [(D + 512, 512)]], 0, DC, MT)
        gemm(f"xo{l}", a["cross_wo"][l], halves, 0, DC, NT)
        for h, (c0, c1) in enumerate(((0, 12), (12, 22))):
            gemm(f"up{l}{h}", a["ffn_w_up"][l],
                 [[(c * P, 256), (FF + c * P, 256)] for c in range(c0, c1, 2)], 0, DC, 4)
            gemm(f"dn{l}{h}", a["ffn_w_down"][l], halves, c0, c1, NT)

    plan_tail(0)
    gemm("dk", a["diff_w_in"][0], [[(1024, 512)], [(1536, 512)]], 0, DC, NT)
    gemm("dq", a["diff_w_in"][0], halves, 0, DC, NT)
    gemm("dv", a["diff_w_in"][0], [[(2048, 512)], [(2560, 512)]], 0, DC, NT)
    gemm("do", a["diff_w_out"][0], halves, 0, DC, NT)
    plan_tail(1)

    class Engine:

        def __init__(self, name, eng):
            self.name, self.e = name, eng
            self.own = Tally(S(f"{name}_own"))
            self.met = 0
            self.split = 0

        def mine(self, instruction):
            self.own.sig(instruction)

        def wait_mine(self):
            self.e.wait_ge(self.own.sem, self.own.n)

        def meet(self):
            self.e.drain().then_inc(S(f"{self.name}_stage"), 1)
            self.met += 1
            for other in ("pe", "act", "dve", "pool"):
                if other != self.name:
                    self.e.wait_ge(S(f"{other}_stage"), self.met)

    def part(t, i):
        w, k, nk, pieces = plan[i]
        return t[:, 0:nk, 0:sum(n for _, n in pieces)]

    def load_slab(e, i):
        w, k, nk, pieces = plan[i]
        off = 0
        for c0, n in pieces:
            e.dma_start(WRAW[i % 2][:, 0:nk, off:off + n],
                        w[k * P:(k + nk) * P, c0:c0 + n].rearrange("(k p) n -> p k n", p=P))\
                .then_inc(S(f"raw_in{i % 2}"), 16)
            off += n

    def split_hi(A, upto):
        while A.split < min(upto, len(plan)):
            i = A.split
            A.e.wait_ge(S(f"raw_in{i % 2}"), raw_level[i])
            if i >= 3:
                A.e.wait_ge(*used_at[i - 3])
            A.e.activation(part(WHI[i % 3], i), part(WRAW[i % 2], i), ACT.Copy).then_inc(S("w_hi"), 1)
            A.split += 1

    def split_lo(V, upto):
        while V.split < min(upto, len(plan)):
            i = V.split
            V.e.wait_ge(S("w_hi"), i + 1)
            V.e.tensor_tensor(part(WLO[i % 3], i), part(WRAW[i % 2], i), part(WHI[i % 3], i).bitcast(F32),
                              ALU.subtract).then_inc(S("w_lo"), 1)
            V.split += 1

    def gemm_pe(T, name, hi, lo, tokens_out=True, nt=SEQ, operand=None, beside=None):
        e = T.e
        for i, gi, si in sorted((i, gi, si) for gi, g in enumerate(gemms[name]) for si, (i, _, _) in enumerate(g[0])):
            steps, nb, banks = gemms[name][gi]
            _, kb, nk = steps[si]
            if beside is not None and gi == 0:
                beside(si)
            e.wait_ge(S("w_lo"), i + 1)
            if operand is not None and gi == 0:
                e.wait_ge(*operand(kb + nk))
            width = sum(n for _, n in plan[i][3])
            for b in range(nb):
                if si == 0 and banks_before[name, gi] is not None:
                    e.wait_ge(*bank_free(name, gi, b))
                n = width if tokens_out else nt
                o = PS[:, bank_base(name, gi) + b, 0:n]
                for kk in range(nk):
                    k = kb + kk
                    for q, (wt, ht) in enumerate(((WHI, hi), (WHI, lo), (WLO, hi))):
                        w = wt[i % 3]
                        if tokens_out:
                            l, r = ht(k)[:, b * P:b * P + P], w[:, kk, 0:width]
                        else:
                            l, r = w[:, kk, b * P:b * P + P], ht(k)[:, 0:nt]
                        mm = e.matmul(o, l, r, start=(si == 0 and kk == 0 and q == 0),
                                      stop=(si == len(steps) - 1 and kk == nk - 1 and q == 2))
                if si == len(steps) - 1:
                    mm.then_inc(sem(name, "done"), 1)
            if si < len(steps) - 1:
                mm.then_inc(sem(name, "wused"), 1)

    def gemm_side(E, name, split, evac, limit=None, beside=None):
        s = 0
        for gi, (steps, nb, banks) in enumerate(gemms[name]):
            for i, _, _ in steps:
                split(E, i + 3 if limit is None else min(i + 3, limit))
                if beside is not None:
                    beside(s)
                s += 1
            if evac is not None:
                for b in range(nb):
                    E.e.wait_ge(*at(name, "done", banks + b + 1))
                    evac(gi, b, banks + b)

    def bank_base(name, gi=0):
        return 4 if name.startswith("dn") or (name, gi) == ("ab", 1) else 0

    banks_before, before = {}, {0: None, 4: None}
    for _name, _groups in gemms.items():
        for _gi, (_, _nb, _banks) in enumerate(_groups):
            banks_before[_name, _gi] = before[bank_base(_name, _gi)]
            before[bank_base(_name, _gi)] = (_name, _nb, _banks)

    def bank_free(name, gi, b):
        other, nb, banks = banks_before[name, gi]
        return at(other, "ev", banks + min(b, nb - 1) + 1)

    hhi, hlo = (lambda k: HHI[k][:, :]), (lambda k: HLO[k][:, :])

    def norm_act_front(A, tag, src, sq, nt, arrives=False):
        e = A.e
        for t in range(nt):
            if arrives:
                e.wait_ge(S(f"x_in{t}"), 16)
            e.activation(sq[:, :], src[:, t, :], ACT.Square, accum_out=SM[:, t:t + 1]).then_inc(sem(tag, "sq"), 1)
            e.wait_ge(*at(tag, "sq", t + 1))

    def norm_act_back(A, tag, nt, gain, hi, b0=0):
        e = A.e
        for k in range(DC):
            e.wait_ge(*at(tag, "tp", k + 1))
            e.activation(hi(k)[:, 0:nt * P], PS[:, b0 + k % 4, 0:nt * P], ACT.Copy,
                         scale=gain(k)).then_inc(sem(tag, "hi"), 1)

    def norm_pool(G, tag, nt):
        G.e.wait_ge(*at(tag, "var", 1))
        G.e.tensor_tensor(SM[:, 8:8 + nt], SM[:, 4:4 + nt], SM[:, 16:16 + nt], ALU.pow).then_inc(sem(tag, "rstd"), 1)

    def norm_dve_front(V, tag, src, xn, nt):
        e = V.e
        e.wait_ge(*at(tag, "sq", nt))
        e.tensor_scalar(SM[:, 4:4 + nt], SM[:, 0:nt], 1.0 / D, EPS, ALU.mult, ALU.add).then_inc(sem(tag, "var"), 1)
        e.wait_ge(*at(tag, "rstd", 1))
        for t in range(nt):
            e.tensor_scalar(xn[:, t, :], src[:, t, :], SM[:, 8 + t:9 + t], None, ALU.mult).then_inc(sem(tag, "xn"), 1)

    def norm_dve_back(V, tag, nt, gain, hi, lo, b0=0, k0=0, k1=DC):
        e = V.e
        for k in range(k0, k1):
            e.wait_ge(*at(tag, "hi", k + 1))
            e.scalar_tensor_tensor(lo(k)[:, 0:nt * P], PS[:, b0 + k % 4, 0:nt * P], gain(k),
                                   hi(k)[:, 0:nt * P].bitcast(F32), ALU.mult, ALU.subtract).then_inc(sem(tag, "lo"), 1)

    def square_tile_act(A, name, tag):
        def evac(gi, b, n):
            if gi == 1:
                A.e.wait_ge(*at(name, "ev", n + 1))
                if b > 0:
                    A.e.wait_ge(*at(tag, "sq", b))
                A.e.activation(SQ[:, :], X[:, b, :], ACT.Square, accum_out=SM[:, b:b + 1]).then_inc(sem(tag, "sq"), 1)
        return evac

    def norm_pool_tiles(G, tag):
        for t in range(NT):
            G.e.wait_ge(*at(tag, "var", t + 1))
            G.e.tensor_tensor(SM[:, 8 + t:9 + t], SM[:, 4 + t:5 + t], SM[:, 16:17], ALU.pow).then_inc(sem(tag, "rstd"), 1)

    def var_tile_dve(V, tag, t):
        V.e.wait_ge(*at(tag, "sq", t + 1))
        V.e.tensor_scalar(SM[:, 4 + t:5 + t], SM[:, t:t + 1], 1.0 / D, EPS, ALU.mult, ALU.add).then_inc(sem(tag, "var"), 1)

    def scale_tile_dve(V, tag, t):
        V.e.wait_ge(*at(tag, "rstd", t + 1))
        V.e.tensor_scalar(XN[:, t, :], X[:, t, :], SM[:, 8 + t:9 + t], None, ALU.mult).then_inc(sem(tag, "xn"), 1)

    def residual_and_norm_dve(V, name, tag):
        add = add_residual(V, name)

        def evac(gi, b, n):
            add(gi, b, n)
            if gi == 1:
                if b >= 1:
                    var_tile_dve(V, tag, b - 1)
                if b >= 2:
                    scale_tile_dve(V, tag, b - 2)
                if b == NT - 1:
                    var_tile_dve(V, tag, b)
                    scale_tile_dve(V, tag, b - 1)
                    scale_tile_dve(V, tag, b)
        return evac

    def norm_pe(T, tag, xn, nt, b0=0):
        e = T.e
        for k in range(DC):
            if k >= 4:
                e.wait_ge(*at(tag, "lo", k - 3))
            for t in range(nt):
                if k == 0:
                    e.wait_ge(*at(tag, "xn", t + 1))
                mm = e.transpose(PS[:, b0 + k % 4, t * P:t * P + P], xn[:, t, k * P:k * P + P], ident)
            mm.then_inc(sem(tag, "tp"), 1)

    def add_residual(V, name):
        def evac(gi, b, n):
            o = X[:, b, gi * 512:gi * 512 + 512]
            V.e.tensor_tensor(o, o, PS[:, bank_base(name, gi) + b, :], ALU.add).then_inc(sem(name, "ev"), 1)
        return evac

    def group_sums_dve(V, tok, sq, t, w, ready=None):
        e, n = V.e, D // w
        if ready is not None:
            e.wait_ge(*at(ready, "ev", gemms[ready][-1][2] + gemms[ready][-1][1]))
        V.mine(e.tensor_tensor(sq[:, :], tok[:, t, :], tok[:, t, :], ALU.mult))
        V.wait_mine()
        V.mine(e.tensor_reduce(SM[:, 32 + t * n:32 + t * n + n], sq[:, :].rearrange("p (g w) -> p g w", w=w),
                               AX.X, ALU.add))
        V.wait_mine()

    def group_var_dve(V, tag, nt, w, sums=32, var=96):
        n = nt * (D // w)
        V.e.tensor_scalar(SM[:, var:var + n], SM[:, sums:sums + n], 1.0 / w, EPS, ALU.mult, ALU.add)\
            .then_inc(sem(tag, "gvar"), 1)

    def group_scale_dve(V, tag, tok, t, w, rstd=160):
        e, n = V.e, D // w
        if t == 0:
            e.wait_ge(*at(tag, "grstd", 1))
        v = tok[:, t, :].rearrange("p (g w) -> p g w", w=w)
        e.tensor_tensor(v, v, SM[:, rstd + t * n:rstd + t * n + n].unsqueeze(2).to_broadcast([P, n, w]),
                        ALU.mult).then_inc(sem(tag, "gn"), 1)

    def group_norm_beside(V, tag, tok, ready):
        def beside(s):
            for t in (2 * (s % 2), 2 * (s % 2) + 1):
                if s < 2:
                    group_sums_dve(V, tok, SQD, t, DHD, ready)
                else:
                    group_scale_dve(V, tag, tok, t, DHD)
            if s == 1:
                group_var_dve(V, tag, NT, DHD)
        return beside

    def head_sums_act(A, name, dst, sums):
        def evac(gi, b, n):
            for q in range(2):
                A.e.activation(SQX[:, 0:XD], PS[:, b, q * XD:q * XD + XD], ACT.Square,
                               accum_out=SM[:, sums + 4 * b + 2 * gi + q:sums + 4 * b + 2 * gi + q + 1])\
                    .then_inc(sem(name, "hsum"), 1)
                A.e.wait_ge(*at(name, "hsum", 2 * n + q + 1))
            A.e.activation(dst(gi, b), PS[:, b, :], ACT.Copy).then_inc(sem(name, "ev"), 1)
        return evac

    def head_norm_dve(V, tag, name, tok, nt, o):
        V.e.wait_ge(*at(name, "ev", gemms[name][-1][2] + gemms[name][-1][1]))
        group_var_dve(V, tag, nt, XD, 32 + o, 96 + o)
        for t in range(nt):
            group_scale_dve(V, tag, tok, t, XD, 160 + o)

    def group_norm_pool(G, tag, nt, w, o=0):
        n = D // w * nt
        G.e.wait_ge(*at(tag, "gvar", 1))
        G.e.tensor_tensor(SM[:, 160 + o:160 + o + n], SM[:, 96 + o:96 + o + n], SM[:, 16:17].to_broadcast([P, n]), ALU.pow)\
            .then_inc(sem(tag, "grstd"), 1)

    def turn_pe(T, tag, tok, nt, bank0=4):
        e = T.e
        for k in range(DC):
            if k >= 4:
                e.wait_ge(*at(tag, "tev", k - 3))
            for t in range(nt):
                if k == 0:
                    e.wait_ge(*at(tag, "gn", t + 1))
                mm = e.transpose(PS[:, bank0 + k % 4, t * P:t * P + P], tok[:, t, k * P:k * P + P], ident)
            mm.then_inc(sem(tag, "ttp"), 1)

    def turn_split_act(A):
        for k in range(DC):
            A.e.wait_ge(*at("dq", "ttp", k + 1))
            for c in range(2):
                r = slice(DHD * c, DHD * c + DHD)
                i = A.e.activation(QF[r, k, c, :], PS[r, 4 + k % 4, :], ACT.Copy,
                                   scale=COLS[r, COL["diff_q_gain"]:COL["diff_q_gain"] + 1])
            i.then_inc(sem("dq", "tev"), 1)

    def turn_act(A, tag, dst, nt, gain, b0=4):
        for k in range(DC):
            A.e.wait_ge(*at(tag, "ttp", k + 1))
            A.e.activation(dst(k), PS[:, b0 + k % 4, 0:nt * P], ACT.Copy, scale=gain(k))\
                .then_inc(sem(tag, "tev"), 1)

    def half(hh):
        return slice(HD * hh, HD * hh + HD)

    ZR, ZK, ZV, ZW, ZA, ZG = 0, 4, 8, 12, 13, 14
    ZN = 15

    def zf_act(A):
        def evac(gi, b, n):
            c = gi * 4 + b
            A.e.activation(ZS[c][:, :], PS[:, b, :], ACT.Copy, scale=SM[:, 200 + c:201 + c]).then_inc(S("zf_main"), 1)
        return evac

    def zf_dve(V):
        def evac(gi, b, n):
            c = gi * 4 + b
            V.e.wait_ge(S("zf_main"), n + 1)
            V.mine(V.e.scalar_tensor_tensor(ZS[c][:, 1:SEQ], PS[:, b, 0:SEQ - 1], col("ab_shift_prev", c),
                                            ZS[c][:, 1:SEQ], ALU.mult, ALU.add))
            V.wait_mine()
            V.e.scalar_tensor_tensor(ZS[c][:, 0:SEQ - 1], PS[:, b, 1:SEQ], col("ab_shift_next", c),
                                     ZS[c][:, 0:SEQ - 1], ALU.mult, ALU.add).then_inc(sem("zf", "ev"), 1)
        return evac

    def zu_act(A):
        def evac(gi, b, n):
            A.e.activation(UG[:, b, :], PS[:, b, :], ACT.Gelu_apprx_tanh).then_inc(sem("zu", "ev"), 1)
        return evac

    def zu_beside_act(A):
        def beside(s):
            if s == 0:
                A.e.wait_ge(*at("zf", "ev", ZN))
                A.e.activation(ZS[ZW][:, :], ZS[ZW][:, :], ACT.Tanh).then_inc(S("rw0_tanh"), 1)
                A.e.activation(ZS[ZG][:, :], ZS[ZG][:, :], ACT.Tanh, scale=0.5).then_inc(S("rw0_tanh"), 1)
            else:
                for j in range(NJ):
                    A.e.wait_ge(S("rw0_ss"), j + 1)
                    A.e.activation(SQN[j][:, :], PS[:, 4 + j, :], ACT.Sqrt, bias=SM[:, 24:25]).then_inc(S("rw0_norm"), 1)
        return beside

    def zu_beside_dve(V):
        e = V.e

        def beside(s):
            if s == 0:
                e.wait_ge(*at("zf", "ev", ZN))
                for j in range(NJ):
                    V.mine(e.tensor_scalar(KK[:, j, :], ZS[ZK + j][:, :], col("rwkv_k_k", j), None, ALU.mult))
                V.wait_mine()
                for j in range(NJ):
                    e.tensor_tensor(SQN[j][:, :], KK[:, j, :], KK[:, j, :], ALU.mult).then_inc(S("rw0_sq"), 1)
                e.memset(RHO[1][:, :, :], 0.0)
            else:
                e.wait_ge(S("rw0_tanh"), 2)
                e.tensor_scalar(ZS[ZG][:, :], ZS[ZG][:, :], 0.5, 0.5, ALU.mult, ALU.add)
                for j in range(NJ):
                    e.wait_ge(S("rw0_norm"), j + 1)
                    V.mine(e.reciprocal(SQN[j][:, :], SQN[j][:, :]))
                    V.wait_mine()
                    V.mine(e.tensor_tensor(KK[:, j, :], KK[:, j, :], SQN[j][:, :], ALU.mult))
        return beside

    def zu_beside_pe(T):
        def beside(s):
            if s == 1:
                T.e.wait_ge(S("c_in"), C_IN)
                for j in range(NJ):
                    T.e.wait_ge(S("rw0_sq"), j + 1)
                    T.e.matmul(PS[:, 4 + j, :], rk("bones"), SQN[j][:, :], start=True, stop=True).then_inc(S("rw0_ss"), 1)
        return beside

    def rw0_pe(T):
        e = T.e
        e.wait_ge(S("rw0_tanh"), 1)
        e.wait_ge(S("rw0_norm"), NJ)
        lora_pe(e, 0, 0, 7)
        lora_pe(e, 0, 1, 6)
        for g in range(SGU_G):
            mm = e.transpose(PS[:, 4, g * P:g * P + P], WS[:, g, :], ident)
        mm.then_inc(S("wst_tp"), 1)

    def rw0_act(A):
        e = A.e
        e.wait_ge(S("w_lo"), fence)
        prep_tanh_act(e, 0, 0, 7)
        prep_tanh_act(e, 0, 1, 6)
        e.wait_ge(S("wst_tp"), 1)
        e.activation(WST[:, :, :], PS[:, 4, :].rearrange("p (g q) -> p g q", g=4), ACT.Copy).then_inc(S("wst"), 1)
        prep_exp_act(e, 0)

    def rw0_dve(V):
        e = V.e
        e.wait_ge(S("w_lo"), fence)
        prep_sum_dve(V, 0)
        e.wait_ge(*at("zu", "done", 4))
        for z in (ALP[:, :, :], RHO[0][:, :, :], BPD[:, :, :, :], KPD[:, :, :, :]):
            V.mine(e.memset(z, 0.0))
        V.wait_mine()
        prep_scale_dve(V, 0)

    def zv_act(A):
        def evac(gi, b, n):
            A.e.activation(VG[:, b, :], PS[:, b, :], ACT.Gelu_apprx_tanh).then_inc(sem("zv", "ev"), 1)
            A.e.wait_ge(*at("zv", "ev", b + 1))
            if b > 0:
                A.e.wait_ge(S("sgu_sq"), b)
            A.e.activation(SQ1[:, :], VG[:, b, :], ACT.Square, accum_out=SM[:, b:b + 1]).then_inc(S("sgu_sq"), 1)
        return evac

    def zv_dve(V):
        e = V.e

        def scale(t):
            e.wait_ge(S("sgu_rstd"), t + 1)
            e.tensor_scalar(VG[:, t, :], VG[:, t, :], SM[:, 8 + t:9 + t], None, ALU.mult).then_inc(S("sgu_vg"), 1)

        def evac(gi, b, n):
            e.wait_ge(S("sgu_sq"), b + 1)
            e.tensor_scalar(SM[:, 4 + b:5 + b], SM[:, b:b + 1], 1.0 / 512, EPS, ALU.mult, ALU.add)\
                .then_inc(S("sgu_var"), 1)
            if b > 0:
                scale(b - 1)
            if b == NT - 1:
                scale(b)
        return evac

    def mix0_act(A):
        e = A.e
        for t in range(NT):
            e.wait_ge(S("rw0_vtp"), t + 1)
            e.activation(VTK[:, t, :], PS[:, 4 + t, :], ACT.Copy).then_inc(S("rw0_vtk"), 1)
        for g in range(SGU_G):
            e.wait_ge(S("sgu_b"), g + 1)
            e.activation(HHI[4 + g][:, :], BT[g % 2][:, :], ACT.Copy).then_inc(S("sgu_hi"), 1)

    def sgu_pool(G):
        for t in range(NT):
            G.e.wait_ge(S("sgu_var"), t + 1)
            G.e.tensor_tensor(SM[:, 8 + t:9 + t], SM[:, 4 + t:5 + t], SM[:, 16:17], ALU.pow).then_inc(S("sgu_rstd"), 1)

    def mix0_dve(V):
        e = V.e

        def low_part(g):
            e.wait_ge(S("sgu_hi"), g + 1)
            e.tensor_tensor(HLO[4 + g][:, :], BT[g % 2][:, :], HHI[4 + g][:, :].bitcast(F32), ALU.subtract)\
                .then_inc(S("sgu_lo"), 1)

        for g in range(SGU_G):
            e.wait_ge(S("sgu_mm"), g + 1)
            if g >= 2:
                e.wait_ge(S("sgu_lo"), g - 1)
            b = BT[g % 2]
            V.mine(e.scalar_tensor_tensor(b[:, :].rearrange("p (n q) -> p n q", n=NT),
                                          PS[:, 4 + g, :].rearrange("p (n q) -> p n q", n=NT), col("sgu_v_gain", g),
                                          SGUB[:, g, :].unsqueeze(1).to_broadcast([P, NT, P]), ALU.mult, ALU.add))
            V.wait_mine()
            e.tensor_tensor(b[:, :], b[:, :], UG[:, g, :], ALU.mult).then_inc(S("sgu_b"), 1)
            if g >= 1:
                low_part(g - 1)
        low_part(SGU_G - 1)

    def mix0_pe(T):
        e = T.e
        e.wait_ge(S("wst"), 1)
        e.wait_ge(S("p_lorafree"), 2)
        for t in range(NT):
            for j in range(NJ):
                mm = e.transpose(PS[:, 4 + t, j * P:j * P + P], ZS[ZV + j][:, t * P:t * P + P], ident)
            mm.then_inc(S("rw0_vtp"), 1)
        e.wait_ge(S("sgu_vg"), NT)
        for g in range(SGU_G):
            e.wait_ge(S("rw0_vtk"), g + 1)
            for n in range(NT):
                mm = e.matmul(PS[:, 4 + g, n * P:n * P + P], VG[:, n, g * P:g * P + P], WST[:, g, :], start=True, stop=True)
            mm.then_inc(S("sgu_mm"), 1)

    NPAIR = 2 * NJ
    LV = 5

    def quad(bank, k=P):
        return PS[:, bank, :].rearrange("p (u k) -> p u k", k=k)

    def uslot(u):
        return slice((u % 4) * P, (u % 4) * P + P)

    def lora_pe(e, n, which, bank):
        d, j = divmod(n, NJ)
        e.matmul(PS[:, bank, :], WL2[half(d), which, j * P:j * P + P], ZS[ZW + which][half(d), :], start=True, stop=True)\
            .then_inc(S("p_lora"), 1)

    def pair_pe(T, n):
        e = T.e
        j = n % NJ
        rho = RHO[n % 2]
        e.wait_ge(S("p_fm"), n + 1)
        for g in range(2):
            for u in range(4 * g, 4 * g + 4):
                t, hh = divmod(u, 2)
                mm = e.matmul(PS[:, 6 + g, uslot(u)], ALP[:, hh, t * P:t * P + P], BET[:, t * P:t * P + P],
                              start=True, stop=True)
            mm.then_inc(S("p_a"), 1)
        for q, (l, r) in enumerate(((KAP, ALP), (BET, rho), (KAP, rho))):
            for g in range(2):
                bank = (2, 3, 4, 5, 0, 1)[2 * q + g]
                if n > 0 and bank in (4, 5, 0, 1):
                    e.wait_ge(S({4: "p_rfree", 5: "p_yfree", 0: "p_pfree", 1: "p_qfree"}[bank]), n)
                for t in (2 * g, 2 * g + 1):
                    mm = e.matmul(PS[:, bank, (t % 2) * 256:(t % 2) * 256 + 256].rearrange("p (h q) -> p h q", h=2),
                                  l[:, t * P:t * P + P], r[:, 0:2, t * P:t * P + P], start=True, stop=True)
                mm.then_inc(S("p_g"), 1)
        for g in range(2):
            e.wait_ge(S("p_t1"), 2 * n + g + 1)
            for u in range(4 * g, 4 * g + 4):
                mm = e.transpose(PS[:, 6 + g, uslot(u)], TT[:, u, :], ident)
            mm.then_inc(S("p_u1"), 1)
        for lv in range(LV):
            for g in range(2):
                e.wait_ge(S("p_u"), (n * (LV + 1) + lv) * 2 + g + 1)
                if lv == 0:
                    e.wait_ge(S("p_gfree"), 6 * n + g + 1)
                else:
                    if lv == 1:
                        e.wait_ge(S("p_gfree"), 6 * n + 3 + g)
                    for u in range(4 * g, 4 * g + 4):
                        mm = e.transpose(PS[:, 4 + g, uslot(u)], UU[:, u, :], ident)
                    mm.then_inc(S("p_ttp"), 1)
                for u in range(4 * g, 4 * g + 4):
                    mm = e.matmul(PS[:, 2 + g, uslot(u)], AI[:, u, :], UU[:, u, :], start=True, stop=True)
                mm.then_inc(S("p_x"), 1)
            for g in range(2):
                e.wait_ge(S("p_xm"), (n * LV + lv) * 2 + g + 1)
                if lv > 0:
                    e.wait_ge(S("p_t"), (n * (LV - 1) + lv - 1) * 2 + g + 1)
                else:
                    e.wait_ge(S("p_gfree"), 6 * n + 5 + g)
                for u in range(4 * g, 4 * g + 4):
                    mm = e.matmul(PS[:, g, uslot(u)], TT[:, u, :], XX[:, u, :], start=True, stop=True)
                mm.then_inc(S("p_un"), 1)
            if lv == LV - 1:
                e.wait_ge(S("p_tokfree"), 3 * n + 3)
                for g in range(2):
                    for u in range(4 * g, 4 * g + 4):
                        mm = e.matmul(PS[:, 6 + g, uslot(u)], GKA[:, u, :], VTK[:, u // 2, j * P:j * P + P],
                                      start=True, stop=True)
                    mm.then_inc(S("p_x0"), 1)
            if lv == 0:
                for hh in range(2):
                    e.wait_ge(S("p_u"), n * (LV + 1) * 2 + hh + 1)
                    for t in range(NT):
                        mm = e.transpose(PS[:, 6 + hh, t * HD:t * HD + HD], ALP[half(hh), hh, t * P:t * P + P],
                                         KC[half(hh), HD * hh:HD * hh + HD])
                mm.then_inc(S("p_tok"), 1)
            if lv == 1:
                e.wait_ge(S("p_tokfree"), 3 * n + 1)
                e.matmul(PS[:, 6, :], rk("bones"), TMP[0][:, :], start=True, stop=True).then_inc(S("p_bonmm"), 1)
                if n + 1 < NPAIR:
                    lora_pe(e, n + 1, 0, 7)
            if lv == 2:
                e.wait_ge(S("p_bonfree"), n + 1)
                if n + 1 < NPAIR:
                    lora_pe(e, n + 1, 1, 6)
                    e.wait_ge(S("p_lorafree"), 2 * n + 3)
                for t in range(NT):
                    mm = e.transpose(PS[:, 7, t * P:t * P + P], BET[:, t * P:t * P + P], ident)
                mm.then_inc(S("p_tok"), 1)
            if lv == 3:
                if n + 1 < NPAIR:
                    e.wait_ge(S("p_lorafree"), 2 * n + 4)
                for t in range(NT):
                    mm = e.transpose(PS[:, 6, t * P:t * P + P], KAP[:, t * P:t * P + P], ident)
                mm.then_inc(S("p_tok"), 1)
        for g in range(2):
            e.wait_ge(S("p_u"), (n * (LV + 1) + LV) * 2 + g + 1)
            e.wait_ge(S("p_ax"), 2 * n + g + 1)
            for u in range(4 * g, 4 * g + 4):
                mm = e.matmul(PS[:, 2 + g, uslot(u)], UU[:, u, :], AXT[:, u, :], start=True, stop=True)
            mm.then_inc(S("p_wu"), 1)
        for u in range(8):
            t, hh = divmod(u, 2)
            e.matmul(PS[half(hh), 5, t * P:t * P + P], VTK[:, t, j * P + HD * hh:j * P + HD * hh + HD], GKR[:, u, :],
                     start=(t == 0), stop=False)
        e.wait_ge(S("p_wuc"), 2 * (n + 1))
        for u in range(8):
            t, hh = divmod(u, 2)
            mm = e.matmul(PS[half(hh), 4, t * P:t * P + P], WU[:, u, 0:HD], GBR[:, u, :], start=True, stop=True)
        mm.then_inc(S("p_r"), 1)
        for u in range(8):
            t, hh = divmod(u, 2)
            mm = e.matmul(PS[half(hh), 5, t * P:t * P + P], WU[:, u, HD:P], GBR[:, u, :], start=False, stop=(t == NT - 1))
        mm.then_inc(S("p_y"), 1)
        for u in range(8):
            t, hh = divmod(u, 2)
            mm = e.matmul(PS[half(hh), 0, t * P:t * P + P].rearrange("p (c k) -> p c k", c=2), WU[:, u, 0:HD],
                          BPD[:, t, :, HD * hh:HD * hh + HD], start=True, stop=True)
        mm.then_inc(S("p_p"), 1)
        for u in (0, 2, 4, 6, 1, 3, 5, 7):
            t, hh = divmod(u, 2)
            for c in range(2):
                o = PS[half(hh), 1, (2 * t + c) * HD:(2 * t + c) * HD + HD]
                e.matmul(o, BPD[:, t, c, HD * hh:HD * hh + HD], WU[:, u, HD:P], start=True, stop=False)
                mm = e.matmul(o, KPD[:, t, c, HD * hh:HD * hh + HD], VTK[:, t, j * P + HD * hh:j * P + HD * hh + HD],
                              start=False, stop=True)
        mm.then_inc(S("p_q"), 1)

    def prep_tanh_act(e, n, which, bank):
        if which == 0:
            if n > 0:
                e.wait_ge(S("p_bonmm"), n)
        e.wait_ge(S("p_lora"), 2 * n + which + 1)
        if which == 1 and n > 0:
            e.wait_ge(S("p_fm"), n)
        e.activation(TMP[which][:, :], PS[:, bank, :], ACT.Tanh, scale=0.5,
                     bias=SM[:, 216 + 8 * which + n:217 + 8 * which + n]).then_inc(S("p_lorafree"), 1)

    def prep_exp_act(e, n):
        e.wait_ge(S("p_c"), n + 1)
        e.activation(TMP[3][:, :], TMP[3][:, :], ACT.Exp).then_inc(S("p_e"), 1)
        e.activation(TMP[0][:, :], TMP[2][:, :], ACT.Exp).then_inc(S("p_e"), 1)
        e.wait_ge(S("p_e"), 3 * n + 2)
        e.activation(TMP[2][:, :], TMP[2][:, :], ACT.Exp, scale=-1.0).then_inc(S("p_e"), 1)

    def pair_act(A, n):
        e = A.e
        j = n % NJ

        def copy_u(src, g):
            e.activation(UU[:, 4 * g:4 * g + 4, :], quad(src + g), ACT.Copy).then_inc(S("p_u"), 1)

        for g in range(2):
            e.wait_ge(S("p_u1"), 2 * n + g + 1)
            copy_u(6, g)
        for lv in range(LV):
            for g in range(2):
                e.wait_ge(S("p_un"), (n * LV + lv) * 2 + g + 1)
                copy_u(0, g)
            if lv + 1 < LV:
                for g in range(2):
                    e.wait_ge(S("p_ttp"), (n * (LV - 1) + lv) * 2 + g + 1)
                    e.activation(TT[:, 4 * g:4 * g + 4, :], quad(4 + g), ACT.Copy).then_inc(S("p_t"), 1)
            if lv == 0:
                e.wait_ge(S("p_tok"), 3 * n + 1)
                for hh in range(2):
                    i = e.activation(AXT[:, :, 0:HD].rearrange("p (t h) k -> p t h k", h=2)[:, :, hh, :],
                                     PS[:, 6 + hh, 0:NT * HD].rearrange("p (t k) -> p t k", t=NT), ACT.Copy)
                i.then_inc(S("p_tokfree"), 1)
            if lv == 1 and n + 1 < NPAIR:
                prep_tanh_act(e, n + 1, 0, 7)
            if lv == 2 and n + 1 < NPAIR:
                prep_tanh_act(e, n + 1, 1, 6)
            if lv in (2, 3):
                dst, bank = ((BPD, 7), (KPD, 6))[lv - 2]
                e.wait_ge(S("p_tok"), 3 * n + lv)
                for c in range(2):
                    i = e.activation(dst[half(c), :, c, :],
                                     PS[half(c), bank, :].rearrange("p (t k) -> p t k", t=NT), ACT.Copy)
                i.then_inc(S("p_tokfree"), 1)
            if lv == 3 and n + 1 < NPAIR:
                prep_exp_act(e, n + 1)
        for g in range(2):
            e.wait_ge(S("p_x0"), 2 * n + g + 1)
            for hh in range(2):
                i = e.activation(
                    AXT[:, 4 * g:4 * g + 4, HD:P].rearrange("p (t h) k -> p t h k", h=2)[:, :, hh, :],
                    PS[:, 6 + g, :].rearrange("p (t h k) -> p t h k", h=2, k=P)[:, :, hh, HD * hh:HD * hh + HD], ACT.Copy)
            i.then_inc(S("p_ax"), 1)
        for g in range(2):
            e.wait_ge(S("p_wu"), 2 * n + g + 1)
            e.activation(WU[:, 4 * g:4 * g + 4, :], quad(2 + g), ACT.Copy).then_inc(S("p_wuc"), 1)
        e.wait_ge(S("p_q"), n + 1)
        e.activation(QT[:, j, :, :], quad(1, HD), ACT.Copy).then_inc(S("p_qfree"), 1)

    def ecl(d, j):
        o = (128 if d == 0 else 64) + j * NCH
        return SM[:, o:o + NCH]

    def prep_sum_dve(V, n):
        e = V.e
        e.wait_ge(S("p_lorafree"), 2 * n + 1)
        V.mine(e.tensor_scalar(TMP[0][:, :], TMP[0][:, :], -0.5 * DECAY, -0.5 * DECAY, ALU.mult, ALU.add))
        e.wait_ge(S("p_lorafree"), 2 * n + 2)
        V.mine(e.tensor_scalar(TMP[1][:, :], TMP[1][:, :], 0.5, 0.5, ALU.mult, ALU.add))
        V.wait_mine()
        if n < NJ:
            V.mine(e.tensor_tensor_scan(TMP[2][:, :], rk("reset"), TMP[0][:, :], 0.0, ALU.mult, ALU.add))
        else:
            V.mine(e.tensor_tensor_scan(TMP[2][:, ::-1], rk("reset"), TMP[0][:, ::-1], 0.0, ALU.mult, ALU.add))
        V.wait_mine()
        e.tensor_tensor(TMP[3][:, :], TMP[2][:, :], TMP[0][:, :], ALU.subtract).then_inc(S("p_c"), 1)

    def prep_scale_dve(V, n):
        e = V.e
        d, j = divmod(n, NJ)
        r, k, kk, rho = ZS[ZR + j], ZS[ZK + j], KK[:, j, :], RHO[n % 2]
        e.wait_ge(S("p_e"), 3 * n + 1)
        for hh in range(2):
            e.scalar_tensor_tensor(ALP[half(hh), hh, :], KK[half(hh), j, :], -1.0, TMP[3][half(hh), :], ALU.mult, ALU.mult)
        e.wait_ge(S("p_e"), 3 * n + 2)
        for hh in range(2):
            V.mine(e.tensor_tensor(rho[half(hh), hh, :], r[half(hh), :], TMP[0][half(hh), :], ALU.mult))
        last = CH - 1 if d == 0 else 0
        V.mine(e.tensor_copy(ecl(d, j), TMP[0][:, last::CH]))
        e.wait_ge(S("p_e"), 3 * n + 3)
        V.wait_mine()
        V.mine(e.tensor_scalar(TMP[3][:, :], TMP[1][:, :], col("rwkv_k_a", j), SM[:, 232 + j:233 + j], ALU.mult, ALU.add))
        if n > 0:
            e.wait_ge(S("p_tok"), 3 * n)
        V.mine(e.tensor_tensor(BET[:, :], kk, TMP[1][:, :], ALU.mult))
        V.wait_mine()
        V.mine(e.tensor_tensor(TMP[3][:, :], TMP[3][:, :], k[:, :], ALU.mult))
        V.wait_mine()
        e.scalar_tensor_tensor(TMP[0][:, :], TMP[3][:, :], col("rwkv_r_k", j), r[:, :], ALU.mult, ALU.mult)
        e.tensor_tensor(BET[:, :], BET[:, :], TMP[2][:, :], ALU.mult)
        e.tensor_tensor(KAP[:, :], TMP[3][:, :], TMP[2][:, :], ALU.mult).then_inc(S("p_fm"), 1)

    def pair_dve(V, n):
        e = V.e
        d, j = divmod(n, NJ)
        id4 = ident.unsqueeze(1).to_broadcast([P, 4, P])
        fb = "fb"[d]
        for g in range(2):
            e.wait_ge(S("p_a"), 2 * n + g + 1)
            ai, tt = AI[:, 4 * g:4 * g + 4, :], TT[:, 4 * g:4 * g + 4, :]
            V.mine(e.tensor_tensor(ai, quad(6 + g), mask4("LT" if d == 0 else "UT"), ALU.mult))
            V.wait_mine()
            V.mine(e.tensor_tensor(ai, ai, id4, ALU.add))
            V.wait_mine()
            e.tensor_tensor(tt, ai, mask4("T1" + fb), ALU.mult).then_inc(S("p_t1"), 1)
        for q, (dst, m) in enumerate(((GKA, "UT" if d == 0 else "LT"), (GBR, "UTI" if d == 0 else "LTI"),
                                      (GKR, "UTI" if d == 0 else "LTI"))):
            for g in range(2):
                e.wait_ge(S("p_g"), 6 * n + 2 * q + g + 1)
                e.tensor_tensor(dst[:, 4 * g:4 * g + 4, :], quad((2, 3, 4, 5, 0, 1)[2 * q + g]), mask4(m),
                                ALU.mult).then_inc(S("p_gfree"), 1)
        for lv in range(LV):
            for g in range(2):
                e.wait_ge(S("p_x"), (n * LV + lv) * 2 + g + 1)
                e.tensor_tensor(XX[:, 4 * g:4 * g + 4, :], quad(2 + g), mask4(f"X{fb}{lv + 2}"), ALU.mult)\
                    .then_inc(S("p_xm"), 1)
            if lv == 1:
                e.wait_ge(S("p_bonmm"), n + 1)
                if d == 0:
                    e.tensor_copy(BON[j][:, :], PS[:, 6, :]).then_inc(S("p_bonfree"), 1)
                else:
                    e.tensor_tensor(BON[j][:, :], BON[j][:, :], PS[:, 6, :], ALU.add).then_inc(S("p_bonfree"), 1)
            if lv == 3 and n + 1 < NPAIR:
                prep_sum_dve(V, n + 1)
        if n + 1 < NPAIR:
            prep_scale_dve(V, n + 1)
        lo, hi, back = (1, NCH, -1) if d == 0 else (0, NCH - 1, 1)
        prev = ecl(d, j)[:, lo + back:hi + back].unsqueeze(2).to_broadcast([P, NCH - 1, HD])
        e.wait_ge(S("p_r"), n + 1)
        for hh in range(2):
            i = e.tensor_tensor(RT[half(hh), j, :], PS[half(hh), 4, :], RHO[n % 2][half(hh), hh, :], ALU.add)
        i.then_inc(S("p_rfree"), 1)
        e.wait_ge(S("p_y"), n + 1)
        if d == 0:
            e.tensor_copy(YL[:, j, :], PS[:, 5, :]).then_inc(S("p_yfree"), 1)
        else:
            e.tensor_tensor(YL[:, j, :], YL[:, j, :], PS[:, 5, :], ALU.add).then_inc(S("p_yfree"), 1)
        e.wait_ge(S("p_rfree"), n + 1)
        r = RT[:, j, lo * CH:hi * CH].rearrange("p (c t) -> p c t", t=CH)
        e.tensor_tensor(r, r, prev, ALU.mult)
        e.wait_ge(S("p_p"), n + 1)
        p = PT[:, j, lo:hi, :]
        e.tensor_tensor(p, quad(0, HD)[:, lo:hi, :], rk("ident2").unsqueeze(1).to_broadcast([P, NCH - 1, HD]), ALU.add)\
            .then_inc(S("p_pfree"), 1)
        e.wait_ge(S("p_pfree"), n + 1)
        e.tensor_tensor(p, p, prev, ALU.mult).then_inc(S("p_pt"), 1)

    def order(d):
        return list(range(NCH)) if d == 0 else list(range(NCH - 1, -1, -1))

    STEPS = NCH - 1

    def chain_pe(T, d):
        e, o = T.e, order(d)
        e.wait_ge(S("p_pt"), NJ * (d + 1))
        e.wait_ge(S("p_qfree"), NJ * (d + 1))
        for i in range(1, NCH):
            if i > 1:
                e.wait_ge(S("c_state"), d * (STEPS - 1) + i - 1)
            if i < STEPS:
                for hh in range(2):
                    for j in range(NJ):
                        mm = e.matmul(PS[half(hh), hh, j * HD:j * HD + HD], PT[half(hh), j, o[i], :],
                                      QT[half(hh), j, o[i - 1], :], start=True, stop=True)
                mm.then_inc(S("c_mm"), 1)
            if i > 2:
                e.wait_ge(S("c_yfree"), d * STEPS + i - 2)
            for hh in range(2):
                for j in range(NJ):
                    mm = e.matmul(PS[half(hh), 2 + 2 * (i % 2) + hh, j * HD:j * HD + HD], QT[half(hh), j, o[i - 1], :],
                                  RT[half(hh), j, o[i] * CH:o[i] * CH + CH], start=True, stop=True)
            mm.then_inc(S("c_y"), 1)
        e.wait_ge(S("c_yfree"), (d + 1) * STEPS)

    def chain_dve(V, d):
        e, o = V.e, order(d)
        e.wait_ge(S("p_yfree"), NJ * (d + 1))
        for i in range(1, NCH):
            if i < STEPS:
                e.wait_ge(S("c_mm"), d * (STEPS - 1) + i)
                for hh in range(2):
                    s = QT[half(hh), :, o[i], :]
                    m = e.tensor_tensor(s, s, PS[half(hh), hh, 0:NJ * HD].rearrange("p (j v) -> p j v", j=NJ), ALU.add)
                m.then_inc(S("c_state"), 1)
            e.wait_ge(S("c_y"), d * STEPS + i)
            for hh in range(2):
                y = YL[half(hh), :, o[i] * CH:o[i] * CH + CH]
                m = e.tensor_tensor(y, y, PS[half(hh), 2 + 2 * (i % 2) + hh, 0:NJ * CH].rearrange("p (j t) -> p j t", j=NJ),
                                    ALU.add)
            m.then_inc(S("c_yfree"), 1)

    def fin_pe(T):
        e = T.e
        for j in range(NJ):
            e.wait_ge(S("f_sq"), j + 1)
            e.matmul(PS[:, j, :], rk("bones"), YQ[j][:, :], start=True, stop=True).then_inc(S("f_mm"), 1)
            e.matmul(PS[:, 4 + j, :], WL2[:, 2, j * P:j * P + P], ZS[ZG][:, :], start=True, stop=True)\
                .then_inc(S("f_mm"), 1)
        e.wait_ge(S("f_norm"), NJ)
        e.wait_ge(S("f_gate"), NJ)

    def fin_act(A):
        e = A.e
        for j in range(NJ):
            e.activation(YQ[j][:, :], YL[:, j, :], ACT.Square).then_inc(S("f_sq"), 1)
        for j in range(NJ):
            e.wait_ge(S("f_mm"), 2 * j + 1)
            e.activation(YQ[4 + j][:, :], PS[:, j, :], ACT.Sqrt, scale=1.0 / HD, bias=SM[:, 25:26])\
                .then_inc(S("f_norm"), 1)
            e.wait_ge(S("f_mm"), 2 * j + 2)
            e.activation(YQ[j][:, :], PS[:, 4 + j, :], ACT.Copy).then_inc(S("f_gate"), 1)
        split_hi(A, fence + 2)
        for j in range(NJ):
            e.wait_ge(S("f_out"), j + 1)
            e.activation(HHI[j][:, :], YQ[4 + j][:, :], ACT.Copy).then_inc(S("f_hi"), 1)

    def fin_dve(V):
        e = V.e
        for j in range(NJ):
            V.mine(e.tensor_tensor(BON[j][:, :], BON[j][:, :], ZS[ZV + j][:, :], ALU.mult))
        for j in range(NJ):
            y = YQ[4 + j]
            e.wait_ge(S("f_norm"), j + 1)
            V.mine(e.reciprocal(y[:, :], y[:, :]))
            V.wait_mine()
            V.mine(e.tensor_tensor(y[:, :], y[:, :], YL[:, j, :], ALU.mult))
            V.wait_mine()
            V.mine(e.scalar_tensor_tensor(y[:, :], y[:, :], col("rwkv_out_gain", j), BON[j][:, :], ALU.mult, ALU.add))
            V.wait_mine()
            e.wait_ge(S("f_gate"), j + 1)
            e.tensor_tensor(y[:, :], y[:, :], YQ[j][:, :], ALU.mult).then_inc(S("f_out"), 1)
            if j == 0:
                split_lo(V, fence + 2)
        for j in range(NJ):
            e.wait_ge(S("f_hi"), j + 1)
            e.tensor_tensor(HLO[j][:, :], YQ[4 + j][:, :], HHI[j][:, :].bitcast(F32), ALU.subtract)\
                .then_inc(S("f_lo"), 1)

    SC = 1.0 / math.sqrt(XD)

    def xattn_pe(T, l):
        e, xa = T.e, f"xa{l}"
        for t in range(NT + 2):
            if t < NT:
                if t >= 2:
                    e.wait_ge(*at(xa, "xe", XH * (t - 1)))
                for h in range(XH):
                    for k in range(2):
                        mm = e.matmul(PS[:, 4 * (t % 2) + h // 2, (h % 2) * MEM:(h % 2) * MEM + MEM],
                                      QFT[:, 2 * h + k, t * P:t * P + P], KFT[:, 2 * h + k, :],
                                      start=(k == 0), stop=(k == 1))
                mm.then_inc(sem(xa, "xl"), 1)
            if 1 <= t <= NT:
                xturn_pe(e, xa, t - 1)
            if t >= 2:
                xout_pe(e, xa, t - 2)

    def xturn_pe(e, xa, t):
        e.wait_ge(*at(xa, "xn", t + 1))
        if t >= 1:
            e.wait_ge(*at(xa, "xpc", 2 * t))
        for hp in range(2):
            for q in range(4):
                h, k = 2 * hp + q // 2, q % 2
                mm = e.transpose(PS[:, 2 + hp, q * P:q * P + P], EX[t % 2][:, h, k * P:k * P + P], ident)
            mm.then_inc(sem(xa, "xtp"), 1)

    def xout_pe(e, xa, t):
        e.wait_ge(*at(xa, "xpc", 2 * (t + 1)))
        for q in range(2):
            if t >= 1:
                e.wait_ge(*at(xa, "xolo", 2 * (t - 1) + q + 1))
            for c in range(4 * q, 4 * q + 4):
                for k in range(MT):
                    mm = e.matmul(PS[:, 6 + q, (c % 4) * P:(c % 4) * P + P], VMEM[:, k, c * P:c * P + P],
                                  PTR[:, c // 2, k, t * P:t * P + P], start=(k == 0), stop=(k == 1))
            mm.then_inc(sem(xa, "xpv"), 1)

    def xout(q):
        return PS[:, 6 + q, :].rearrange("p (c k) -> p c k", c=4)

    def xattn_act(A, l):
        e, xa = A.e, f"xa{l}"
        for t in range(NT + 2):
            if t < NT:
                e.wait_ge(*at(xa, "xmx", t + 1))
                for h in range(XH):
                    e.activation(EX[t % 2][:, h, :], PS[:, 4 * (t % 2) + h // 2, (h % 2) * MEM:(h % 2) * MEM + MEM],
                                 ACT.Exp, scale=SC, bias=SM[:, 40 + 4 * (t % 2) + h:41 + 4 * (t % 2) + h],
                                 accum_out=SM[:, 48 + 4 * (t % 2) + h:49 + 4 * (t % 2) + h]).then_inc(sem(xa, "xe"), 1)
            if 1 <= t <= NT:
                for hp in range(2):
                    e.wait_ge(*at(xa, "xtp", 2 * (t - 1) + hp + 1))
                    e.activation(PTR[:, 2 * hp:2 * hp + 2, :, (t - 1) * P:t * P],
                                 PS[:, 2 + hp, :].rearrange("p (h k q) -> p h k q", h=2, k=2), ACT.Copy)\
                        .then_inc(sem(xa, "xpc"), 1)
            if t >= 2:
                for q in range(2):
                    e.wait_ge(*at(xa, "xpv", 2 * (t - 2) + q + 1))
                    e.activation(HIS[:, 4 * q:4 * q + 4, (t - 2) * P:(t - 1) * P], xout(q), ACT.Copy)\
                        .then_inc(sem(xa, "xohi"), 1)

    def xattn_dve(V, l):
        e, xa = V.e, f"xa{l}"
        for t in range(NT + 2):
            b = 4 * (t % 2)
            if t < NT:
                e.wait_ge(*at(xa, "xl", t + 1))
                if t >= 2:
                    e.wait_ge(*at(xa, "xtp", 2 * (t - 1)))
                for q in range(2):
                    V.mine(e.tensor_reduce(SM[:, 32 + b + 2 * q:34 + b + 2 * q],
                                           PS[:, b + q, :].rearrange("p (h k) -> p h k", h=2), AX.X, ALU.max))
                V.wait_mine()
                e.tensor_scalar(SM[:, 40 + b:44 + b], SM[:, 32 + b:36 + b], -SC, None, ALU.mult).then_inc(sem(xa, "xmx"), 1)
                e.wait_ge(*at(xa, "xe", XH * (t + 1)))
                V.mine(e.reciprocal(SM[:, 56 + b:60 + b], SM[:, 48 + b:52 + b]))
                V.wait_mine()
                v = EX[t % 2][:, :, :]
                e.tensor_tensor(v, v, SM[:, 56 + b:60 + b].unsqueeze(2).to_broadcast([P, XH, MEM]), ALU.mult)\
                    .then_inc(sem(xa, "xn"), 1)
            if t >= 2:
                for q in range(2):
                    o = (slice(None), slice(4 * q, 4 * q + 4), slice((t - 2) * P, (t - 1) * P))
                    e.wait_ge(*at(xa, "xohi", 2 * (t - 2) + q + 1))
                    e.tensor_tensor(LOS[o], xout(q), HIS[o].bitcast(F32), ALU.subtract).then_inc(sem(xa, "xolo"), 1)

    def convw(l, tap, c):
        i = (l * 3 + tap) * 44 + c
        tile, row = divmod(i, 88)
        return COLS[:, (2 + tile) * P + row:(2 + tile) * P + row + 1]

    def up_act(A, l, h):
        name = f"up{l}{h}"

        def evac(gi, b, n):
            c = 12 * h + 2 * gi + b % 2
            dst = (CG if b < 2 else CV)[b % 2]
            cc = c if b < 2 else FC + c
            if gi > 0:
                A.e.wait_ge(*at(name, "lo", 2 * (gi - 1) + b % 2 + 1))
            A.e.activation(dst[:, :], PS[:, b, :], ACT.Identity, scale=convw(l, 1, cc),
                           bias=col("ffn_conv_b", l * 44 + cc)).then_inc(sem(name, "main"), 1)
            if b < 2:
                A.e.wait_ge(*at(name, "ev", n + 1))
                A.e.activation(SG[b][:, :], CG[b][:, :], ACT.Silu).then_inc(sem(name, "silu"), 1)
            else:
                A.e.wait_ge(*at(name, "g", 2 * gi + b - 1))
                A.e.activation(GHI[2 * gi + b - 2][:, :], SG[b - 2][:, :], ACT.Copy).then_inc(sem(name, "hi"), 1)
        return evac

    def up_dve(V, l, h):
        name = f"up{l}{h}"

        def evac(gi, b, n):
            c = 12 * h + 2 * gi + b % 2
            cc = c if b < 2 else FC + c
            dst = (CG if b < 2 else CV)[b % 2]
            V.e.wait_ge(*at(name, "main", n + 1))
            V.mine(V.e.scalar_tensor_tensor(dst[:, 1:SEQ], PS[:, b, 0:SEQ - 1], convw(l, 0, cc), dst[:, 1:SEQ],
                                            ALU.mult, ALU.add))
            V.wait_mine()
            V.e.scalar_tensor_tensor(dst[:, 0:SEQ - 1], PS[:, b, 1:SEQ], convw(l, 2, cc), dst[:, 0:SEQ - 1],
                                     ALU.mult, ALU.add).then_inc(sem(name, "ev"), 1)
            if b >= 2:
                i = 2 * gi + b - 2
                V.e.wait_ge(*at(name, "silu", i + 1))
                V.e.wait_ge(*at(name, "ev", n + 1))
                V.e.tensor_tensor(SG[b - 2][:, :], SG[b - 2][:, :], CV[b - 2][:, :], ALU.mult).then_inc(sem(name, "g"), 1)
                V.e.wait_ge(*at(name, "hi", i + 1))
                V.e.tensor_tensor(GLO[i][:, :], SG[b - 2][:, :], GHI[i][:, :].bitcast(F32), ALU.subtract)\
                    .then_inc(sem(name, "lo"), 1)
        return evac

    DSC = 1.0 / math.sqrt(DHD)
    NM = DH * NT

    def dlog_pe(e, m):
        h, t = divmod(m, NT)
        b = 2 * (m % 2)
        if m >= 2:
            e.wait_ge(S("ds"), 2 * (m - 1))
        for c in range(2):
            e.matmul(PS[:, b + c, :], QF[:, h, c, t * P:t * P + P], KF[:, h, :], start=True, stop=True).then_inc(S("dl"), 1)

    def dturn_pe(e, m):
        e.wait_ge(S("dat"), m + 1)
        if m >= 2:
            e.wait_ge(S("datc"), m - 1)
        for k in range(NT):
            mm = e.transpose(PS[:, 4 + m % 2, k * P:k * P + P], AT[m % 2][:, k * P:k * P + P], ident)
        mm.then_inc(S("dtp"), 1)

    def dpv_pe(e, m):
        h, t = divmod(m, NT)
        e.wait_ge(S("datc"), m + 1)
        if m >= 2:
            e.wait_ge(S("dov"), m - 1)
        for k in range(NT):
            mm = e.matmul(PS[:, 6 + m % 2, 0:P], ATT[m % 2][:, k, :], VV[:, k, h * P:h * P + P],
                          start=(k == 0), stop=(k == NT - 1))
        mm.then_inc(S("dpv"), 1)

    def dattn_pe(T):
        for m in range(NM + 3):
            if m < NM:
                dlog_pe(T.e, m)
            if 2 <= m < NM + 2:
                dturn_pe(T.e, m - 2)
            if m >= 3:
                dpv_pe(T.e, m - 3)

    def sx(m, i, n=1):
        o = 32 + 16 * (m % 4) + i
        return SM[:, o:o + n]

    def dattn_act(A):
        e = A.e

        def copy(m):
            e.wait_ge(S("dtp"), m + 1)
            if m >= 2:
                e.wait_ge(S("dpv"), m - 1)
            e.activation(ATT[m % 2][:, :, :], PS[:, 4 + m % 2, :].rearrange("p (k q) -> p k q", k=NT), ACT.Copy)\
                .then_inc(S("datc"), 1)

        def out(m):
            h, t = divmod(m, NT)
            e.wait_ge(S("dpv"), m + 1)
            e.activation(OTK[:, t, h * P:h * P + P], PS[:, 6 + m % 2, 0:P], ACT.Copy, scale=sx(m, 6))\
                .then_inc(S("dov"), 1)

        def bias(h):
            if h >= 2:
                e.wait_ge(S("ds"), 2 * NT * (h - 1))
            slope = 2.0 ** (-8.0 * (h + 1) / DH)
            e.activation(BIAS[h % 2][:, :], DIST[:, :], ACT.Copy, scale=-slope / DSC).then_inc(S("dbias"), 1)

        e.wait_ge(S("dist_in"), 16)
        bias(0)
        for m in range(NM + 3):
            if m < NM:
                if m % NT == 1 and m // NT + 1 < DH:
                    bias(m // NT + 1)
                e.wait_ge(S("dmx"), m + 1)
                for c in range(2):
                    e.activation(SS[m % 3][:, c, :], SS[m % 3][:, c, :], ACT.Exp, scale=DSC, bias=sx(m, 2 + c),
                                 accum_out=sx(m, 4 + c)).then_inc(S("de"), 1)
            if 2 <= m < NM + 2:
                copy(m - 2)
            if m >= 3:
                out(m - 3)

    def dattn_dve(V):
        e = V.e

        def first(m):
            h, t = divmod(m, NT)
            b = 2 * (m % 2)
            if t == 0:
                e.wait_ge(S("dbias"), h + 1)
            for c in range(2):
                e.wait_ge(S("dl"), 2 * m + c + 1)
                o = 384 - P * t
                e.tensor_tensor_reduce(SS[m % 3][:, c, :], PS[:, b + c, :], BIAS[h % 2][:, o:o + SEQ], 1.0, -3e38,
                                       ALU.add, ALU.max, sx(m, c)).then_inc(S("ds"), 1)
            e.wait_ge(S("ds"), 2 * m + 2)
            e.tensor_scalar(sx(m, 2, 2), sx(m, 0, 2), -DSC, None, ALU.mult).then_inc(S("dmx"), 1)

        def second(m):
            e.wait_ge(S("de"), 2 * m + 2)
            V.mine(e.reciprocal(sx(m, 6, 2), sx(m, 4, 2)))
            V.wait_mine()
            V.mine(e.scalar_tensor_tensor(sx(m, 8), sx(m, 4), SM[:, 26:27], sx(m, 7), ALU.mult, ALU.mult))
            V.wait_mine()
            if m >= 2:
                e.wait_ge(S("dtp"), m - 1)
            e.scalar_tensor_tensor(AT[m % 2][:, :], SS[m % 3][:, 1, :], sx(m, 8), SS[m % 3][:, 0, :],
                                   ALU.mult, ALU.add).then_inc(S("dat"), 1)

        def square(m):
            h, t = divmod(m, NT)
            e.wait_ge(S("dov"), m + 1)
            o = OTK[:, t, h * P:h * P + P]
            V.wait_mine()
            V.mine(e.tensor_tensor_reduce(SQO[:, :], o, o, 1.0, 0.0, ALU.mult, ALU.add,
                                          SM[:, 96 + h * NT + t:97 + h * NT + t]))
            if t == NT - 1:
                V.wait_mine()
                hs = slice(128 + h * NT, 128 + h * NT + NT)
                e.tensor_scalar(SM[:, hs], SM[:, 96 + h * NT:96 + h * NT + NT], 1.0 / P, EPS, ALU.mult, ALU.add)\
                    .then_inc(sem("do", "gvar"), 1)

        def normalise(h):
            e.wait_ge(*at("do", "grstd", h + 1))
            o = OTK[:, :, h * P:h * P + P]
            e.tensor_tensor(o, o, SM[:, 160 + h * NT:160 + h * NT + NT].unsqueeze(2).to_broadcast([P, NT, P]),
                            ALU.mult).then_inc(sem("do", "gn"), 1)

        for m in range(NM + 4):
            if m < NM:
                first(m)
            if 1 <= m < NM + 1:
                second(m - 1)
            if m >= 4:
                square(m - 4)
                if m % NT == 0 and m >= 2 * NT:
                    normalise(m // NT - 2)
        normalise(DH - 1)

    def dturn_out_pe(T):
        e = T.e
        for h in range(DH):
            e.wait_ge(*at("do", "gn", h + 1))
            if h >= 4:
                e.wait_ge(*at("do", "tev", h - 3))
            for t in range(NT):
                mm = e.transpose(PS[:, 4 + h % 4, t * P:t * P + P], OTK[:, t, h * P:h * P + P], ident)
            mm.then_inc(sem("do", "ttp"), 1)

    def dout_act(A):
        e = A.e
        for k in range(DC):
            e.wait_ge(*at("do", "ttp", k + 1))
            e.activation(HHI[k][:, :], PS[:, 4 + k % 4, :], ACT.Copy, scale=SM[:, 27:28]).then_inc(sem("do", "hi"), 1)

    def dout_dve(V):
        e = V.e
        for k in range(DC):
            e.wait_ge(*at("do", "hi", k + 1))
            e.scalar_tensor_tensor(HLO[k][:, :], PS[:, 4 + k % 4, :], SM[:, 27:28], HHI[k][:, :].bitcast(F32), ALU.mult,
                                   ALU.subtract).then_inc(sem("do", "tev"), 1)

    def load_x(e):
        for t in range(NT):
            e.dma_start(X[:, t, :], a["x"][0, t * P:t * P + P, :]).then_inc(S(f"x_in{t}"), 16)

    def load_vectors(e):
        e.dma_start(KC[:, :], a["ident"]).then_inc(S("ident_in"), 16)
        e.wait_ge(S("v_zero"), 5)
        n = 0
        for i, tile in enumerate(VEC_TILES):
            row = 0
            for name, rows in tile:
                src = a[name]
                if name in ("diff_q_gain", "diff_k_gain"):
                    for h in range(2):
                        e.dma_start(VROW[i][row:row + 1, HD * h:HD * h + HD], src[0:1, :]).then_inc(S("v_in"), 16)
                        n += 16
                else:
                    if name == "ffn_conv_w":
                        v = src.rearrange("l t (r p) -> (l t r) p", p=P)[(i - 2) * 88:(i - 1) * 88, :]
                    elif name in ("rwkv_r_k", "rwkv_out_gain"):
                        v = src.rearrange("e (r h) n -> (e r) (h n)", h=2)
                    elif name in ("rwkv_w0", "rwkv_a0"):
                        v = src.rearrange("e d (r p) -> (e d r) p", p=P)
                    elif name == "mem_norm":
                        v = src.rearrange("(r p) -> r p", p=P)
                    else:
                        v = src.rearrange("e (r p) -> (e r) p", p=P)
                    e.dma_start(VROW[i][row:row + rows, :], v).then_inc(S("v_first" if i == 0 else "v_in"), 16)
                    n += 16 * (i > 0)
                row += rows
        assert n == V_IN

    def load_constants(e):
        e.dma_start(RC[:, :], a["rkc"]).then_inc(S("c_in"), 16)
        e.dma_start(WL2[:, 0, :], a["rwkv_w2"].rearrange("e d r c -> (e d r) c")).then_inc(S("c_in"), 16)
        e.dma_start(WL2[:, 1, :], a["rwkv_a2"].rearrange("e d r c -> (e d r) c")).then_inc(S("c_in"), 16)
        e.dma_start(WL2[:, 2, :], a["rwkv_g2"][0]).then_inc(S("c_in"), 16)
        e.dma_start(WS[:, :, :], a["sgu_w_s"][0].rearrange("g p q -> p g q")).then_inc(S("c_in"), 16)
        e.dma_start(SGUB[:, :, :].rearrange("p g q -> p (g q)"),
                    a["sgu_b"].rearrange("e g q -> e (g q)").to_broadcast([P, 512])).then_inc(S("c_in"), 16)
        for i, name in enumerate(("q1", "k1", "q2", "k2")):
            e.dma_start(LAM[:, HD * i:HD * i + HD], a[f"diff_lambda_{name}"].to_broadcast([P, HD])).then_inc(S("c_in"), 16)

    C_IN = 16 * 10
    V_FIRST = 16 * len(VEC_TILES[0])
    V_IN = 16 * (sum(len(t) for t in VEC_TILES[1:]) + 2)

    def setup_pe(T):
        e = T.e
        e.wait_ge(S("ident_in"), 16)
        e.wait_ge(S("v_first"), V_FIRST)
        e.transpose(PS[:, 0, 0:P], VROW[0][:, :], ident).then_inc(S("v_tp"), 1)
        norm_pe(T, "n0", XN, NT, 4)
        e.wait_ge(S("v_in"), V_IN)
        for i in range(1, 5):
            e.transpose(PS[:, 1, (i - 1) * P:i * P], VROW[i][:, :], ident).then_inc(S("v_tp"), 1)

    def setup_pool(G):
        G.mine(G.e.memset(SM[:, 24:25], 1e-12))
        G.mine(G.e.memset(SM[:, 25:26], EPS))
        G.mine(G.e.memset(SM[:, 16:24], -0.5))
        G.wait_mine()

    def setup_dve(V):
        V.e.wait_ge(S("v_tp"), 1)
        V.e.tensor_copy(COLS[:, 0:P], PS[:, 0, 0:P]).then_inc(S("cols"), 1)
        V.e.wait_ge(S("cols"), 1)

    def factors_dve(V):
        e = V.e
        e.wait_ge(S("v_tp"), 5)
        V.mine(e.tensor_copy(COLS[:, P:5 * P], PS[:, 1, :]))
        V.wait_mine()
        V.mine(e.tensor_tensor(SM[:, 200:215], col("ab_shift_prev", 0, 15), col("ab_shift_next", 0, 15), ALU.add))
        V.wait_mine()
        e.tensor_scalar(SM[:, 200:215], SM[:, 200:215], -1.0, 1.0, ALU.mult, ALU.add)
        e.tensor_scalar(SM[:, 216:224], col("rwkv_w0", 0, 8), 0.5, None, ALU.mult)
        e.tensor_scalar(SM[:, 224:232], col("rwkv_a0", 0, 8), 0.5, None, ALU.mult)
        e.tensor_scalar(SM[:, 232:236], col("rwkv_k_a", 0, 4), -1.0, 1.0, ALU.mult, ALU.add)
        e.tensor_scalar(SM[:, 27:28], col("diff_out_gain"), 1.0 - LAMBDA_INIT, None, ALU.mult)\
            .then_inc(S("factors"), 1)

    def lambda_dve(V):
        e = V.e
        e.wait_ge(S("c_in"), C_IN)
        for i in range(2):
            V.mine(e.tensor_tensor(LAM[:, P * i:P * i + HD], LAM[:, P * i:P * i + HD], LAM[:, P * i + HD:P * i + P], ALU.mult))
        V.wait_mine()
        for i in range(2):
            e.tensor_reduce(SM[:, 28 + i:29 + i], LAM[:, P * i:P * i + HD], AX.X, ALU.add).then_inc(S("lam_dot"), 1)
        e.wait_ge(S("lam_exp"), 1)
        V.mine(e.tensor_tensor(SM[:, 26:27], SM[:, 29:30], SM[:, 28:29], ALU.subtract))
        V.wait_mine()
        e.tensor_scalar(SM[:, 26:27], SM[:, 26:27], -LAMBDA_INIT, None, ALU.add)

    def lambda_act(A):
        A.e.wait_ge(S("lam_dot"), 2)
        A.e.activation(SM[:, 28:30], SM[:, 28:30], ACT.Exp).then_inc(S("lam_exp"), 1)

    def gcol(name, l=0):
        return lambda k: col(name, l * DC + k)

    def norm_shares(tag, nt, by_tile=False):
        n = nt if by_tile else 1
        shares(tag, "norm", sq=nt, var=n, rstd=n, xn=nt, tp=DC, hi=DC, lo=DC)

    def turn_shares(tag, nt):
        n = DH if tag == "do" else 1
        shares(tag, "turn", gvar=n, grstd=n, gn=DH if tag == "do" else nt, ttp=DC, tev=DC, hi=DC if tag == "do" else 0)

    norm_shares("n0", NT)
    for l in range(2):
        if l == 1:
            norm_shares("n1", NT, True)
            for tag in ("dk", "dq", "do"):
                turn_shares(tag, NT)
        norm_shares(f"m{l}", MT)
        norm_shares(f"nx{l}", NT)
        turn_shares(f"xk{l}", MT)
        turn_shares(f"xqn{l}", NT)
        shares(f"kk{l}", "hs", hsum=4 * MT)
        shares(f"xq{l}", "hs", hsum=4 * NT)
        shares(f"xa{l}", "xa", xe=XH * NT, xl=NT, xpc=2 * NT, xolo=DC, xpv=DC, xn=NT, xtp=2 * NT, xmx=NT, xohi=DC)
        norm_shares(f"nf{l}", NT, True)
        for h in range(2):
            n = len(gemms[f"up{l}{h}"])
            shares(f"up{l}{h}", "up", main=4 * n, silu=2 * n, g=2 * n, hi=2 * n, lo=2 * n)

    mhi, mlo = (lambda k: MNT[k][:, :]), (lambda k: MNL[k][:, :])
    ghi, glo = (lambda k: GHI[k][:, :]), (lambda k: GLO[k][:, :])

    def copy_out(A, name, dst):
        def evac(gi, b, n):
            A.e.activation(dst(gi, b), PS[:, b, :], ACT.Copy).then_inc(sem(name, "ev"), 1)
        return evac

    def to_tok(tok):
        return lambda gi, b: tok[:, b, gi * 512:gi * 512 + 512]

    def tensor_program(T):
        setup_pe(T)
        T.e.wait_ge(S("factors"), 1)
        gemm_pe(T, "zf", hhi, hlo, tokens_out=False, operand=lambda k: at("n0", "lo", k))
        gemm_pe(T, "zu", hhi, hlo, tokens_out=False, beside=zu_beside_pe(T))
        rw0_pe(T)
        gemm_pe(T, "zv", hhi, hlo)
        mix0_pe(T)
        T.meet()
        for d in range(2):
            for j in range(NJ):
                pair_pe(T, d * NJ + j)
            chain_pe(T, d)
        T.meet()
        fin_pe(T)
        for l in range(2):
            if l == 1:
                norm_pe(T, "n1", XN, NT, 4)
                gemm_pe(T, "dk", hhi, hlo, operand=lambda k: at("n1", "lo", k))
                gemm_pe(T, "dq", hhi, hlo)
                turn_pe(T, "dk", TOKK, NT)
                gemm_pe(T, "dv", hhi, hlo)
                turn_pe(T, "dq", TOKQ, NT)
                T.meet()
                dattn_pe(T)
                T.meet()
                dturn_out_pe(T)
            if l == 0:
                gemm_pe(T, "ab", hhi, hlo, operand=lambda k: (S("f_lo"), NJ) if k <= NJ else (S("sgu_lo"), SGU_G))
            else:
                gemm_pe(T, "do", hhi, hlo, operand=lambda k: at("do", "tev", k))
            if l == 0:
                T.e.wait_ge(*at("ab", "ev", NT))
            norm_pe(T, f"m{l}", MXN, MT, 4 * l)
            T.meet()
            gemm_pe(T, f"kk{l}", mhi, mlo)
            norm_pe(T, f"nx{l}", XN, NT, 4)
            T.e.wait_ge(*at(f"nx{l}", "lo", DC))
            gemm_pe(T, f"xq{l}", hhi, hlo)
            turn_pe(T, f"xk{l}", KTOK, MT)
            gemm_pe(T, f"kv{l}", mhi, mlo)
            turn_pe(T, f"xqn{l}", QTOK, NT)
            T.meet()
            xattn_pe(T, l)
            gemm_pe(T, f"xo{l}", hhi, hlo, operand=lambda k, l=l: at(f"xa{l}", "xolo", DC))
            norm_pe(T, f"nf{l}", XN, NT, 4)
            for h in range(2):
                gemm_pe(T, f"up{l}{h}", hhi, hlo, tokens_out=False,
                        operand=(lambda k, l=l: at(f"nf{l}", "lo", k)) if h == 0 else None)
                gemm_pe(T, f"dn{l}{h}", ghi, glo, operand=lambda k, l=l, h=h: at(f"up{l}{h}", "lo", k))

    def scalar_program(A):
        def side(name, evac=None, limit=None, beside=None):
            gemm_side(A, name, split_hi, evac, limit, beside)

        norm_act_front(A, "n0", X, SQ, NT, arrives=True)
        split_hi(A, 1)
        A.e.wait_ge(S("cols"), 1)
        norm_act_back(A, "n0", NT, gcol("mix_norm", 0), hhi, 4)
        A.e.wait_ge(S("factors"), 1)
        side("zf", zf_act(A), fence)
        lambda_act(A)
        side("zu", zu_act(A), fence, zu_beside_act(A))
        rw0_act(A)
        side("zv", zv_act(A), fence)
        mix0_act(A)
        A.meet()
        for n in range(NPAIR):
            pair_act(A, n)
        split_hi(A, fence + 1)
        A.meet()
        fin_act(A)
        for l in range(2):
            if l == 1:
                norm_act_back(A, "n1", NT, gcol("mix_norm", 1), hhi, 4)
                side("dk", copy_out(A, "dk", to_tok(TOKK)))
                side("dq", copy_out(A, "dq", to_tok(TOKQ)))
                turn_act(A, "dk", lambda k: KF[:, k, :], NT, lambda k: col("diff_k_gain"))
                side("dv", copy_out(A, "dv", to_tok(VV)))
                turn_split_act(A)
                A.meet()
                dattn_act(A)
                A.meet()
                dout_act(A)

            def mem_front(s):
                if s == 1:
                    A.e.wait_ge(S("mem_in"), 16 * (l + 1))
                    norm_act_front(A, f"m{l}", MRAW, SQM, MT)

            side(("ab", "do")[l], beside=mem_front)
            norm_act_back(A, f"m{l}", MT, gcol("mem_norm"), mhi, 4 * l)
            A.meet()
            norm_act_front(A, f"nx{l}", X, SQ, NT)
            side(f"kk{l}", head_sums_act(A, f"kk{l}", to_tok(KTOK), 64))
            norm_act_back(A, f"nx{l}", NT, gcol("cross_norm", l), hhi, 4)
            side(f"xq{l}", head_sums_act(A, f"xq{l}", to_tok(QTOK), 32))
            turn_act(A, f"xk{l}", lambda k: KFT[:, k, :], MT, lambda k: col("cross_k_gain", 2 * l + k % 2))
            side(f"kv{l}", copy_out(A, f"kv{l}", to_tok(VMEM)))
            turn_act(A, f"xqn{l}", lambda k: QFT[:, k, :], NT, lambda k: col("cross_q_gain", 2 * l + k % 2))
            A.meet()
            xattn_act(A, l)
            side(f"xo{l}", square_tile_act(A, f"xo{l}", f"nf{l}"))
            norm_act_back(A, f"nf{l}", NT, gcol("ffn_norm", l), hhi, 4)
            for h in range(2):
                side(f"up{l}{h}", up_act(A, l, h))
                side(f"dn{l}{h}", square_tile_act(A, "dn01", "n1") if (l, h) == (0, 1) else None)

    def vector_program(V):
        def side(name, evac=None, limit=None, beside=None):
            gemm_side(V, name, split_lo, evac, limit, beside)

        norm_dve_front(V, "n0", X, XN, NT)
        split_lo(V, 1)
        setup_dve(V)
        norm_dve_back(V, "n0", NT, gcol("mix_norm", 0), hhi, hlo, 4, 0, 4)
        factors_dve(V)
        norm_dve_back(V, "n0", NT, gcol("mix_norm", 0), hhi, hlo, 4, 4, DC)
        side("zf", zf_dve(V), fence)
        lambda_dve(V)
        side("zu", None, fence, zu_beside_dve(V))
        rw0_dve(V)
        side("zv", zv_dve(V), fence)
        mix0_dve(V)
        V.meet()
        for d in range(2):
            for j in range(NJ):
                pair_dve(V, d * NJ + j)
            chain_dve(V, d)
        split_lo(V, fence + 1)
        V.meet()
        fin_dve(V)
        for l in range(2):
            if l == 1:
                norm_dve_back(V, "n1", NT, gcol("mix_norm", 1), hhi, hlo, 4)
                for h in range(2):
                    V.e.memset(QF[DHD * (1 - h):DHD * (1 - h) + DHD, :, h, :], 0.0)
                side("dk")
                side("dq", beside=group_norm_beside(V, "dk", TOKK, "dk"))
                side("dv", beside=group_norm_beside(V, "dq", TOKQ, "dq"))
                V.meet()
                dattn_dve(V)
                V.meet()
                dout_dve(V)

            def mem_front(s):
                if s == 2:
                    norm_dve_front(V, f"m{l}", MRAW, MXN, MT)

            side(("ab", "do")[l], add_residual(V, ("ab", "do")[l]), beside=mem_front)
            norm_dve_back(V, f"m{l}", MT, gcol("mem_norm"), mhi, mlo, 4 * l)
            V.meet()
            norm_dve_front(V, f"nx{l}", X, XN, NT)
            side(f"kk{l}")
            norm_dve_back(V, f"nx{l}", NT, gcol("cross_norm", l), hhi, hlo, 4)
            head_norm_dve(V, f"xk{l}", f"kk{l}", KTOK, MT, 32)
            side(f"xq{l}")
            head_norm_dve(V, f"xqn{l}", f"xq{l}", QTOK, NT, 0)
            side(f"kv{l}")
            V.meet()
            xattn_dve(V, l)
            side(f"xo{l}", residual_and_norm_dve(V, f"xo{l}", f"nf{l}"))
            norm_dve_back(V, f"nf{l}", NT, gcol("ffn_norm", l), hhi, hlo, 4)
            for h in range(2):
                side(f"up{l}{h}", up_dve(V, l, h))
                side(f"dn{l}{h}", residual_and_norm_dve(V, "dn01", "n1") if (l, h) == (0, 1)
                     else add_residual(V, f"dn{l}{h}"))

    def pool_program(G):
        load_constants(G.e)
        setup_pool(G)
        norm_pool(G, "n0", NT)
        sgu_pool(G)
        G.meet()
        G.meet()
        G.e.wait_ge(S("f_mm"), 2 * NJ)
        G.e.wait_ge(S("f_out"), NJ)
        for l in range(2):
            if l == 1:
                group_norm_pool(G, "dk", NT, DHD)
                group_norm_pool(G, "dq", NT, DHD)
                G.meet()
                for h in range(DH):
                    G.e.wait_ge(*at("do", "gvar", h + 1))
                    G.e.tensor_tensor(SM[:, 160 + h * NT:160 + h * NT + NT], SM[:, 128 + h * NT:128 + h * NT + NT],
                                      SM[:, 16:20], ALU.pow).then_inc(sem("do", "grstd"), 1)
                G.meet()
                G.e.wait_ge(*at("do", "ttp", DC))
            if l == 0:
                G.e.dma_start(DIST[:, :], a["dist"]).then_inc(S("dist_in"), 16)
            G.e.dma_start(MRAW[:, :, :], a["mem"][0].rearrange("(t p) d -> p t d", p=P)).then_inc(S("mem_in"), 16)
            norm_pool(G, f"m{l}", MT)
            G.meet()
            norm_pool(G, f"nx{l}", NT)
            group_norm_pool(G, f"xk{l}", MT, XD, 32)
            group_norm_pool(G, f"xqn{l}", NT, XD)
            G.meet()
            norm_pool_tiles(G, f"nf{l}")
            if l == 0:
                norm_pool_tiles(G, "n1")

    block = nc.Block()
    with block:
        @block.tensor
        def _(e):
            T = Engine("pe", e)
            tensor_program(T)

        @block.scalar
        def _(e):
            scalar_program(Engine("act", e))

        @block.vector
        def _(e):
            for i in range(5):
                e.memset(VROW[i][:, :], 0.0).then_inc(S("v_zero"), 1)
            vector_program(Engine("dve", e))

        @block.gpsimd
        def _(e):
            pool_program(Engine("pool", e))

        @block.sync
        def _(e):
            load_x(e)
            load_slab(e, 0)
            load_vectors(e)
            for i in range(1, len(plan)):
                if i == fence:
                    e.wait_ge(S("p_q"), NPAIR)
                if i >= 2:
                    e.wait_ge(S("w_lo"), i - 1)
                load_slab(e, i)
            for g in range(2):
                for t in range(NT):
                    e.wait_ge(*at("dn11", "ev", NT * g + t + 1))
                    e.dma_start(out[0, t * P:t * P + P, g * 512:g * 512 + 512], X[:, t, g * 512:g * 512 + 512])\
                        .then_inc(S("stored"), 16)
            e.wait_ge(S("stored"), 16 * 2 * NT)


def host_constants():
    import numpy as np
    i = np.arange(P)
    p, f = i[:, None], i[None, :]
    same = lambda b: p // b == f // b
    c = {"LT": (p > f) & same(CH), "UT": (p < f) & same(CH), "UTI": (p <= f) & same(CH), "LTI": (p >= f) & same(CH),
         "T1f": (p >= f) & same(2), "T1b": (p <= f) & same(2)}
    for lv in range(2, 7):
        level = same(1 << lv) & ~same(1 << (lv - 1))
        c[f"Xf{lv}"] = (level & (p < f)) | (p == f)
        c[f"Xb{lv}"] = (level & (p > f)) | (p == f)
    c["bones"] = same(HD)
    c["reset"] = np.broadcast_to((np.arange(SEQ) % CH != 0)[None, :], (P, SEQ))
    c["ident2"] = (p % HD) == np.arange(HD)[None, :]
    rkc = np.zeros((P, RK_W), np.float32)
    for n, (o, w) in RK.items():
        rkc[:, o:o + w] = c[n]
    return {"ident": (p == f).astype(np.float32), "rkc": rkc,
            "dist": np.abs(p + 384 - np.arange(DIST_W)[None, :]).astype(np.float32)}


_INS = ['x', 'mem', 'mem_norm', 'mix_norm', 'cross_norm', 'ffn_norm', 'ab_w_in', 'ab_shift_prev', 'ab_shift_next',
        'rwkv_w0', 'rwkv_w2', 'rwkv_a0', 'rwkv_a2', 'rwkv_g2', 'rwkv_k_k', 'rwkv_k_a', 'rwkv_r_k', 'rwkv_out_gain',
        'sgu_v_gain', 'sgu_w_s', 'sgu_b', 'ab_w_out', 'diff_w_in', 'diff_q_gain', 'diff_k_gain', 'diff_lambda_q1',
        'diff_lambda_k1', 'diff_lambda_q2', 'diff_lambda_k2', 'diff_out_gain', 'diff_w_out', 'cross_wq', 'cross_wkv',
        'cross_q_gain', 'cross_k_gain', 'cross_wo', 'ffn_w_up', 'ffn_conv_w', 'ffn_conv_b', 'ffn_w_down']


def kernel(**inputs):
    import numpy as np
    import concourse.bacc as bacc
    from concourse.bass_utils import run_bass_kernel_spmd

    nc = bacc.Bacc("TRN2", target_bir_lowering=False, num_devices=1)
    arrays = {n: np.ascontiguousarray(inputs[n]) for n in _INS}
    arrays.update(host_constants())
    aps = {n: nc.dram_tensor(n, v.shape, mybir.dt.from_np(v.dtype), kind="ExternalInput").ap() for n, v in arrays.items()}
    out = nc.dram_tensor("out", (1, SEQ, D), F32, kind="ExternalOutput").ap()
    build(nc, aps, out)
    r = run_bass_kernel_spmd(nc, [arrays], core_ids=[0])
    return r.results[0]["out"]
```
